# Optimizing a Trainium2 kernel written in Bass

```python
import math
import jax, jax.numpy as jnp
from jax import lax
import numpy as np

D_MODEL = 1024
BATCH = 1
SEQ = 512
DEPTH = 1
DEC_BATCH = 8
DEC_SEQ = 4
PAST_LEN = 1024
PAGE_SIZE = 128

MIX_WIDTH = D_MODEL
MLA_HEADS = 8
MLA_V_DIM = 64
MLA_NOPE_DIM = 64
MLA_ROPE_DIM = 32
MLA_Q_LORA = 256
MLA_KV_LORA = 128
MLA_WIDTH = MLA_HEADS * MLA_V_DIM
NSA_HEADS = 8
NSA_KV_HEADS = 2
NSA_HEAD_DIM = 64
NSA_GROUP = NSA_HEADS // NSA_KV_HEADS
NSA_WIDTH = NSA_HEADS * NSA_HEAD_DIM
NSA_KV_WIDTH = 2 * NSA_KV_HEADS * NSA_HEAD_DIM
CMP_BLOCK = 32
CMP_STRIDE = 16
SEL_BLOCK = 64
SEL_TOP_N = 16
WINDOW = 512
Q_BLOCK = 128
ROPE_THETA = 10000.0
RMS_EPS = 1e-6
LN_EPS = 1e-5
NEG_INF = -1e30
MLA_SCALE = (MLA_NOPE_DIM + MLA_ROPE_DIM) ** -0.5
NSA_SCALE = NSA_HEAD_DIM ** -0.5
ALPHA = (2 * DEPTH) ** 0.25
BETA = (8 * DEPTH) ** -0.25
IN_SPLITS = (MLA_Q_LORA, MLA_KV_LORA, MLA_ROPE_DIM, MLA_WIDTH, NSA_WIDTH, NSA_KV_WIDTH, NSA_KV_WIDTH, NSA_KV_WIDTH, 3 * NSA_HEADS, NSA_WIDTH)
IN_WIDTH = MLA_Q_LORA + MLA_KV_LORA + MLA_ROPE_DIM + MLA_WIDTH + NSA_WIDTH + 3 * NSA_KV_WIDTH + 3 * NSA_HEADS + NSA_WIDTH

kernel_name = 'hymba_mla_nsa_deepnorm_step'

def rms_norm(x, g):
    xf = x.astype(jnp.float32)
    y = xf * lax.rsqrt(jnp.mean(xf * xf, -1, keepdims=True) + RMS_EPS)
    return (y * g.astype(jnp.float32)).astype(x.dtype)

def layer_norm(x, g, b):
    xf = x.astype(jnp.float32)
    mu = jnp.mean(xf, -1, keepdims=True)
    var = jnp.mean(jnp.square(xf - mu), -1, keepdims=True)
    y = (xf - mu) * lax.rsqrt(var + LN_EPS) * g.astype(jnp.float32) + b.astype(jnp.float32)
    return y.astype(x.dtype)

def rope(x, pos):
    d = x.shape[-1]
    inv = 1.0 / (ROPE_THETA ** (jnp.arange(0, d, 2, dtype=jnp.float32) / d))
    ang = pos.astype(jnp.float32)[:, None] * inv[None, :]
    shp = (1, pos.shape[0]) + (1,) * (x.ndim - 3) + (d // 2,)
    cos = jnp.cos(ang).reshape(shp).astype(x.dtype)
    sin = jnp.sin(ang).reshape(shp).astype(x.dtype)
    x1, x2 = x[..., : d // 2], x[..., d // 2:]
    return jnp.concatenate([x1 * cos - x2 * sin, x2 * cos + x1 * sin], axis=-1)

def rope_k(kv, pos):
    return jnp.stack([rope(kv[:, :, 0], pos), kv[:, :, 1]], axis=2)

def masked_softmax(s, mask):
    p = jax.nn.softmax(jnp.where(mask, s, NEG_INF), axis=-1)
    return jnp.where(mask, p, 0.0)

def pad_to(a, m):
    r = (-a.shape[1]) % m
    return jnp.pad(a, [(0, 0), (0, r)] + [(0, 0)] * (a.ndim - 2))

def importance_map(nc, ns):
    i = np.arange(nc)[:, None]
    j = np.arange(ns)[None, :]
    lo = np.maximum(i * CMP_STRIDE, j * SEL_BLOCK)
    hi = np.minimum(i * CMP_STRIDE + CMP_BLOCK, (j + 1) * SEL_BLOCK)
    return jnp.asarray(np.maximum(hi - lo, 0).astype(np.float32) / CMP_BLOCK)

def project(x, pos, w):
    B, T, _ = x.shape
    cuts = np.cumsum(np.array(IN_SPLITS))[:-1].tolist()
    c_q, c_kv, k_r, z_mla, q_n, cmp_kv, sel_kv, win_kv, g_br, z_nsa = jnp.split(x @ w['w_in'], cuts, axis=-1)
    q = (rms_norm(c_q, w['q_norm_g']) @ w['w_uq']).reshape(B, T, MLA_HEADS, MLA_NOPE_DIM + MLA_ROPE_DIM)
    w_uk = w['w_uk'].reshape(MLA_KV_LORA, MLA_HEADS, MLA_NOPE_DIM)
    q_lat = jnp.einsum('bthn,chn->bthc', q[..., :MLA_NOPE_DIM], w_uk)
    q_rope = rope(q[..., MLA_NOPE_DIM:], pos)
    mla_row = jnp.concatenate([rms_norm(c_kv, w['kv_norm_g']), rope(k_r, pos)], axis=-1)
    q_n = q_n.reshape(B, T, NSA_KV_HEADS, NSA_GROUP, NSA_HEAD_DIM)
    kv_shape = (B, T, 2, NSA_KV_HEADS, NSA_HEAD_DIM)
    gates = jax.nn.sigmoid(g_br.astype(jnp.float32)).astype(x.dtype).reshape(B, T, 3, NSA_KV_HEADS, NSA_GROUP)
    return dict(q_lat=q_lat, q_rope=q_rope, mla_row=mla_row, z_mla=z_mla,
                q_n=q_n, q_rot=rope(q_n, pos), cmp_kv=cmp_kv.reshape(kv_shape),
                sel_kv=rope_k(sel_kv.reshape(kv_shape), pos), win_kv=rope_k(win_kv.reshape(kv_shape), pos),
                gates=gates, z_nsa=z_nsa)

def compress(kv, w):
    B, T = kv.shape[:2]
    n_chunk = T // CMP_STRIDE
    ratio = CMP_BLOCK // CMP_STRIDE
    nc = n_chunk - ratio + 1
    ch = kv.reshape(B, n_chunk, CMP_STRIDE, 2, NSA_KV_HEADS, NSA_HEAD_DIM)
    w1 = w['cmp_w1']
    w1c = w1.reshape(2, ratio, CMP_STRIDE, NSA_HEAD_DIM, NSA_HEAD_DIM)
    bias = w['cmp_b1'] + jnp.einsum('pkd,kpde->ke', w['cmp_pos_emb'], w1)
    hid = bias[None, None, :, None, :]
    for r in range(ratio):
        proj = jnp.einsum('bcpkgd,kpde->bckge', ch, w1c[:, r])
        hid = hid + proj[:, r:r + nc]
    return jnp.einsum('bckge,ked->bckgd', jax.nn.silu(hid), w['cmp_w2'])

def mla_attend(q_lat, q_rope, q_pos, kv_row, k_pos):
    ckv, krope = kv_row[..., :MLA_KV_LORA], kv_row[..., MLA_KV_LORA:]
    s = jnp.einsum('bthc,bkc->bhtk', q_lat, ckv) + jnp.einsum('bthr,bkr->bhtk', q_rope, krope)
    p = masked_softmax(s.astype(jnp.float32) * MLA_SCALE, k_pos[None, :] <= q_pos[:, None])
    return jnp.einsum('bhtk,bkc->bthc', p.astype(ckv.dtype), ckv)

def nsa_attend(q, q_rot, q_pos, gates, kv_c, cmp_end, imp_map, gather_sel, win_kv, win_pos):
    dt = q.dtype
    s = jnp.einsum('btghd,bngd->bghtn', q, kv_c[:, :, 0]).astype(jnp.float32) * NSA_SCALE
    p_cmp = masked_softmax(s, cmp_end[None, :] <= q_pos[:, None])
    o_cmp = jnp.einsum('bghtn,bngd->btghd', p_cmp.astype(dt), kv_c[:, :, 1])
    ns = imp_map.shape[1]
    imp = jnp.einsum('bghtn,nj->bgtj', p_cmp, imp_map)
    j = jnp.arange(ns, dtype=jnp.int32)[None, :]
    cur = (q_pos // SEL_BLOCK)[:, None]
    avail = j * SEL_BLOCK <= q_pos[:, None]
    forced = (j == 0) | (j == cur) | (j == cur - 1)
    imp = jnp.where(avail, jnp.where(forced, jnp.inf, imp), -jnp.inf)
    top_val, top_idx = lax.top_k(imp, min(SEL_TOP_N, ns))
    kv_s = gather_sel(top_idx)
    tok_pos = top_idx[..., None] * SEL_BLOCK + jnp.arange(SEL_BLOCK, dtype=jnp.int32)
    sel_mask = (top_val > -jnp.inf)[..., None] & (tok_pos <= q_pos[None, None, :, None, None])
    s = jnp.einsum('btghd,bgtnpd->bghtnp', q_rot, kv_s[..., 0, :]).astype(jnp.float32) * NSA_SCALE
    B, G, hg, Tq, n, sb = s.shape
    p = masked_softmax(s.reshape(B, G, hg, Tq, n * sb), sel_mask.reshape(B, G, 1, Tq, n * sb)).reshape(s.shape)
    o_sel = jnp.einsum('bghtnp,bgtnpd->btghd', p.astype(dt), kv_s[..., 1, :])
    s = jnp.einsum('btghd,bkgd->bghtk', q_rot, win_kv[:, :, 0]).astype(jnp.float32) * NSA_SCALE
    dpos = q_pos[:, None] - win_pos[None, :]
    p = masked_softmax(s, (dpos >= 0) & (dpos < WINDOW) & (win_pos >= 0)[None, :])
    o_win = jnp.einsum('bghtk,bkgd->btghd', p.astype(dt), win_kv[:, :, 1])
    g = gates[..., None]
    o = g[:, :, 0] * o_cmp + g[:, :, 1] * o_sel + g[:, :, 2] * o_win
    return o.reshape(o.shape[0], o.shape[1], NSA_WIDTH)

def finish(x, o_lat, o_nsa, z_mla, z_nsa, w):
    B, T, _ = x.shape
    w_uv = w['w_uv'].reshape(MLA_KV_LORA, MLA_HEADS, MLA_V_DIM)
    o_mla = jnp.einsum('bthc,chv->bthv', o_lat, w_uv).reshape(B, T, MLA_WIDTH)
    mixed = jnp.concatenate([o_mla * jax.nn.silu(z_mla), o_nsa * jax.nn.silu(z_nsa)], axis=-1)
    return layer_norm(ALPHA * x + mixed @ w['w_o'], w['ln_g'], w['ln_b'])

def prompt_layer(x, w):
    B, T, _ = x.shape
    pos = jnp.arange(T, dtype=jnp.int32)
    P = project(x, pos, w)
    kv_c = compress(pad_to(P['cmp_kv'], CMP_STRIDE), w)
    nc = kv_c.shape[1]
    cmp_end = jnp.arange(nc, dtype=jnp.int32) * CMP_STRIDE + (CMP_BLOCK - 1)
    sel = pad_to(P['sel_kv'], SEL_BLOCK)
    ns = sel.shape[1] // SEL_BLOCK
    sel_blocks = sel.reshape(B, ns, SEL_BLOCK, 2, NSA_KV_HEADS, NSA_HEAD_DIM)
    imp_map = importance_map(nc, ns)
    bi = jnp.arange(B)[:, None, None, None]
    gi = jnp.arange(NSA_KV_HEADS)[None, :, None, None]
    gather_sel = lambda idx: sel_blocks[bi, idx, :, :, gi]
    win_pad = jnp.pad(P['win_kv'], ((0, 0), (WINDOW, 0), (0, 0), (0, 0), (0, 0)))

    def block(s):
        q_pos = s + jnp.arange(Q_BLOCK, dtype=jnp.int32)
        qs = lambda a: lax.dynamic_slice_in_dim(a, s, Q_BLOCK, axis=1)
        o_lat = mla_attend(qs(P['q_lat']), qs(P['q_rope']), q_pos, P['mla_row'], pos)
        win = lax.dynamic_slice_in_dim(win_pad, s, WINDOW + Q_BLOCK, axis=1)
        win_pos = s - WINDOW + jnp.arange(WINDOW + Q_BLOCK, dtype=jnp.int32)
        o_nsa = nsa_attend(qs(P['q_n']), qs(P['q_rot']), q_pos, qs(P['gates']), kv_c, cmp_end,
                           imp_map, gather_sel, win, win_pos)
        return o_lat, o_nsa

    o_lat, o_nsa = lax.map(block, jnp.arange(T // Q_BLOCK, dtype=jnp.int32) * Q_BLOCK)
    unblock = lambda o: jnp.moveaxis(o, 0, 1).reshape((B, T) + o.shape[3:])
    y = finish(x, unblock(o_lat), unblock(o_nsa), P['z_mla'], P['z_nsa'], w)
    new = (P['mla_row'], P['cmp_kv'], P['sel_kv'], P['win_kv'][:, T - min(WINDOW, T):])
    return y, new

def sample_layer(x, cache_mla, cache_cmp, cache_sel, win_state, page_table, w):
    B, T, _ = x.shape
    n_pages = page_table.shape[1]
    past = n_pages * PAGE_SIZE
    pos = past + jnp.arange(T, dtype=jnp.int32)
    P = project(x, pos, w)

    def gather_past(cache):
        return cache[page_table].reshape((B, past) + cache.shape[2:])

    k_pos = jnp.arange(past + T, dtype=jnp.int32)
    mla_all = jnp.concatenate([gather_past(cache_mla), P['mla_row']], axis=1)
    o_lat = mla_attend(P['q_lat'], P['q_rope'], pos, mla_all, k_pos)
    cmp_all = jnp.concatenate([gather_past(cache_cmp), P['cmp_kv']], axis=1)
    kv_c = compress(pad_to(cmp_all, CMP_STRIDE), w)
    nc = kv_c.shape[1]
    cmp_end = jnp.arange(nc, dtype=jnp.int32) * CMP_STRIDE + (CMP_BLOCK - 1)
    nb_past = past // SEL_BLOCK
    new_sel = pad_to(P['sel_kv'], SEL_BLOCK)
    nnb = new_sel.shape[1] // SEL_BLOCK
    new_blocks = new_sel.reshape(B, nnb, SEL_BLOCK, 2, NSA_KV_HEADS, NSA_HEAD_DIM)
    sub = PAGE_SIZE // SEL_BLOCK
    pool = cache_sel.reshape((cache_sel.shape[0], sub, SEL_BLOCK) + cache_sel.shape[2:])
    bi = jnp.arange(B)[:, None, None, None]
    gi = jnp.arange(NSA_KV_HEADS)[None, :, None, None]

    def gather_sel(idx):
        jp = jnp.minimum(idx, nb_past - 1)
        phys = page_table[bi, jp // sub]
        old = pool[phys, jp % sub, :, :, gi]
        new = new_blocks[bi, jnp.clip(idx - nb_past, 0, nnb - 1), :, :, gi]
        return jnp.where((idx < nb_past)[..., None, None, None], old, new)

    imp_map = importance_map(nc, nb_past + nnb)
    w_buf = win_state.shape[1]
    win_all = jnp.concatenate([win_state, P['win_kv']], axis=1)
    win_pos = past - w_buf + jnp.arange(w_buf + T, dtype=jnp.int32)
    o_nsa = nsa_attend(P['q_n'], P['q_rot'], pos, P['gates'], kv_c, cmp_end, imp_map, gather_sel, win_all, win_pos)
    y = finish(x, o_lat, o_nsa, P['z_mla'], P['z_nsa'], w)
    new = (P['mla_row'], P['cmp_kv'], P['sel_kv'], win_all[:, T:])
    return y, new

def setup_inputs(seed: int = 0) -> dict:
    key = jax.random.key(seed)
    ks = jax.random.split(key, 24)
    n_pages = PAST_LEN // PAGE_SIZE
    n_used = DEC_BATCH * n_pages
    n_pool = n_used + max(1, n_used // 4)
    w_buf = min(WINDOW, PAST_LEN)
    nrm = lambda k, shape, scale: jax.random.normal(k, shape, jnp.float32) * scale
    page_table = jax.random.permutation(ks[6], n_pool)[:n_used].reshape(DEC_BATCH, n_pages).astype(jnp.int32)
    kvd = (2, NSA_KV_HEADS, NSA_HEAD_DIM)
    return {
        'x_prompt': nrm(ks[0], (BATCH, SEQ, D_MODEL), 1.0),
        'x_sample': nrm(ks[1], (DEC_BATCH, DEC_SEQ, D_MODEL), 1.0),
        'cache_mla': nrm(ks[2], (DEPTH, n_pool, PAGE_SIZE, MLA_KV_LORA + MLA_ROPE_DIM), 1.0),
        'cache_cmp_kv': nrm(ks[3], (DEPTH, n_pool, PAGE_SIZE) + kvd, 1.0),
        'cache_sel_kv': nrm(ks[4], (DEPTH, n_pool, PAGE_SIZE) + kvd, 1.0),
        'state_win_kv': nrm(ks[5], (DEPTH, DEC_BATCH, w_buf) + kvd, 1.0),
        'page_table': page_table,
        'w_in': nrm(ks[7], (DEPTH, D_MODEL, IN_WIDTH), D_MODEL ** -0.5),
        'q_norm_g': 1.0 + nrm(ks[8], (DEPTH, MLA_Q_LORA), 0.02),
        'w_uq': nrm(ks[9], (DEPTH, MLA_Q_LORA, MLA_HEADS * (MLA_NOPE_DIM + MLA_ROPE_DIM)), MLA_Q_LORA ** -0.5),
        'kv_norm_g': 1.0 + nrm(ks[10], (DEPTH, MLA_KV_LORA), 0.02),
        'w_uk': nrm(ks[11], (DEPTH, MLA_KV_LORA, MLA_HEADS * MLA_NOPE_DIM), MLA_KV_LORA ** -0.5),
        'w_uv': nrm(ks[12], (DEPTH, MLA_KV_LORA, MLA_HEADS * MLA_V_DIM), MLA_KV_LORA ** -0.5),
        'cmp_pos_emb': nrm(ks[13], (DEPTH, CMP_BLOCK, 2, NSA_HEAD_DIM), 0.1),
        'cmp_w1': nrm(ks[14], (DEPTH, 2, CMP_BLOCK, NSA_HEAD_DIM, NSA_HEAD_DIM), (CMP_BLOCK * NSA_HEAD_DIM) ** -0.5),
        'cmp_b1': nrm(ks[15], (DEPTH, 2, NSA_HEAD_DIM), 0.02),
        'cmp_w2': nrm(ks[16], (DEPTH, 2, NSA_HEAD_DIM, NSA_HEAD_DIM), NSA_HEAD_DIM ** -0.5),
        'w_o': nrm(ks[17], (DEPTH, MIX_WIDTH, D_MODEL), MIX_WIDTH ** -0.5 * BETA),
        'ln_g': 1.0 + nrm(ks[18], (DEPTH, D_MODEL), 0.02),
        'ln_b': nrm(ks[19], (DEPTH, D_MODEL), 0.02),
    }

def reference(x_prompt, x_sample, cache_mla, cache_cmp_kv, cache_sel_kv, state_win_kv, page_table,
              w_in, q_norm_g, w_uq, kv_norm_g, w_uk, w_uv, cmp_pos_emb, cmp_w1, cmp_b1, cmp_w2,
              w_o, ln_g, ln_b):
    hp, hs = x_prompt, x_sample
    rows = [[] for _ in range(8)]
    for l in range(DEPTH):
        w = dict(w_in=w_in[l], q_norm_g=q_norm_g[l], w_uq=w_uq[l], kv_norm_g=kv_norm_g[l], w_uk=w_uk[l],
                 w_uv=w_uv[l], cmp_pos_emb=cmp_pos_emb[l], cmp_w1=cmp_w1[l], cmp_b1=cmp_b1[l],
                 cmp_w2=cmp_w2[l], w_o=w_o[l], ln_g=ln_g[l], ln_b=ln_b[l])
        hp, new_p = prompt_layer(hp, w)
        hs, new_s = sample_layer(hs, cache_mla[l], cache_cmp_kv[l], cache_sel_kv[l], state_win_kv[l], page_table, w)
        for k, a in enumerate(new_p + new_s):
            rows[k].append(a)
    p_mla, p_cmp, p_sel, p_win, s_mla, s_cmp, s_sel, s_win = [jnp.stack(r) for r in rows]
    return (hp, hs, p_mla, p_cmp, p_sel, p_win, s_mla, s_cmp, s_sel, s_win)


_drawn_inputs = setup_inputs


def setup_inputs(seed=0):
    import zlib

    import numpy as np

    out = dict(_drawn_inputs(seed))
    spreads = {}
    factors = {'cache_mla': 5.186,
     'cache_cmp_kv': 5.856,
     'cache_sel_kv': 8.0,
     'q_norm_g': 8.0,
     'kv_norm_g': 2.78,
     'cmp_pos_emb': 8.0,
     'cmp_b1': 8.0,
     'ln_g': 2.899,
     'ln_b': 2.842}
    for name, (base, spread) in spreads.items():
        noise = np.random.default_rng([zlib.crc32(name.encode()), seed]).standard_normal(out[name].shape)
        drawn = base * np.exp(spread * noise) if base else spread * noise
        out[name] = __import__('jax').numpy.asarray(drawn.astype(out[name].dtype))
    for name, factor in factors.items():
        out[name] = (out[name] * factor).astype(out[name].dtype)
    return out
```

```python
import math
from contextlib import ExitStack

import numpy as np

import concourse.bass as bass
from concourse import mybir
from concourse.alu_op_type import AluOpType as ALU

F32 = mybir.dt.float32
I32 = mybir.dt.int32
ACT = mybir.ActivationFunctionType
AX_X = mybir.AxisListType.X

P = 128
D_MODEL = 1024
SEQ = 512
DEC_B, DEC_T = 8, 4
PAST = 1024
PAGE = 128
PAGES = PAST // PAGE
NS_TOK = DEC_B * DEC_T
NTOK = SEQ + NS_TOK
PT = SEQ // P
NT = PT + 1
ST = PT
KC = D_MODEL // P
H = 8
G, HG = 2, 4
HD = 64
NOPE, ROPE, KVL, QL = 64, 32, 128, 256
QH = NOPE + ROPE
ROW = KVL + ROPE
MW = H * HD
KVW = 2 * G * HD
CMP_B, CMP_S, SELB = 32, 16, 64
WIN = 512
CH = PAST // CMP_S
CHP = SEQ // CMP_S
NBLK = PAST // SELB
SEL_TILES = NBLK + 1
GB = 4
NG = DEC_B // GB
RB = DEC_T * H
MLA_SCALE = (NOPE + ROPE) ** -0.5
NSA_SCALE = HD ** -0.5
ALPHA = 2 ** 0.25
RMS_EPS, LN_EPS = 1e-6, 1e-5
NEG = -1e30
CLAMP = 1e28

CUTS = np.cumsum([0, QL, KVL, ROPE, MW, MW, KVW, KVW, KVW, 3 * H, MW]).tolist()
BLK = [(CUTS[0], CUTS[3] - CUTS[0]), (CUTS[3], MW), (CUTS[4], MW), (CUTS[5], 2 * KVW),
       (CUTS[7], KVW + 3 * H), (CUTS[9], MW)]
B_MLA, B_ZMLA, B_Q, B_CMPSEL, B_WINGATE, B_ZNSA = range(6)
IN_W = CUTS[-1]

C_PARTS = [("ident", P), ("cosn", NT * 32), ("sinn", NT * 64), ("cosm", NT * 16), ("sinm", NT * 32),
           ("winzero", 4), ("zero", 512), ("tri", P), ("cmpmask", PT * CHP), ("newmask", NG * NS_TOK),
           ("imap", SEL_TILES), ("headsum", P), ("jidx", SEL_TILES), ("cmplast", PAST // CMP_S), ("eps", 2)]
C_AT = {}
C_W = 0
for _n, _w in C_PARTS:
    C_AT[_n] = (C_W, _w)
    C_W += _w


def rows(t):
    return P if t < PT else NS_TOK


def constants():
    c = np.zeros((P, C_W), np.float32)

    def put(name):
        a, w = C_AT[name]
        return c[:, a:a + w]

    put("ident")[:] = np.eye(P, dtype=np.float32)
    for t in range(NT):
        r = rows(t)
        pos = np.arange(r) + P * t if t < PT else PAST + np.arange(r) % DEC_T
        for d, cn, sn in ((HD, "cosn", "sinn"), (ROPE, "cosm", "sinm")):
            inv = (np.float32(1.0) / (np.float32(10000.0) ** (np.arange(0, d, 2, dtype=np.float32) / np.float32(d)))).astype(np.float32)
            ang = pos.astype(np.float32)[:, None] * inv[None, :]
            h = d // 2
            put(cn)[:r, t * h:(t + 1) * h] = np.cos(ang)
            put(sn)[:r, t * d:t * d + h] = -np.sin(ang)
            put(sn)[:r, t * d + h:(t + 1) * d] = np.sin(ang)
    p = np.arange(P)
    tok = (p // H) % DEC_T
    put("winzero")[:] = np.where(np.arange(4)[None, :] <= tok[:, None], NEG, 0.0)
    put("tri")[:] = np.where(p[None, :] > p[:, None], NEG, 0.0)
    for t in range(PT):
        n = np.arange(CHP)
        bad = (n[None, :] * CMP_S + CMP_B - 1 > (p + P * t)[:, None]) | (n[None, :] >= CHP - 1)
        put("cmpmask")[:, t * CHP:(t + 1) * CHP] = np.where(bad, NEG, 0.0)
    for g in range(NG):
        s = np.arange(NS_TOK)
        b = GB * g + p // RB
        ok = (s[None, :] // DEC_T == b[:, None]) & (s[None, :] % DEC_T <= tok[:, None])
        put("newmask")[:, g * NS_TOK:(g + 1) * NS_TOK] = np.where(ok, 0.0, NEG)
    i, j = np.arange(CH)[:, None], np.arange(SEL_TILES)[None, :]
    lo, hi = np.maximum(i * CMP_S, j * SELB), np.minimum(i * CMP_S + CMP_B, (j + 1) * SELB)
    put("imap")[:CH] = np.maximum(hi - lo, 0) / CMP_B
    put("headsum")[:] = (p[:, None] // HG == p[None, :] // HG)
    put("jidx")[:] = np.arange(SEL_TILES)[None, :]
    put("cmplast")[:, CH - 1] = NEG
    put("eps")[:] = (RMS_EPS, LN_EPS)
    return c


class Uses:

    def __init__(self, n, stages):
        self.n, self.base, at = n, {}, 0
        for name, count in stages:
            self.base[name] = at
            at += count
        self.total = at

    def at(self, name, i=0):
        return self.base[name] + i


def build(nc, io):
    STEPS = [("x", 0, 0), ("x", 0, 1)]
    POSTS = (B_MLA, B_Q, B_WINGATE)
    seq = [(b, t) for b in range(len(BLK)) for t in range(NT)]
    for n, (b, t) in enumerate(seq):
        STEPS.append(("proj", b, t))
        if b == 0 and t + 2 < NT:
            STEPS.append(("x", 0, t + 2))
        if n >= 1 and seq[n - 1][0] in POSTS:
            STEPS.append(("post", *seq[n - 1]))
    t_steps = {"x": 2, ("post", B_MLA): 1, ("post", B_Q): 2, ("post", B_WINGATE): 1}

    S = Uses(4, [("proj", len(seq)), ("bias", 1), ("hid", NT), ("qup_s", 2), ("qlat", 1)]
             + [(f"mla{g}", 3) for g in range(NG)] + [("omla", 1)]
             + [(f"{k}{g}", n) for g in range(NG) for k, n in (("cmp", 1), ("imp", 2), ("sel", 3), ("win", 2))]
             + [(f"out{ST}", 2), ("kup", HG), ("vup", PT)]
             + [(f"{k}{i}", n) for i in range(PT) for k, n in
                (("qup", 2), ("pcmp", G), ("psel", H), ("pwin", H), ("pmla", H), ("out", 2))])
    T = Uses(2, [(f"{k}{b}_{t}", t_steps[k] if k == "x" else t_steps[(k, b)]) for k, b, t in STEPS if k != "proj"]
             + [("pos", 1), ("wuk", 2), ("ch", NT * 8), ("qhead", 1)]
             + [(f"mla{g}", GB * 4 + 3) for g in range(NG)]
             + [(f"{k}{g}", n) for g in range(NG) for k, n in
                (("cmp", 1), ("selK", GB * 2), ("selP", 3), ("winK", GB), ("winP", 2))]
             + [("onsa", 1), (f"mix{ST}", 2)]
             + [(f"{k}{i}", n) for i in range(PT) for k, n in
                (("qh", 2), ("pcmp", G), ("psel", H), ("pwin", H), ("pmla", H), ("mix", 2))])
    O = Uses(2, [("cmp", NT)] + [(f"mla{g}", 1) for g in range(NG)] + [(f"nsa{g}", 1) for g in range(NG)]
             + [(f"{k}{i}", 1) for i in range(PT) for k in ("pcmp", "psel", "pwin", "pmla")])
    SLOT = 2048
    R = Uses(5, [("ch", 2 * NT)] + [(f"mla{g}", GB) for g in range(NG)]
             + [(f"{k}{g}", n) for g in range(NG) for k, n in (("sel", GB), ("win", GB // 2))])
    r_dmas = {}
    for u in range(2 * NT):
        r_dmas[R.at("ch", u)] = 2 * PAGES if u < 2 * PT else 1
    for g in range(NG):
        for b in range(GB):
            r_dmas[R.at(f"mla{g}", b)] = PAGES
            r_dmas[R.at(f"sel{g}", b)] = PAGES
        for b in range(GB // 2):
            r_dmas[R.at(f"win{g}", b)] = 2

    def ring_landed(u):
        return 16 * sum(r_dmas[v] for v in range(u % R.n, u + 1, R.n))

    KINDS = ("pcmp", "psel", "pwin", "pmla")
    UNITS = [(i, kind, h, S.at(f"{kind}{i}", h), T.at(f"{kind}{i}", h)) for i in range(PT) for kind in KINDS
             for h in range(G if kind == "pcmp" else H)]
    NU = len(UNITS) // PT
    LAST = {G - 1: "pcmp", G + H - 1: "psel", G + 2 * H - 1: "pwin", NU - 1: "pmla"}
    T_LAG, V_LAG = 2, 3
    ORDER = [ST] + list(range(PT))

    with ExitStack() as ctx:
        def sb(name, parts, cols, dt=F32):
            return ctx.enter_context(nc.sbuf_tensor(name, [parts, cols], dt))

        def sem(name):
            return ctx.enter_context(nc.semaphore(name))

        psum = ctx.enter_context(nc.psum_tensor("psum", [P, 8, 512], F32))

        def sbank(u):
            return psum[:, u % S.n, :]

        def tbank(u):
            return psum[:, 4 + u % T.n, :]

        def obank(u):
            return psum[:, 6 + u % O.n, :]

        const = sb("const", P, C_W)
        gains = sb("gains", P, QL + KVL)
        wuq = sb("wuq", P, 2 * H * QH)
        wuk = sb("wuk", P, H * NOPE)
        wuv = sb("wuv", P, H * HD)
        w2 = sb("w2", HD, 2 * HD)
        b1 = sb("b1", HD, 2)
        wring = sb("wring", P, 2 * 4096)
        row = sb("row", P, NT * ROW)
        zsil = sb("zsil", P, NT * 2 * MW)
        kv = sb("kv", P, NT * 3 * KVW)
        gate = sb("gate", P, NT * 3 * H)
        cqT = sb("cqT", P, 2 * NTOK)
        ckvT = sb("ckvT", P, NTOK)
        krT = sb("krT", QH, NTOK)
        selKT = sb("selKT", P, NTOK)
        winKT = sb("winKT", P, NTOK)
        qnT = sb("qnT", P, HG * NTOK)
        qrT = sb("qrT", P, HG * NTOK)
        small = sb("small", P, 256)
        rtmp = sb("rtmp", P, 2 * 512)
        ring = sb("ring", P, R.n * SLOT)
        mid = sb("mid", P, 4096)
        w1h = sb("w1h", P, 2048 + 1536)
        bufA = sb("bufA", P, 4864)
        comp = sb("comp", P, 2080)
        ptab = sb("ptab", 1, DEC_B * PAGES, I32)
        gdram = nc.dram_tensor("gate_rows", [3, DEC_B * RB], F32).ap()

        def C(name):
            a, w = C_AT[name]
            return const[:, a:a + w]

        ident = C("ident")
        wr = wring[:, :].rearrange("p (s c n) -> p s c n", s=2, c=KC)
        wo = wring[:, :].rearrange("p (c n) -> p c n", c=KC)
        row3 = row[:, :].rearrange("p (t n) -> p t n", t=NT)
        zs = zsil[:, :].rearrange("p (t n) -> p t n", t=NT)
        kv3 = kv[:, :].rearrange("p (t n) -> p t n", t=NT)
        gate3 = gate[:, :].rearrange("p (t n) -> p t n", t=NT)
        cqT3 = cqT[:, :].rearrange("p (c t) -> p c t", c=2)
        qnT3 = qnT[:, :].rearrange("p (h t) -> p h t", h=HG)
        qrT3 = qrT[:, :].rearrange("p (h t) -> p h t", h=HG)
        wuq3 = wuq[:, :].rearrange("p (c n) -> p c n", c=2)

        class Carve:

            def __init__(self, buf):
                self.buf, self.at = buf, 0

            def __call__(self, n, parts=P):
                self.at += n
                assert self.at <= self.buf.shape[1]
                return self.buf[0:parts, self.at - n:self.at]

        take = Carve(bufA)
        xT = take(KC * NTOK).rearrange("p (c t) -> p c t", c=KC)
        take = Carve(mid)
        xin = take(2048).rearrange("p (s n) -> p s n", s=2)
        araw = take(2 * 416).rearrange("p (s n) -> p s n", s=2)
        peN = take(256, 16)
        peT = take(32).rearrange("p (k n) -> p k n", k=2)
        chT = mid[:, :].rearrange("p (k g c n) -> p k g c n", k=2, g=G, c=8)
        take = Carve(comp)
        qraw = take(1024).rearrange("p (s n) -> p s n", s=2)
        qrot = take(1024).rearrange("p (s n) -> p s n", s=2)
        take = Carve(comp)
        kcT = take(NTOK)
        vc = take(DEC_B * P, CH).rearrange("p (b n) -> p b n", b=DEC_B)
        vcbd = take(G * HG * HD).rearrange("p (g n) -> p g n", g=G)
        take = Carve(w1h)
        w1 = take(2048).rearrange("p (k c r e) -> p k c r e", k=2, c=8, r=2)
        ezr = w1h[:, 2048:3072].rearrange("p (s n) -> p s n", s=2)
        hsh = take(512, HD).rearrange("p (k g n) -> p k g n", k=2, g=G)
        hid = take(512, HD).rearrange("p (k g n) -> p k g n", k=2, g=G)
        hez = take(512, HD).rearrange("p (k g n) -> p k g n", k=2, g=G)
        SR = DEC_B * RB
        take = Carve(bufA)
        qnbd, qrbd = take(SR), take(SR)
        qlatT = take(SR)
        qrope = take(SR)
        krp = mid[0:ROPE, 2048:4096].rearrange("p (s n) -> p s n", s=2)
        Ps = take(PAST + NS_TOK)
        olatT = take(SR)
        qm_s = take(H * QH)
        qhT = take(H * NS_TOK, NOPE)
        wukT = take(H * P, NOPE)
        take = Carve(w1h)
        kt = take(2048).rearrange("p (s n) -> p s n", s=2)
        PTs = take(9 * P).rearrange("p (k n) -> p k n", k=9)
        oTs = take(HG * NS_TOK).rearrange("p (h t) -> p h t", h=HG)
        PcT = take(256, CH).rearrange("p (v n) -> p v n", v=2)
        take = Carve(ring)
        QT = take(2048, QH).rearrange("p (s h n) -> p s h n", s=2, h=H)
        KT = take(4096, QH).rearrange("p (h n) -> p h n", h=H)
        Vm = take(2048).rearrange("p (t n) -> p t n", t=PT)
        Pp = take(2048).rearrange("p (s n) -> p s n", s=4)
        PTp = mid[:, 0:2048].rearrange("p (s n) -> p s n", s=4)
        take = Carve(bufA)
        mixT = take(KC * P).rearrange("p (c n) -> p c n", c=KC)
        acc = take(MW)
        yb = take(2 * D_MODEL).rearrange("p (s n) -> p s n", s=2)
        qm_p = take(H * QH)
        otmp = take(MW)
        take = Carve(w1h)
        lng, lnb = take(D_MODEL), take(D_MODEL)
        take = Carve(small)
        ssq = take(2 * NT).rearrange("p (t n) -> p t n", t=NT)
        rstd = take(2 * NT).rearrange("p (t n) -> p t n", t=NT)
        nmin = take(4)
        lsum, rl = take(1), take(1)
        grow = take(6).rearrange("p (b g) -> p b g", b=3)
        impr, impm, dropb = take(SEL_TILES), take(SEL_TILES), take(SEL_TILES)
        selc = take(2)
        biasv = take(2, HD)
        nmp = take(4 * H).rearrange("p (s h) -> p s h", s=4)
        lp = take(4 * H).rearrange("p (s h) -> p s h", s=4)
        coef = take(H)
        bnst = take(12).rearrange("p (s n) -> p s n", s=2)
        bnag = take(2)
        lnr = take(1)

        s_full = [sem(f"s_full{i}") for i in range(S.n)]
        s_free = [sem(f"s_free{i}") for i in range(S.n)]
        t_full = [sem(f"t_full{i}") for i in range(T.n)]
        t_free = [sem(f"t_free{i}") for i in range(T.n)]
        o_full = [sem(f"o_full{i}") for i in range(O.n)]
        o_free = [sem(f"o_free{i}") for i in range(O.n)]
        r_land = [sem(f"r_land{i}") for i in range(R.n)]
        sel_read = sem("sel_read")
        const_in, page_in, wsmall_in, pos_in, wo_in, ln_in = (
            sem(n) for n in ("const_in", "page_in", "wsmall_in", "pos_in", "wo_in", "ln_in"))
        x_in = [sem(f"x_in{i}") for i in range(2)]
        w_in = [sem(f"w_in{i}") for i in range(2)]
        y_in = [sem(f"y_in{i}") for i in range(2)]
        y_out = [sem(f"y_out{i}") for i in range(2)]
        cmp_out, rows_out, win_copy, grow_out, grow_in = (
            sem(n) for n in ("cmp_out", "rows_out", "win_copy", "grow_out", "grow_in"))
        roped = sem("roped")
        sqrt_done = sem("sqrt_done")
        normed = sem("normed")
        z_done = sem("z_done")
        gate_done = sem("gate_done")
        bias_done = sem("bias_done")
        h_shift, h_exp, h_done = sem("h_shift"), sem("h_exp"), sem("h_done")
        q_roped_s = sem("q_roped_s")
        bd_ready = sem("bd_ready")
        sp_min, sp_exp, sp_norm = sem("sp_min"), sem("sp_exp"), sem("sp_norm")
        mixed = sem("mixed")
        key_rows = sem("key_rows")
        q_roped_p = sem("q_roped_p")
        p_exp = sem("p_exp")
        y_var, y_sqrt, y_done = sem("y_var"), sem("y_sqrt"), sem("y_done")
        act_own, dve_own, pool_own = sem("act_own"), sem("dve_own"), sem("pool_own")

        def own(eng, s):
            count = [0]

            def f(ins):
                count[0] += 1
                ins.then_inc(s, 1)
                eng.wait_ge(s, count[0])
            return f

        def chunks_out(copy, arrive, t, k, j):
            n = P if t < PT else CHP
            u = T.at("ch", t * 8 + k * 4 + j)
            bank = arrive(u)[:, 0:4 * n].rearrange("p (c z n) -> p c z n", c=2, z=2)
            for g in range(G):
                for z in range(2):
                    ins = copy(chT[z * HD:(z + 1) * HD, k, g, 2 * j:2 * j + 2, 0:n],
                               bank[g * HD:(g + 1) * HD, :, z, :])
            ins.then_inc(t_free[u % T.n], 1)

        block = ctx.enter_context(nc.Block())

        @block.sync
        def _(sp):
            def load_x(t):
                if t >= 2:
                    u = T.at(f"x0_{t - 2}", 1)
                    sp.wait_ge(t_full[u % T.n], u // T.n + 1)
                src = (io["x_prompt"][0, t * P:(t + 1) * P] if t < PT
                       else io["x_sample"].rearrange("b t d -> (b t) d"))
                sp.dma_start(xin[0:rows(t), t % 2, :], src).then_inc(x_in[t % 2], 16)

            def load_w(b):
                if b >= 2:
                    u = S.at("proj", (b - 1) * NT - 1)
                    sp.wait_ge(s_full[u % S.n], u // S.n + 1)
                a, w = BLK[b]
                src = io["w_in"][0].rearrange("(c p) n -> p c n", p=P)[:, :, a:a + w]
                sp.dma_start(wr[:, b % 2, :, 0:w], src).then_inc(w_in[b % 2], 16)

            def page(b, k):
                return sp.value_load(ptab[0:1, b * PAGES + k:b * PAGES + k + 1], min_val=0,
                                     max_val=io["cache_mla"].shape[1] - 1)

            def ring_slot(u):
                v = u - R.n
                for name, count in (("ch", 2 * NT), ("mla0", GB), ("mla1", GB), ("sel0", GB), ("win0", GB // 2),
                                    ("sel1", GB)):
                    k = v - R.base[name]
                    if not 0 <= k < count:
                        continue
                    if name == "ch":
                        n = T.at("ch", k // 2 * 8 + 5 + 2 * (k % 2))
                        sp.wait_ge(t_full[n % T.n], n // T.n + 1)
                    elif name[:3] == "sel":
                        sp.wait_ge(sel_read, int(name[3]) * GB + k + 1)
                    else:
                        n = O.at({"mla": "mla", "win": "nsa"}[name[:3]] + name[3])
                        sp.wait_ge(o_full[n % O.n], n // O.n + 1)
                return ring[:, (u % R.n) * SLOT:(u % R.n + 1) * SLOT]

            def load_chunks(t):
                ua, ub = R.at("ch", 2 * t), R.at("ch", 2 * t + 1)
                da, db = ring_slot(ua), ring_slot(ub)
                if t == PT:
                    sp.wait_ge(cmp_out, 16 * NT)
                    src = io["p_cmp"].rearrange("a b (c s) k g d -> (a b c) (s k g d)", s=CMP_S)
                    sp.dma_start(da[0:CHP, :], src[:, 0:SLOT]).then_inc(r_land[ua % R.n], 16)
                    sp.dma_start(db[0:CHP, :], src[:, SLOT:]).then_inc(r_land[ub % R.n], 16)
                    return
                cache = io["cache_cmp_kv"][0].rearrange("n (c s) k g d -> n c (s k g d)", s=CMP_S)
                for s in range(2):
                    for k in range(PAGES):
                        n = page(2 * t + s, k)
                        o = s * CH + k * (PAGE // CMP_S)
                        src = cache[bass.ds(n, 1)].rearrange("a c f -> (a c) f")
                        sp.dma_start(da[o:o + 8, :], src[:, 0:SLOT]).then_inc(r_land[ua % R.n], 16)
                        sp.dma_start(db[o:o + 8, :], src[:, SLOT:]).then_inc(r_land[ub % R.n], 16)

            def load_pages(u, b, cache, w):
                dst = ring_slot(u)[:, 0:PAGES * w].rearrange("p (k n) -> p k n", k=PAGES)
                for k in range(PAGES):
                    n = page(b, k)
                    sp.dma_start(dst[:, k, :], cache[bass.ds(n, 1)].rearrange("a t f -> (a t) f")).then_inc(
                        r_land[u % R.n], 16)

            sp.dma_start(const[:, :], io["const"]).then_inc(const_in, 16)
            load_x(0)
            load_x(1)
            load_w(0)
            sp.dma_start(gains[:, 0:QL], io["q_norm_g"][0].partition_broadcast(P)).then_inc(wsmall_in, 16)
            sp.dma_start(gains[:, QL:], io["kv_norm_g"][0].partition_broadcast(P)).then_inc(wsmall_in, 16)
            load_x(2)
            sp.dma_start(wuk[:, :], io["w_uk"][0]).then_inc(wsmall_in, 16)
            sp.dma_start(wuv[:, :], io["w_uv"][0]).then_inc(wsmall_in, 16)
            sp.dma_start(wuq3, io["w_uq"][0].rearrange("(c p) n -> p c n", p=P)).then_inc(wsmall_in, 16)
            load_w(1)
            load_x(3)
            for k in range(2):
                for r in range(2):
                    sp.dma_start(w1[:, k, :, r, :],
                                 io["cmp_w1"][0, k, r * CMP_S:(r + 1) * CMP_S].rearrange(
                                     "(c q) d e -> (q d) c e", q=2)).then_inc(wsmall_in, 16)
            sp.dma_start(w2[:, :].rearrange("p (k n) -> p k n", k=2),
                         io["cmp_w2"][0].rearrange("k e d -> e k d")).then_inc(wsmall_in, 16)
            with nc.allow_non_contiguous_dma(reason="128 values"):
                sp.dma_start(b1[:, :], io["cmp_b1"][0].rearrange("k e -> e k")).then_inc(wsmall_in, 16)
            for k in range(2):
                sp.dma_start(peN[:, k * P:(k + 1) * P].rearrange("p (q d) -> p q d", q=2),
                             io["cmp_pos_emb"][0, :, k].rearrange("(n q) d -> n q d", q=2)).then_inc(pos_in, 16)
            sp.dma_start(ptab[:, :], io["page_table"].rearrange("b k -> (b k)").unsqueeze(0)).then_inc(page_in, 16)
            load_x(4)
            sp.wait_ge(page_in, 16)
            load_chunks(0)
            load_chunks(1)
            load_w(2)
            load_w(3)
            load_w(4)
            sp.dma_start(io["s_win"][0, :, 0:WIN - DEC_T].rearrange("b t k g d -> b (t k g d)"),
                         io["state_win_kv"][0, :, DEC_T:].rearrange("b t k g d -> b (t k g d)")).then_inc(win_copy, 16)
            for t in range(NT):
                u = S.at("proj", B_CMPSEL * NT + t)
                sp.wait_ge(s_free[u % S.n], u // S.n + 1)
                dst = (io["p_cmp"][0, 0, t * P:(t + 1) * P] if t < PT
                       else io["s_cmp"][0].rearrange("b t k g d -> (b t) k g d"))
                sp.dma_start(dst.rearrange("t k g d -> t (k g d)"), kv3[0:rows(t), t, 0:KVW]).then_inc(cmp_out, 16)
            load_w(5)
            for t in range(NT):
                sp.wait_ge(normed, t + 1)
                sp.wait_ge(roped, t + 1)
                dst = io["p_mla"][0, 0, t * P:(t + 1) * P] if t < PT else io["s_mla"][0].rearrange("b t f -> (b t) f")
                sp.dma_start(dst, row3[0:rows(t), t, :]).then_inc(rows_out, 16)
            for t in range(NT):
                sp.wait_ge(roped, 3 * NT + t + 1)
                r = rows(t)
                dst = (io["p_sel"][0, 0, t * P:(t + 1) * P] if t < PT
                       else io["s_sel"][0].rearrange("b t k g d -> (b t) k g d"))
                sp.dma_start(dst.rearrange("t k g d -> t (k g d)"), kv3[0:r, t, KVW:2 * KVW]).then_inc(rows_out, 16)
                if t < PT:
                    sp.dma_start(io["p_win"][0, 0, t * P:(t + 1) * P].rearrange("t k g d -> t (k g d)"),
                                 kv3[0:r, t, 2 * KVW:]).then_inc(rows_out, 16)
                else:
                    for b in range(DEC_B):
                        sp.dma_start(io["s_win"][0, b, WIN - DEC_T:].rearrange("t k g d -> t (k g d)"),
                                     kv3[b * DEC_T:(b + 1) * DEC_T, t, 2 * KVW:]).then_inc(rows_out, 16)
            sp.wait_ge(gate_done, NT)
            with nc.allow_non_contiguous_dma(reason="768 values"):
                sp.dma_start(gdram.rearrange("b (t h) -> t b h", h=H),
                             gate3[0:NS_TOK, ST, :].rearrange("p (b h) -> p b h", b=3)).then_inc(grow_out, 16)
                sp.wait_ge(grow_out, 16)
                sp.dma_start(grow, gdram.rearrange("b (g p) -> p b g", p=P)).then_inc(grow_in, 16)
            u = S.at("proj", len(seq) - 1)
            sp.wait_ge(s_full[u % S.n], u // S.n + 1)
            for t in range(2, NT):
                load_chunks(t)
            for g in range(NG):
                for b in range(GB):
                    load_pages(R.at(f"mla{g}", b), g * GB + b, io["cache_mla"][0], ROW)
            sp.dma_start(wo, io["w_o"][0].rearrange("(c p) n -> p c n", p=P)).then_inc(wo_in, 16)
            for g in range(NG):
                for b in range(GB):
                    load_pages(R.at(f"sel{g}", b), g * GB + b,
                               io["cache_sel_kv"][0].rearrange("n t k g d -> n t (k g d)"), KVW)
                for b in range(GB // 2):
                    u = R.at(f"win{g}", b)
                    dst = ring_slot(u).rearrange("p (b k n) -> p b k n", b=2, n=KVW)
                    for c in range(2):
                        src = io["state_win_kv"][0, g * GB + 2 * b + c].rearrange("(k p) z g d -> p k (z g d)", p=P)
                        sp.dma_start(dst[:, c], src).then_inc(r_land[u % R.n], 16)
            u = S.at(f"win{NG - 1}", 0)
            sp.wait_ge(s_full[u % S.n], u // S.n + 1)
            sp.dma_start(lng, io["ln_g"][0].partition_broadcast(P)).then_inc(ln_in, 16)
            sp.dma_start(lnb, io["ln_b"][0].partition_broadcast(P)).then_inc(ln_in, 16)
            u = T.at("onsa")
            sp.wait_ge(t_full[u % T.n], u // T.n + 1)

            def store_y(n):
                t = ORDER[n]
                sp.wait_ge(y_done, n + 1)
                dst = (io["y_prompt"][0, t * P:(t + 1) * P] if t < PT
                       else io["y_sample"].rearrange("b t d -> (b t) d"))
                sp.dma_start(dst, yb[0:rows(t), n % 2, :]).then_inc(y_out[n % 2], 16)

            for n, t in enumerate(ORDER):
                if n >= 2:
                    sp.wait_ge(y_out[n % 2], 16 * (n // 2))
                src = (io["x_prompt"][0, t * P:(t + 1) * P] if t < PT
                       else io["x_sample"].rearrange("b t d -> (b t) d"))
                sp.dma_start(yb[0:rows(t), n % 2, :], src).then_inc(y_in[n % 2], 16)
                if n >= 1:
                    store_y(n - 1)
            store_y(NT - 1)
            sp.wait_ge(y_out[0], 16 * ((NT + 1) // 2))
            sp.wait_ge(y_out[1], 16 * (NT // 2))
            sp.wait_ge(win_copy, 16)
            sp.wait_ge(rows_out, 16 * (NT + 2 * PT + 1 + DEC_B))

        @block.tensor
        def _(pe):
            def s_claim(u):
                if u >= S.n:
                    pe.wait_ge(s_free[u % S.n], u // S.n)
                return sbank(u)

            def t_claim(u):
                if u >= T.n:
                    pe.wait_ge(t_free[u % T.n], u // T.n)
                return tbank(u)

            def o_claim(u):
                if u >= O.n:
                    pe.wait_ge(o_free[u % O.n], u // O.n)
                return obank(u)

            def s_copied(u):
                pe.wait_ge(s_free[u % S.n], u // S.n + 1)

            def t_copied(u):
                pe.wait_ge(t_free[u % T.n], u // T.n + 1)

            def turn(out, in_):
                return pe.transpose(out, in_, ident[0:in_.shape[0], 0:in_.shape[0]])

            def turn_x(t):
                pe.wait_ge(x_in[t % 2], 16 * (t // 2 + 1))
                r = rows(t)
                for j in range(2):
                    u = T.at(f"x0_{t}", j)
                    bank = t_claim(u)
                    for c in range(4):
                        k = 4 * j + c
                        ins = turn(bank[:, c * r:(c + 1) * r], xin[0:r, t % 2, k * P:(k + 1) * P])
                    ins.then_inc(t_full[u % T.n], 1)

            def project(b, t):
                if t == 0:
                    pe.wait_ge(w_in[b % 2], 16 * (b // 2 + 1))
                if b == 0:
                    t_copied(T.at(f"x0_{t}", 0))
                    t_copied(T.at(f"x0_{t}", 1))
                w = BLK[b][1]
                u = S.at("proj", b * NT + t)
                bank = s_claim(u)
                for c in range(KC):
                    ins = pe.matmul(bank[0:rows(t), 0:w], xT[:, c, t * P:t * P + rows(t)], wr[:, b % 2, c, 0:w],
                                    start=(c == 0), stop=(c == KC - 1))
                ins.then_inc(s_full[u % S.n], 1)

            def post(b, t):
                r = rows(t)
                if b == B_MLA:
                    pe.wait_ge(normed, t + 1)
                    pe.wait_ge(roped, t + 1)
                    u = T.at(f"post{b}_{t}")
                    bank = t_claim(u)
                    for c in range(2):
                        turn(bank[:, c * r:(c + 1) * r], araw[0:r, t % 2, c * P:(c + 1) * P])
                    turn(bank[:, 2 * r:3 * r], row3[0:r, t, 0:KVL])
                    turn(bank[0:QH, 3 * r:4 * r], row3[0:r, t, ROW - QH:ROW]).then_inc(t_full[u % T.n], 1)
                elif b == B_Q:
                    for v, src in enumerate((qraw, qrot)):
                        if v == 0:
                            s_copied(S.at("proj", b * NT + t))
                        else:
                            pe.wait_ge(roped, NT + t + 1)
                        u = T.at(f"post{b}_{t}", v)
                        bank = t_claim(u)
                        for hh in range(HG):
                            ins = turn(bank[:, hh * r:(hh + 1) * r], src[0:r, t % 2, hh * P:(hh + 1) * P])
                        ins.then_inc(t_full[u % T.n], 1)
                else:
                    pe.wait_ge(roped, 3 * NT + t + 1)
                    u = T.at(f"post{b}_{t}")
                    bank = t_claim(u)
                    turn(bank[:, 0:r], kv3[0:r, t, KVW:KVW + G * HD])
                    turn(bank[:, r:2 * r], kv3[0:r, t, 2 * KVW:2 * KVW + G * HD]).then_inc(t_full[u % T.n], 1)

            pe.wait_ge(const_in, 16)
            for kind, b, t in STEPS:
                if kind == "x":
                    turn_x(t)
                elif kind == "proj":
                    project(b, t)
                else:
                    post(b, t)

            pe.wait_ge(pos_in, 32)
            u = T.at("pos")
            bank = t_claim(u)
            for k in range(2):
                ins = turn(bank[:, 16 * k:16 * k + 16], peN[:, k * P:(k + 1) * P])
            ins.then_inc(t_full[u % T.n], 1)
            pe.wait_ge(wsmall_in, 16 * 11)
            t_copied(u)
            u = S.at("bias")
            bank = s_claim(u)
            for k in range(2):
                for r in range(2):
                    for c in range(8):
                        ins = pe.matmul(bank[0:HD, k:k + 1], w1[:, k, c, r, :], peT[:, k, 8 * r + c:8 * r + c + 1],
                                        start=(r == 0 and c == 0), stop=(r == 1 and c == 7))
            ins.then_inc(s_full[u % S.n], 1)
            for j in range(2):
                u = T.at("wuk", j)
                bank = t_claim(u)
                for c in range(4):
                    h = 4 * j + c
                    ins = turn(bank[0:NOPE, c * P:(c + 1) * P], wuk[:, h * NOPE:(h + 1) * NOPE])
                ins.then_inc(t_full[u % T.n], 1)

            def nchunks(t):
                return P if t < PT else CHP

            def hidden(t, k, bank):
                n = nchunks(t)
                for j in range(4):
                    t_copied(T.at("ch", t * 8 + k * 4 + j))
                for g in range(G):
                    q = (k * G + g) * P
                    for c in range(8):
                        ins = pe.matmul(bank[:, q:q + n], w1[:, k, c, :, :].rearrange("p r e -> p (r e)"),
                                        chT[:, k, g, c, 0:n], start=(c == 0), stop=(c == 7))
                return ins

            def compress(t):
                n = nchunks(t)
                uh = S.at("hid", t)
                bank_h = s_claim(uh)
                for k in range(2):
                    for j in range(4):
                        ur = R.at("ch", 2 * t + j // 2)
                        if k == 0 and j % 2 == 0:
                            pe.wait_ge(r_land[ur % R.n], ring_landed(ur))
                        src = ring[0:n, (ur % R.n) * SLOT:(ur % R.n + 1) * SLOT].rearrange(
                            "p (s k f) -> p s k f", k=2, f=G * HD)
                        u = T.at("ch", t * 8 + k * 4 + j)
                        bank = t_claim(u)
                        for c in range(4):
                            ins = turn(bank[:, c * n:(c + 1) * n], src[:, j % 2 * 4 + c, k, :])
                        ins.then_inc(t_full[u % T.n], 1)
                    if k == 1:
                        hidden(t, 0, bank_h)
                hidden(t, 1, bank_h).then_inc(s_full[uh % S.n], 1)

            def compress_out(t):
                pe.wait_ge(h_done, t + 1)
                n, u = nchunks(t), O.at("cmp", t)
                bank = o_claim(u)
                wk, wv = w2[:, 0:HD], w2[:, HD:2 * HD]
                for g in range(G):
                    pe.matmul(bank[g * HD:(g + 1) * HD, 0:n], wk, hid[:, 0, g, 0:n], start=True, stop=True)
                for g in range(G):
                    if t < PT:
                        for s in range(2):
                            o = P + (s * G + g) * HD
                            ins = pe.matmul(bank[0:CH, o:o + HD], hid[:, 1, g, s * CH:(s + 1) * CH], wv,
                                            start=True, stop=True)
                    else:
                        for hh in range(HG):
                            ins = pe.matmul(bank[hh * CHP:(hh + 1) * CHP, P + g * HD:P + (g + 1) * HD],
                                            hid[:, 1, g, 0:CHP], wv, start=True, stop=True)
                ins.then_inc(o_full[u % O.n], 1)

            for t in range(NT):
                compress(t)
                if t >= 1:
                    compress_out(t - 1)
            compress_out(NT - 1)

            for half in range(2):
                u = S.at("qup_s", half)
                bank = s_claim(u)
                for c in range(2):
                    ins = pe.matmul(bank[0:NS_TOK, 0:4 * QH], cqT3[:, c, SEQ:NTOK],
                                    wuq3[:, c, half * 4 * QH:(half + 1) * 4 * QH], start=(c == 0), stop=(c == 1))
                ins.then_inc(s_full[u % S.n], 1)
            pe.wait_ge(q_roped_s, 1)
            u = T.at("qhead")
            bank = t_claim(u)
            for h in range(H):
                ins = turn(bank[0:QH, h * NS_TOK:(h + 1) * NS_TOK], qm_s[0:NS_TOK, h * QH:(h + 1) * QH])
            ins.then_inc(t_full[u % T.n], 1)
            t_copied(u)
            u = S.at("qlat")
            bank = s_claim(u)
            for h in range(H):
                ins = pe.matmul(bank[:, h * NS_TOK:(h + 1) * NS_TOK], wukT[:, h * P:(h + 1) * P],
                                qhT[:, h * NS_TOK:(h + 1) * NS_TOK], start=True, stop=True)
            ins.then_inc(s_full[u % S.n], 1)
            s_copied(u)

            def slot(u, w):
                return ring[:, (u % R.n) * SLOT:(u % R.n) * SLOT + w]

            softmaxes = [0]

            def turn_probs(u0, tiles):
                softmaxes[0] += 1
                pe.wait_ge(sp_norm, softmaxes[0])
                for j in range(0, tiles, 4):
                    u = u0 + j // 4
                    bank = t_claim(u)
                    for k in range(j, min(j + 4, tiles)):
                        w = P if k < tiles - 1 else NS_TOK
                        ins = turn(bank[0:w, (k - j) * P:(k - j + 1) * P], Ps[:, k * P:k * P + w])
                    ins.then_inc(t_full[u % T.n], 1)
                for j in range(0, tiles, 4):
                    t_copied(u0 + j // 4)

            for g in range(NG):
                cols = slice(g * P, (g + 1) * P)
                us = [S.at(f"mla{g}", j) for j in range(3)]
                banks = [s_claim(u) for u in us]
                pe.matmul(banks[2][:, 0:NS_TOK], qlatT[:, cols], ckvT[:, SEQ:NTOK], start=True, stop=False)
                pe.matmul(banks[2][:, 0:NS_TOK], qrope[NOPE:QH, cols], krT[NOPE:QH, SEQ:NTOK],
                          start=False, stop=True).then_inc(s_full[us[2] % S.n], 1)

                def pages_of(b):
                    return slot(R.at(f"mla{g}", b), PAGES * ROW).rearrange("p (k n) -> p k n", k=PAGES)

                def turn_mla(b):
                    ur = R.at(f"mla{g}", b)
                    pe.wait_ge(r_land[ur % R.n], ring_landed(ur))
                    src = pages_of(b)
                    for j in range(4):
                        u = T.at(f"mla{g}", 4 * b + j)
                        bank = t_claim(u)
                        for k in range(4):
                            page = src[:, 4 * (j % 2) + k, :]
                            if j < 2:
                                ins = turn(bank[:, k * P:(k + 1) * P], page[:, 0:KVL])
                            else:
                                ins = turn(bank[0:ROPE, k * P:(k + 1) * P], page[:, KVL:ROW])
                        ins.then_inc(t_full[u % T.n], 1)

                def score_mla(b):
                    for j in range(4):
                        t_copied(T.at(f"mla{g}", 4 * b + j))
                    rc = slice(g * P + b * RB, g * P + (b + 1) * RB)
                    for j in range(2):
                        out = banks[j][b * RB:(b + 1) * RB, :]
                        pe.matmul(out, qlatT[:, rc], kt[:, b % 2, j * 512:(j + 1) * 512], start=True, stop=False)
                        ins = pe.matmul(out, qrope[0:ROPE, rc], krp[:, b % 2, j * 512:(j + 1) * 512],
                                        start=False, stop=True)
                        if b == GB - 1:
                            ins.then_inc(s_full[us[j] % S.n], 1)

                turn_mla(0)
                for b in range(1, GB):
                    turn_mla(b)
                    score_mla(b - 1)
                score_mla(GB - 1)
                turn_probs(T.at(f"mla{g}", 4 * GB), PAGES + 1)
                uo = O.at(f"mla{g}")
                bank = o_claim(uo)
                pe.matmul(bank[:, 0:P], row3[0:NS_TOK, ST, 0:KVL], PTs[0:NS_TOK, PAGES, :], start=True, stop=False)
                for b in range(GB):
                    for k in range(PAGES):
                        ins = pe.matmul(bank[:, b * RB:(b + 1) * RB], pages_of(b)[:, k, 0:KVL],
                                        PTs[:, k, b * RB:(b + 1) * RB], start=False,
                                        stop=(b == GB - 1 and k == PAGES - 1))
                ins.then_inc(o_full[uo % O.n], 1)
            for g in range(NG):
                uo = O.at(f"mla{g}")
                pe.wait_ge(o_free[uo % O.n], uo // O.n + 1)
            u = S.at("omla")
            bank = s_claim(u)
            oh = olatT.rearrange("p (t h) -> p t h", h=H)
            for h in range(H):
                ins = pe.matmul(bank[0:NS_TOK, h * HD:(h + 1) * HD], oh[:, :, h], wuv[:, h * HD:(h + 1) * HD],
                                start=True, stop=True)
            ins.then_inc(s_full[u % S.n], 1)

            pe.wait_ge(bd_ready, 1)
            for g in range(NG):
                cols = slice(g * P, (g + 1) * P)
                u = S.at(f"cmp{g}")
                bank = s_claim(u)
                for b in range(GB):
                    bb = g * GB + b
                    ins = pe.matmul(bank[b * RB:(b + 1) * RB, 0:CH], qnbd[:, bb * RB:(bb + 1) * RB],
                                    kcT[:, bb * CH:(bb + 1) * CH], start=True, stop=True)
                ins.then_inc(s_full[u % S.n], 1)
                softmaxes[0] += 1
                pe.wait_ge(sp_norm, softmaxes[0])
                uc = T.at(f"cmp{g}")
                bank = t_claim(uc)
                turn(bank[0:CH, 0:P], Ps[:, 0:CH])
                turn(bank[0:CH, P:2 * P], Ps[:, CH:2 * CH]).then_inc(t_full[uc % T.n], 1)
                t_copied(uc)
                u = S.at(f"imp{g}", 0)
                bank = s_claim(u)
                pe.matmul(bank[:, 0:SEL_TILES], PcT[:, 0, :], C("imap")[0:CH, :], start=True,
                          stop=True).then_inc(s_full[u % S.n], 1)
                s_copied(u)
                u = S.at(f"imp{g}", 1)
                bank = s_claim(u)
                pe.matmul(bank[:, 0:SEL_TILES], C("headsum"), impr, start=True, stop=True).then_inc(s_full[u % S.n], 1)
                uo = O.at(f"nsa{g}")
                out = o_claim(uo)
                for name, kT_new, col in (("sel", selKT, KVW), ("win", winKT, 2 * KVW)):
                    pages = PAGES if name == "sel" else WIN // PAGE
                    nb = pages // 4
                    us = [S.at(f"{name}{g}", j) for j in range(nb + 1)]
                    banks = [s_claim(v) for v in us]
                    pe.matmul(banks[nb][:, 0:NS_TOK], qrbd[:, cols], kT_new[:, SEQ:NTOK], start=True,
                              stop=True).then_inc(s_full[us[nb] % S.n], 1)

                    def source(b):
                        if name == "sel":
                            u = R.at(f"sel{g}", b)
                            return u, slot(u, SLOT).rearrange("p (k n) -> p k n", k=PAGES)
                        u = R.at(f"win{g}", b // 2)
                        return u, slot(u, SLOT).rearrange("p (b k n) -> p b k n", b=2, k=4)[:, b % 2]

                    def turn_keys(b):
                        ur, src = source(b)
                        pe.wait_ge(r_land[ur % R.n], ring_landed(ur))
                        for j in range(nb):
                            u = T.at(f"{name}K{g}", nb * b + j)
                            bank = t_claim(u)
                            for k in range(4):
                                ins = turn(bank[:, k * P:(k + 1) * P], src[:, 4 * j + k, 0:G * HD])
                            ins.then_inc(t_full[u % T.n], 1)

                    def score(b):
                        rc = slice(g * P + b * RB, g * P + (b + 1) * RB)
                        for j in range(nb):
                            t_copied(T.at(f"{name}K{g}", nb * b + j))
                            ins = pe.matmul(banks[j][b * RB:(b + 1) * RB, :], qrbd[:, rc],
                                            kt[:, b % 2, j * 512:(j + 1) * 512], start=True, stop=True)
                            if b == GB - 1:
                                ins.then_inc(s_full[us[j] % S.n], 1)

                    turn_keys(0)
                    for b in range(1, GB):
                        turn_keys(b)
                        score(b - 1)
                    score(GB - 1)
                    turn_probs(T.at(f"{name}P{g}"), pages + 1)
                    pe.matmul(out[:, 0:P], kv3[0:NS_TOK, ST, col + G * HD:col + KVW], PTs[0:NS_TOK, pages, :],
                              start=(name == "sel"), stop=False)
                    if name == "sel":
                        for b in range(GB):
                            pe.matmul(out[:, b * RB:(b + 1) * RB], vc[:, g * GB + b, :],
                                      PcT[:, 1, b * RB:(b + 1) * RB], start=False, stop=False)
                    for b in range(GB):
                        for k in range(pages):
                            last = name == "win" and b == GB - 1 and k == pages - 1
                            ins = pe.matmul(out[:, b * RB:(b + 1) * RB], source(b)[1][:, k, G * HD:KVW],
                                            PTs[:, k, b * RB:(b + 1) * RB], start=False, stop=last)
                        if name == "sel":
                            ins.then_inc(sel_read, 1)
                ins.then_inc(o_full[uo % O.n], 1)
            for g in range(NG):
                uo = O.at(f"nsa{g}")
                pe.wait_ge(o_free[uo % O.n], uo // O.n + 1)
            u = T.at("onsa")
            bank = t_claim(u)
            for hh in range(HG):
                ins = turn(bank[0:NS_TOK, hh * P:(hh + 1) * P], oTs[:, hh, :])
            ins.then_inc(t_full[u % T.n], 1)

            def output(n):
                t = ORDER[n]
                r = rows(t)
                if n == 0:
                    s_copied(S.at("omla"))
                    t_copied(T.at("onsa"))
                else:
                    pe.wait_ge(mixed, 2 * n)
                for j in range(2):
                    u = T.at(f"mix{t}", j)
                    bank = t_claim(u)
                    for c in range(4):
                        ins = turn(bank[:, c * r:(c + 1) * r], zs[0:r, t, (4 * j + c) * P:(4 * j + c + 1) * P])
                    ins.then_inc(t_full[u % T.n], 1)
                t_copied(T.at(f"mix{t}", 0))
                t_copied(T.at(f"mix{t}", 1))
                for half in range(2):
                    u = S.at(f"out{t}", half)
                    bank = s_claim(u)
                    for c in range(KC):
                        ins = pe.matmul(bank[0:r, :], mixT[:, c, 0:r], wo[:, c, half * 512:(half + 1) * 512],
                                        start=(c == 0), stop=(c == KC - 1))
                    ins.then_inc(s_full[u % S.n], 1)

            pe.wait_ge(wo_in, 16)
            output(0)

            for j in range(HG):
                u = S.at("kup", j)
                bank = s_claim(u)
                pe.matmul(bank, wuk[:, j * P:(j + 1) * P], ckvT[:, 0:SEQ], start=True,
                          stop=True).then_inc(s_full[u % S.n], 1)
            for t in range(PT):
                u = S.at("vup", t)
                bank = s_claim(u)
                pe.matmul(bank, ckvT[:, t * P:(t + 1) * P], wuv[:, :], start=True,
                          stop=True).then_inc(s_full[u % S.n], 1)

            def scores(n):
                i, kind, h, u, _ = UNITS[n]
                bank = s_claim(u)
                q, keys = slice(i * P, (i + 1) * P), (i + 1) * P
                if kind == "pcmp":
                    for hh in range(HG):
                        ins = pe.matmul(bank[:, hh * CHP:(hh + 1) * CHP], qnT3[h * HD:(h + 1) * HD, hh, q],
                                        kcT[h * HD:(h + 1) * HD, SEQ:NTOK], start=True, stop=True)
                elif kind == "pmla":
                    if h == 0:
                        t_copied(T.at(f"qh{i}", 0))
                        t_copied(T.at(f"qh{i}", 1))
                    if h == 0 and i == 0:
                        for j in range(HG):
                            s_copied(S.at("kup", j))
                        pe.wait_ge(key_rows, 1)
                    ins = pe.matmul(bank[:, 0:keys], QT[:, i % 2, h, :], KT[:, h, 0:keys], start=True, stop=True)
                else:
                    g, hh = h // HG, h % HG
                    kT = selKT if kind == "psel" else winKT
                    ins = pe.matmul(bank[:, 0:keys], qrT3[g * HD:(g + 1) * HD, hh, q], kT[g * HD:(g + 1) * HD, 0:keys],
                                    start=True, stop=True)
                ins.then_inc(s_full[u % S.n], 1)

            def turn_p(n):
                i, kind, h, _, u = UNITS[n]
                pe.wait_ge(p_exp, n + 1)
                bank = t_claim(u)
                for j in range(1 if kind == "pcmp" else i + 1):
                    ins = turn(bank[:, j * P:(j + 1) * P], Pp[:, n % 4, j * P:(j + 1) * P])
                ins.then_inc(t_full[u % T.n], 1)

            def values(n):
                i, kind, h, _, u = UNITS[n]
                uo = O.at(f"{kind}{i}")
                bank = o_claim(uo) if h == 0 else obank(uo)
                t_copied(u)
                if kind == "pcmp":
                    ins = pe.matmul(bank[:, h * 256:(h + 1) * 256], PTp[:, n % 4, 0:P], vcbd[:, h, :],
                                    start=True, stop=True)
                else:
                    if kind == "pmla" and h == 0 and i == 0:
                        for t in range(PT):
                            s_copied(S.at("vup", t))
                    for j in range(i + 1):
                        if kind == "pmla":
                            v = Vm[:, j, h * HD:(h + 1) * HD]
                        else:
                            o = (KVW if kind == "psel" else 2 * KVW) + G * HD + (h // HG) * HD
                            v = kv3[:, j, o:o + HD]
                        ins = pe.matmul(bank[:, h * HD:(h + 1) * HD], PTp[:, n % 4, j * P:(j + 1) * P], v,
                                        start=(j == 0), stop=(j == i))
                if n % NU in LAST:
                    ins.then_inc(o_full[uo % O.n], 1)

            uo = O.at("cmp", NT - 1)
            pe.wait_ge(o_free[uo % O.n], uo // O.n + 1)
            for i in range(PT):
                for half in range(2):
                    u = S.at(f"qup{i}", half)
                    bank = s_claim(u)
                    for c in range(2):
                        ins = pe.matmul(bank[:, 0:4 * QH], cqT3[:, c, i * P:(i + 1) * P],
                                        wuq3[:, c, half * 4 * QH:(half + 1) * 4 * QH], start=(c == 0), stop=(c == 1))
                    ins.then_inc(s_full[u % S.n], 1)
                pe.wait_ge(q_roped_p, i + 1)
                for half in range(2):
                    u = T.at(f"qh{i}", half)
                    bank = t_claim(u)
                    for c in range(4):
                        h = 4 * half + c
                        ins = turn(bank[0:QH, c * P:(c + 1) * P], qm_p[:, h * QH:(h + 1) * QH])
                    ins.then_inc(t_full[u % T.n], 1)
                for m in range(NU + V_LAG):
                    n = i * NU + m
                    if m < NU:
                        scores(n)
                    if T_LAG <= m < NU + T_LAG:
                        turn_p(n - T_LAG)
                    if m >= V_LAG:
                        values(n - V_LAG)
                output(i + 1)

        @block.scalar
        def _(act):
            ok = own(act, act_own)

            def s_arrive(u):
                act.wait_ge(s_full[u % S.n], u // S.n + 1)
                return sbank(u)

            def t_arrive(u):
                act.wait_ge(t_full[u % T.n], u // T.n + 1)
                return tbank(u)

            def block_out(b, t):
                r, w = rows(t), BLK[b][1]
                u = S.at("proj", b * NT + t)
                bank = s_arrive(u)
                free = s_free[u % S.n]
                if b == B_MLA:
                    if t >= 2:
                        v = T.at(f"post{b}_{t - 2}")
                        act.wait_ge(t_full[v % T.n], v // T.n + 1)
                    act.copy(araw[0:r, t % 2, :], bank[0:r, 0:w]).then_inc(free, 1)
                    act.wait_ge(free, u // S.n + 1)
                    junk = zs[0:r, t, 0:QL]
                    ok(act.activation(junk, araw[0:r, t % 2, 0:QL], ACT.Square, accum_out=ssq[0:r, t, 0:1]))
                    ok(act.activation(junk[:, 0:KVL], araw[0:r, t % 2, QL:QL + KVL], ACT.Square,
                                      accum_out=ssq[0:r, t, 1:2]))
                    eps = C("eps")[0:r, 0:1]
                    act.activation(rstd[0:r, t, 0:1], ssq[0:r, t, 0:1], ACT.Sqrt, bias=eps, scale=1.0 / QL)
                    act.activation(rstd[0:r, t, 1:2], ssq[0:r, t, 1:2], ACT.Sqrt, bias=eps,
                                   scale=1.0 / KVL).then_inc(sqrt_done, 1)
                elif b in (B_ZMLA, B_ZNSA):
                    m, o = (t, 0) if b == B_ZMLA else (NT + t, MW)
                    if m >= 2:
                        act.wait_ge(z_done, m - 1)
                    act.copy(zs[0:r, t, o:o + MW], bank[0:r, :])
                    act.activation(ezr[0:r, m % 2, :], bank[0:r, :], ACT.Exp, scale=-1.0).then_inc(free, 1)
                elif b == B_Q:
                    if t >= 2:
                        v = T.at(f"post{b}_{t - 2}", 1)
                        act.wait_ge(t_full[v % T.n], v // T.n + 1)
                    act.copy(qraw[0:r, t % 2, :].rearrange("p (h g d) -> p h g d", h=HG, g=G),
                             bank[0:r, :].rearrange("p (g h d) -> p h g d", h=HG, g=G)).then_inc(free, 1)
                elif b == B_CMPSEL:
                    act.copy(kv3[0:r, t, 0:2 * KVW], bank[0:r, :]).then_inc(free, 1)
                else:
                    act.copy(kv3[0:r, t, 2 * KVW:3 * KVW], bank[0:r, 0:KVW])
                    act.activation(gate3[0:r, t, :], bank[0:r, KVW:w], ACT.Exp, scale=-1.0).then_inc(free, 1)

            act.wait_ge(const_in, 16)
            for kind, b, t in STEPS:
                if kind == "x":
                    u, r = T.at(f"x0_{t}", 0), rows(t)
                    act.copy(xT[:, 0:4, t * P:t * P + r],
                             t_arrive(u)[:, 0:4 * r].rearrange("p (c n) -> p c n", c=4)).then_inc(t_free[u % T.n], 1)
                elif kind == "proj":
                    block_out(b, t)

            for t in range(NT):
                n = P if t < PT else CHP
                for k in range(2):
                    for j in (0, 2):
                        chunks_out(act.copy, t_arrive, t, k, j)
                bank = s_arrive(S.at("hid", t))
                bh = bank[HD:P, :].rearrange("p (k g n) -> p k g n", k=2, g=G)
                act.copy(hsh[:, :, :, 0:n - 1], bh[:, :, :, 1:n]).then_inc(h_shift, 1)
                u = S.at("hid", t)
                act.wait_ge(s_free[u % S.n], u // S.n + 1)
                act.activation(hez[:, :, :, 0:n], hid[:, :, :, 0:n], ACT.Exp, scale=-1.0).then_inc(h_exp, 1)

            for half in range(2):
                u = S.at("qup_s", half)
                act.copy(qm_s[0:NS_TOK, half * 4 * QH:(half + 1) * 4 * QH],
                         s_arrive(u)[0:NS_TOK, 0:4 * QH]).then_inc(s_free[u % S.n], 1)
            u = S.at("qlat")
            act.copy(qlatT.rearrange("p (t h) -> p h t", h=H),
                     s_arrive(u)[:, 0:SR].rearrange("p (h t) -> p h t", h=H)).then_inc(s_free[u % S.n], 1)

            softmaxes = [0]

            def exponents(w):
                n = softmaxes[0] = softmaxes[0] + 1
                act.wait_ge(sp_min, n)
                act.activation(Ps[:, 0:w], Ps[:, 0:w], ACT.Exp, bias=nmin[:, 3:4], scale=-1.0,
                               accum_out=lsum).then_inc(sp_exp, 1)

            def keys_out(u, b, j):
                act.copy(kt[:, b % 2, j * 512:(j + 1) * 512], t_arrive(u)).then_inc(t_free[u % T.n], 1)

            def probs_out(u0, tiles):
                for j in range(0, tiles, 8):
                    u = u0 + j // 4
                    m = min(4, tiles - j)
                    bank = t_arrive(u)
                    r = NS_TOK if m == 1 else P
                    act.copy(PTs[0:r, j:j + m, :], bank[0:r, 0:m * P].rearrange("p (k n) -> p k n", k=m)).then_inc(
                        t_free[u % T.n], 1)

            for g in range(NG):
                for b in range(GB):
                    keys_out(T.at(f"mla{g}", 4 * b), b, 0)
                    u = T.at(f"mla{g}", 4 * b + 2)
                    act.copy(krp[:, b % 2, 0:512], t_arrive(u)[0:ROPE, :]).then_inc(t_free[u % T.n], 1)
                exponents(PAST + NS_TOK)
                probs_out(T.at(f"mla{g}", 4 * GB), PAGES + 1)
                u = O.at(f"mla{g}")
                act.wait_ge(o_full[u % O.n], u // O.n + 1)
                act.copy(olatT[:, g * P:(g + 1) * P], obank(u)[:, 0:P]).then_inc(o_free[u % O.n], 1)
            for g in range(NG):
                exponents(CH)
                for b in range(GB):
                    keys_out(T.at(f"selK{g}", 2 * b), b, 0)
                exponents(PAST + NS_TOK)
                probs_out(T.at(f"selP{g}"), PAGES + 1)
                for b in range(GB):
                    keys_out(T.at(f"winK{g}", b), b, 0)
                exponents(WIN + NS_TOK)
                probs_out(T.at(f"winP{g}"), WIN // PAGE + 1)

            def mix_out(t):
                u, r = T.at(f"mix{t}", 0), rows(t)
                act.copy(mixT[:, 0:4, 0:r],
                         t_arrive(u)[:, 0:4 * r].rearrange("p (c n) -> p c n", c=4)).then_inc(t_free[u % T.n], 1)

            def ln_root(n):
                r = rows(ORDER[n])
                act.wait_ge(y_var, n + 1)
                act.activation(lnr[0:r], bnag[0:r, 1:2], ACT.Sqrt, bias=C("eps")[0:r, 1:2]).then_inc(y_sqrt, 1)

            mix_out(ST)
            ln_root(0)
            for j in range(HG):
                u = S.at("kup", j)
                bank = s_arrive(u)
                act.copy(KT[0:NOPE, 2 * j, :], bank[0:NOPE, :])
                act.copy(KT[0:NOPE, 2 * j + 1, :], bank[NOPE:P, :]).then_inc(s_free[u % S.n], 1)

            def exp_unit(n):
                i, kind, h, u, _ = UNITS[n]
                k = KINDS.index(kind)
                act.wait_ge(s_free[u % S.n], u // S.n + 1)
                if kind == "pcmp":
                    for hh in range(HG):
                        c = h * HG + hh
                        ins = act.activation(Pp[:, n % 4, hh * CHP:(hh + 1) * CHP], Pp[:, n % 4, hh * CHP:(hh + 1) * CHP],
                                             ACT.Exp, bias=nmp[:, k, c:c + 1], scale=-1.0, accum_out=lp[:, k, c:c + 1])
                else:
                    w = (i + 1) * P
                    ins = act.activation(Pp[:, n % 4, 0:w], Pp[:, n % 4, 0:w], ACT.Exp, bias=nmp[:, k, h:h + 1],
                                         scale=-1.0, accum_out=lp[:, k, h:h + 1])
                ins.then_inc(p_exp, 1)

            def turned_out(n):
                i, kind, _, _, u = UNITS[n]
                w = P if kind == "pcmp" else (i + 1) * P
                act.copy(PTp[:, n % 4, 0:w], t_arrive(u)[:, 0:w]).then_inc(t_free[u % T.n], 1)

            for i in range(PT):
                for half in range(2):
                    u = S.at(f"qup{i}", half)
                    act.copy(qm_p[:, half * 4 * QH:(half + 1) * 4 * QH],
                             s_arrive(u)[:, 0:4 * QH]).then_inc(s_free[u % S.n], 1)
                u = T.at(f"qh{i}", 0)
                act.copy(QT[:, i % 2, 0:4, :],
                         t_arrive(u)[0:QH, :].rearrange("p (h n) -> p h n", h=4)).then_inc(t_free[u % T.n], 1)
                for m in range(NU + T_LAG):
                    n = i * NU + m
                    if m < NU:
                        exp_unit(n)
                    if m >= T_LAG and (n - T_LAG) % 2 == 0:
                        turned_out(n - T_LAG)
                mix_out(i)
                ln_root(i + 1)

        @block.vector
        def _(dve):
            ok = own(dve, dve_own)

            def s_arrive(u):
                dve.wait_ge(s_full[u % S.n], u // S.n + 1)
                return sbank(u)

            def t_arrive(u):
                dve.wait_ge(t_full[u % T.n], u // T.n + 1)
                return tbank(u)

            def o_arrive(u):
                dve.wait_ge(o_full[u % O.n], u // O.n + 1)
                return obank(u)

            def four(bank, n):
                return bank[:, 0:4 * n].rearrange("p (c n) -> p c n", c=4)

            def work_on(b, t):
                r = rows(t)
                u = S.at("proj", b * NT + t)
                if b == B_MLA:
                    if t == 0:
                        dve.wait_ge(wsmall_in, 16 * 11)
                    dve.wait_ge(sqrt_done, t + 1)
                    ok(dve.reciprocal(rstd[0:r, t, :], rstd[0:r, t, :]))
                    a = araw[0:r, t % 2, :]
                    dve.scalar_tensor_tensor(out=row3[0:r, t, 0:KVL], in0=a[:, QL:QL + KVL], scalar=rstd[0:r, t, 1:2],
                                             in1=gains[0:r, QL:], op0=ALU.mult, op1=ALU.mult)
                    dve.scalar_tensor_tensor(out=a[:, 0:QL], in0=a[:, 0:QL], scalar=rstd[0:r, t, 0:1],
                                             in1=gains[0:r, 0:QL], op0=ALU.mult, op1=ALU.mult).then_inc(normed, 1)
                elif b in (B_ZMLA, B_ZNSA):
                    m, o = (t, 0) if b == B_ZMLA else (NT + t, MW)
                    dve.wait_ge(s_free[u % S.n], u // S.n + 1)
                    e = ezr[0:r, m % 2, :]
                    ok(dve.tensor_scalar(e, e, 1.0, None, ALU.add))
                    ok(dve.reciprocal(e, e))
                    z = zs[0:r, t, o:o + MW]
                    dve.tensor_tensor(z, z, e, ALU.mult).then_inc(z_done, 1)
                elif b == B_WINGATE:
                    dve.wait_ge(s_free[u % S.n], u // S.n + 1)
                    e = gate3[0:r, t, :]
                    ok(dve.tensor_scalar(e, e, 1.0, None, ALU.add))
                    dve.reciprocal(e, e).then_inc(gate_done, 1)

            def post_out(b, t):
                r, c0 = rows(t), t * P
                if b == B_MLA:
                    u = T.at(f"post{b}_{t}")
                    bank = t_arrive(u)
                    dve.tensor_copy(cqT3[:, :, c0:c0 + r], bank[:, 0:2 * r].rearrange("p (c n) -> p c n", c=2))
                    dve.tensor_copy(ckvT[:, c0:c0 + r], bank[:, 2 * r:3 * r])
                    dve.tensor_copy(krT[NOPE:QH, c0:c0 + r], bank[NOPE:QH, 3 * r:4 * r]).then_inc(t_free[u % T.n], 1)
                elif b == B_Q:
                    for v, dst in enumerate((qnT3, qrT3)):
                        u = T.at(f"post{b}_{t}", v)
                        dve.tensor_copy(dst[:, :, c0:c0 + r], four(t_arrive(u), r)).then_inc(t_free[u % T.n], 1)
                else:
                    u = T.at(f"post{b}_{t}")
                    bank = t_arrive(u)
                    dve.tensor_copy(selKT[:, c0:c0 + r], bank[:, 0:r])
                    dve.tensor_copy(winKT[:, c0:c0 + r], bank[:, r:2 * r]).then_inc(t_free[u % T.n], 1)

            for kind, b, t in STEPS:
                if kind == "x":
                    u, r = T.at(f"x0_{t}", 1), rows(t)
                    dve.tensor_copy(xT[:, 4:8, t * P:t * P + r], four(t_arrive(u), r)).then_inc(t_free[u % T.n], 1)
                elif kind == "proj":
                    work_on(b, t)
                else:
                    post_out(b, t)

            u = T.at("pos")
            dve.tensor_copy(peT, t_arrive(u)[:, 0:32].rearrange("p (k n) -> p k n", k=2)).then_inc(t_free[u % T.n], 1)
            u = S.at("bias")
            dve.tensor_tensor(biasv, s_arrive(u)[0:HD, 0:2], b1[:, :], ALU.add).then_inc(s_free[u % S.n], 1)
            dve.wait_ge(s_free[u % S.n], u // S.n + 1)
            for j in range(2):
                u = T.at("wuk", j)
                dve.tensor_copy(wukT[:, j * 512:(j + 1) * 512], t_arrive(u)[0:NOPE, :]).then_inc(t_free[u % T.n], 1)
            ok(dve.memset(vcbd, 0.0))

            def compressed(t):
                u = O.at("cmp", t)
                bank = o_arrive(u)
                if t < PT:
                    dve.tensor_copy(kcT[:, t * P:(t + 1) * P], bank[:, 0:P])
                    ins = dve.tensor_copy(vc[:, 2 * t:2 * t + 2, :],
                                          bank[0:CH, P:3 * P].rearrange("p (b n) -> p b n", b=2))
                else:
                    dve.tensor_copy(kcT[:, SEQ:NTOK], bank[:, 0:CHP])
                    for hh in range(HG):
                        s = slice(hh * CHP, (hh + 1) * CHP)
                        ins = dve.tensor_copy(vcbd[s, :, hh * HD:(hh + 1) * HD],
                                              bank[s, P:2 * P].rearrange("p (g d) -> p g d", g=G))
                ins.then_inc(o_free[u % O.n], 1)

            for t in range(NT):
                n = P if t < PT else CHP
                for k in range(2):
                    for j in (1, 3):
                        chunks_out(dve.tensor_copy, t_arrive, t, k, j)
                if t >= 1:
                    compressed(t - 1)
                u = S.at("hid", t)
                bank = s_arrive(u)[0:HD, :].rearrange("p (k g n) -> p k g n", k=2, g=G)
                dve.wait_ge(h_shift, t + 1)
                dve.memset(hid[:, :, :, n - 1:n], 0.0)
                for k in range(2):
                    ins = dve.scalar_tensor_tensor(out=hid[:, k, :, 0:n - 1], in0=bank[:, k, :, 0:n - 1],
                                                   scalar=biasv[:, k:k + 1], in1=hsh[:, k, :, 0:n - 1],
                                                   op0=ALU.add, op1=ALU.add)
                ins.then_inc(s_free[u % S.n], 1)
                dve.wait_ge(h_exp, t + 1)
                e, h = hez[:, :, :, 0:n], hid[:, :, :, 0:n]
                ok(dve.tensor_scalar(e, e, 1.0, None, ALU.add))
                ok(dve.reciprocal(e, e))
                dve.tensor_tensor(h, h, e, ALU.mult).then_inc(h_done, 1)
            compressed(NT - 1)

            u = T.at("qhead")
            bank = t_arrive(u)[:, 0:H * NS_TOK]
            dve.tensor_copy(qhT, bank[0:NOPE, :])
            for p0 in (0, NOPE):
                ins = dve.tensor_copy(qrope[p0:p0 + ROPE, :].rearrange("p (t h) -> p h t", h=H),
                                      bank[NOPE:QH, :].rearrange("p (h t) -> p h t", h=H))
            ins.then_inc(t_free[u % T.n], 1)

            softmaxes = [0]

            def minima(us, masks, scale):
                at = 0
                for j, (u, mask) in enumerate(zip(us, masks)):
                    bank = s_arrive(u)
                    w = mask.shape[1] if len(mask.shape) == 2 else mask.shape[1] * mask.shape[2]
                    out, src = Ps[:, at:at + w], bank[:, 0:w]
                    if len(mask.shape) == 3:
                        out, src = (x.rearrange("p (a b) -> p a b", b=SELB) for x in (out, src))
                    ins = dve.tensor_tensor_reduce(out, src, mask, -scale, CLAMP, ALU.add, ALU.min, nmin[:, j:j + 1])
                    ins.then_inc(s_free[u % S.n], 1)
                    at += w
                n = softmaxes[0] = softmaxes[0] + 1
                for u in us:
                    dve.wait_ge(s_free[u % S.n], u // S.n + 1)
                dve.tensor_reduce(nmin[:, 3:4], nmin[:, 0:len(us)], AX_X, ALU.min).then_inc(sp_min, 1)
                dve.wait_ge(sp_exp, n)
                ok(dve.reciprocal(rl, lsum))

            def normalise(w, gates):
                if gates is None:
                    dve.tensor_scalar(Ps[:, 0:w], Ps[:, 0:w], rl, None, ALU.mult).then_inc(sp_norm, 1)
                else:
                    dve.tensor_scalar(Ps[:, 0:w], Ps[:, 0:w], rl, gates, ALU.mult, ALU.mult).then_inc(sp_norm, 1)

            def keys_out(u, b, j):
                dve.tensor_copy(kt[:, b % 2, j * 512:(j + 1) * 512], t_arrive(u)).then_inc(t_free[u % T.n], 1)

            def probs_out(u0, tiles):
                for j in range(4, tiles, 8):
                    u = u0 + j // 4
                    m = min(4, tiles - j)
                    bank = t_arrive(u)
                    r = NS_TOK if m == 1 else P
                    dve.tensor_copy(PTs[0:r, j:j + m, :],
                                    bank[0:r, 0:m * P].rearrange("p (k n) -> p k n", k=m)).then_inc(t_free[u % T.n], 1)

            zero = C("zero")
            for g in range(NG):
                for b in range(GB):
                    keys_out(T.at(f"mla{g}", 4 * b + 1), b, 1)
                    u = T.at(f"mla{g}", 4 * b + 3)
                    dve.tensor_copy(krp[:, b % 2, 512:], t_arrive(u)[0:ROPE, :]).then_inc(t_free[u % T.n], 1)
                newmask = C("newmask")[:, g * NS_TOK:(g + 1) * NS_TOK]
                minima([S.at(f"mla{g}", j) for j in range(3)], [zero, zero, newmask], MLA_SCALE)
                normalise(PAST + NS_TOK, None)
                probs_out(T.at(f"mla{g}", 4 * GB), PAGES + 1)
            u = S.at("omla")
            zm = zs[0:NS_TOK, ST, 0:MW]
            dve.tensor_tensor(zm, s_arrive(u)[0:NS_TOK, :], zm, ALU.mult).then_inc(s_free[u % S.n], 1)

            dve.wait_ge(grow_in, 16)
            for g in range(NG):
                newmask = C("newmask")[:, g * NS_TOK:(g + 1) * NS_TOK]
                minima([S.at(f"cmp{g}")], [C("cmplast")], NSA_SCALE)
                ok(dve.tensor_scalar(Ps[:, 0:CH], Ps[:, 0:CH], rl, None, ALU.mult))
                dve.tensor_scalar(Ps[:, CH:2 * CH], Ps[:, 0:CH], grow[:, 0, g:g + 1], None, ALU.mult).then_inc(sp_norm, 1)
                u = T.at(f"cmp{g}")
                dve.tensor_copy(PcT, t_arrive(u)[0:CH, 0:2 * P].rearrange("p (v n) -> p v n", v=2)).then_inc(
                    t_free[u % T.n], 1)
                u = S.at(f"imp{g}", 0)
                dve.tensor_copy(impr, s_arrive(u)[:, 0:SEL_TILES]).then_inc(s_free[u % S.n], 1)
                u = S.at(f"imp{g}", 1)
                dve.tensor_copy(impm, s_arrive(u)[:, 0:SEL_TILES]).then_inc(s_free[u % S.n], 1)
                dve.wait_ge(s_free[u % S.n], u // S.n + 1)
                mids = slice(1, SEL_TILES - 2)
                ok(dve.tensor_reduce(selc[:, 0:1], impm[:, mids], AX_X, ALU.min))
                ok(dve.scalar_tensor_tensor(out=impm[:, mids], in0=impm[:, mids], scalar=selc[:, 0:1],
                                            in1=C("jidx")[:, mids], op0=ALU.is_le, op1=ALU.mult))
                ok(dve.tensor_reduce(selc[:, 1:2], impm[:, mids], AX_X, ALU.max))
                ok(dve.tensor_scalar(dropb, C("jidx"), selc[:, 1:2], NEG, ALU.is_equal, ALU.mult))
                for b in range(GB):
                    keys_out(T.at(f"selK{g}", 2 * b + 1), b, 1)
                blocks = [dropb[:, j:j + 8].unsqueeze(2).broadcast_to([P, 8, SELB]) for j in (0, 8)]
                minima([S.at(f"sel{g}", j) for j in range(3)], blocks + [newmask], NSA_SCALE)
                normalise(PAST + NS_TOK, grow[:, 1, g:g + 1])
                probs_out(T.at(f"selP{g}"), PAGES + 1)
                a = C_AT["winzero"][0]
                minima([S.at(f"win{g}", j) for j in range(2)], [const[:, a:a + WIN], newmask], NSA_SCALE)
                normalise(WIN + NS_TOK, grow[:, 2, g:g + 1])
                probs_out(T.at(f"winP{g}"), WIN // PAGE + 1)
                u = O.at(f"nsa{g}")
                bank = o_arrive(u)
                for k in range(G):
                    s = slice(k * HD, (k + 1) * HD)
                    ins = dve.tensor_copy(
                        oTs[s, :, g * GB * DEC_T:(g + 1) * GB * DEC_T],
                        bank[s, 0:P].rearrange("p (t h) -> p h t", h=H)[:, k * HG:(k + 1) * HG, :])
                ins.then_inc(o_free[u % O.n], 1)
            u = T.at("onsa")
            zn = zs[0:NS_TOK, ST, MW:].rearrange("p (g h d) -> p h g d", g=G, h=HG)
            on = t_arrive(u)[0:NS_TOK, :].rearrange("p (h g d) -> p h g d", g=G, h=HG)
            for k in range(G):
                ins = dve.tensor_tensor(zn[:, :, k, :], on[:, :, k, :], zn[:, :, k, :], ALU.mult)
            ins.then_inc(t_free[u % T.n], 1)

            def output(n):
                t = ORDER[n]
                r = rows(t)
                u = T.at(f"mix{t}", 1)
                dve.tensor_copy(mixT[:, 4:8, 0:r], four(t_arrive(u), r)).then_inc(t_free[u % T.n], 1)
                dve.wait_ge(y_in[n % 2], 16 * (n // 2 + 1))
                y = yb[0:r, n % 2, :]
                for half in range(2):
                    u = S.at(f"out{t}", half)
                    yh = y[:, half * 512:(half + 1) * 512]
                    dve.scalar_tensor_tensor(out=yh, in0=yh, scalar=ALPHA, in1=s_arrive(u)[0:r, :],
                                             op0=ALU.mult, op1=ALU.add).then_inc(s_free[u % S.n], 1)
                    dve.wait_ge(s_free[u % S.n], u // S.n + 1)
                    ok(dve.bn_stats(bnst[0:r, half, :], yh))
                dve.bn_aggr(bnag[0:r], bnst[0:r]).then_inc(y_var, 1)
                dve.wait_ge(y_sqrt, n + 1)
                ok(dve.reciprocal(lnr[0:r], lnr[0:r]))
                ok(dve.tensor_scalar(y, y, bnag[0:r, 0:1], lnr[0:r], ALU.subtract, ALU.mult))
                if n == 0:
                    dve.wait_ge(ln_in, 32)
                ok(dve.tensor_tensor(y, y, lng[0:r], ALU.mult))
                dve.tensor_tensor(y, y, lnb[0:r], ALU.add).then_inc(y_done, 1)

            output(0)
            for t in range(PT):
                u = S.at("vup", t)
                dve.tensor_copy(Vm[:, t, :], s_arrive(u)).then_inc(s_free[u % S.n], 1)

            a_tri = C_AT["tri"][0]

            def min_unit(n):
                i, kind, h, u, _ = UNITS[n]
                k = KINDS.index(kind)
                bank = s_arrive(u)
                if kind == "pcmp":
                    for hh in range(HG):
                        s = slice(hh * CHP, (hh + 1) * CHP)
                        c = h * HG + hh
                        ins = dve.tensor_tensor_reduce(Pp[:, n % 4, s], bank[:, s],
                                                       C("cmpmask")[:, i * CHP:(i + 1) * CHP], -NSA_SCALE, CLAMP,
                                                       ALU.add, ALU.min, nmp[:, k, c:c + 1])
                else:
                    w = (i + 1) * P
                    mask = const[:, a_tri - i * P:a_tri + P]
                    ins = dve.tensor_tensor_reduce(Pp[:, n % 4, 0:w], bank[:, 0:w], mask,
                                                   -(MLA_SCALE if kind == "pmla" else NSA_SCALE), CLAMP,
                                                   ALU.add, ALU.min, nmp[:, k, h:h + 1])
                ins.then_inc(s_free[u % S.n], 1)

            def turned_out(n):
                i, kind, _, _, u = UNITS[n]
                w = P if kind == "pcmp" else (i + 1) * P
                dve.tensor_copy(PTp[:, n % 4, 0:w], t_arrive(u)[:, 0:w]).then_inc(t_free[u % T.n], 1)

            def heads(x):
                return x.rearrange("p (h d) -> p h d", h=H)

            def branch_out(i, kind):
                k = KINDS.index(kind)
                u = O.at(f"{kind}{i}")
                bank = heads(o_arrive(u))
                ok(dve.tensor_scalar(coef, lp[:, k, :], 1e-30, None, ALU.max))
                ok(dve.reciprocal(coef, coef))
                if kind != "pmla":
                    ok(dve.tensor_tensor(coef, coef, gate3[:, i, k * H:(k + 1) * H], ALU.mult))
                dst = acc if kind == "pcmp" else otmp
                dve.tensor_tensor(heads(dst), bank, coef.unsqueeze(2).broadcast_to([P, H, HD]), ALU.mult).then_inc(
                    o_free[u % O.n], 1)
                dve.wait_ge(o_free[u % O.n], u // O.n + 1)
                if kind in ("psel", "pwin"):
                    ok(dve.tensor_tensor(acc, acc, otmp, ALU.add))
                if kind == "pwin":
                    z = zs[:, i, MW:]
                    dve.tensor_tensor(z, z, acc, ALU.mult).then_inc(mixed, 1)
                if kind == "pmla":
                    z = zs[:, i, 0:MW]
                    dve.tensor_tensor(z, z, otmp, ALU.mult).then_inc(mixed, 1)

            for i in range(PT):
                u = T.at(f"qh{i}", 1)
                dve.tensor_copy(QT[:, i % 2, 4:8, :],
                                t_arrive(u)[0:QH, :].rearrange("p (h n) -> p h n", h=4)).then_inc(t_free[u % T.n], 1)
                for m in range(NU + V_LAG + 1):
                    n = i * NU + m
                    if m < NU:
                        min_unit(n)
                    if T_LAG <= m < NU + T_LAG and (n - T_LAG) % 2 == 1:
                        turned_out(n - T_LAG)
                    if m - V_LAG - 1 in LAST:
                        branch_out(i, LAST[m - V_LAG - 1])
                output(i + 1)

        @block.gpsimd
        def _(pool):
            ok = own(pool, pool_own)

            def rope(out, x, r, n, d, t, table, done):
                h = d // 2
                ta, tb = (rtmp[0:r, j * 512:j * 512 + n * d].rearrange("p (n z h) -> p n z h", n=n, z=2)
                          for j in range(2))
                cos = C("cos" + table)[0:r, t * h:(t + 1) * h]
                sin = C("sin" + table)[0:r, t * d:(t + 1) * d].rearrange("p (z h) -> p z h", z=2)
                for z in range(2):
                    pool.tensor_tensor(ta[:, :, z, :], x[:, :, z, :], cos.unsqueeze(1).broadcast_to([r, n, h]), ALU.mult)
                    ins = pool.tensor_tensor(tb[:, :, z, :], x[:, :, 1 - z, :],
                                             sin[:, z, :].unsqueeze(1).broadcast_to([r, n, h]), ALU.mult)
                ok(ins)
                ins = pool.tensor_tensor(out, ta, tb, ALU.add)
                ok(ins) if done is None else ins.then_inc(done, 1)
                if done is not None:
                    waits[done] = waits.get(done, 0) + 1
                    pool.wait_ge(done, waits[done])

            waits = {}

            def halves(x, n):
                return x.rearrange("p (n z h) -> p n z h", n=n, z=2)

            pool.wait_ge(const_in, 16)
            for b, t in seq:
                u, r = S.at("proj", b * NT + t), rows(t)
                if b not in (B_MLA, B_Q, B_CMPSEL, B_WINGATE):
                    continue
                pool.wait_ge(s_free[u % S.n], u // S.n + 1)
                if b == B_MLA:
                    rope(halves(row3[0:r, t, KVL:ROW], 1), halves(araw[0:r, t % 2, QL + KVL:], 1), r, 1, ROPE, t, "m", roped)
                elif b == B_Q:
                    if t >= 2:
                        v = T.at(f"post{b}_{t - 2}", 1)
                        pool.wait_ge(t_full[v % T.n], v // T.n + 1)
                    rope(halves(qrot[0:r, t % 2, :], H), halves(qraw[0:r, t % 2, :], H), r, H, HD, t, "n", roped)
                else:
                    o = KVW if b == B_CMPSEL else 2 * KVW
                    k = halves(kv3[0:r, t, o:o + G * HD], G)
                    rope(k, k, r, G, HD, t, "n", roped)

            u = S.at("proj", len(seq) - 1)
            pool.wait_ge(s_full[u % S.n], u // S.n + 1)
            ok(pool.memset(bufA[:, 0:2 * SR], 0.0))
            u = T.at("pos")
            pool.wait_ge(t_full[u % T.n], u // T.n + 1)
            for dst, src in ((qnbd, qnT3), (qrbd, qrT3)):
                for g in range(G):
                    s = slice(g * HD, (g + 1) * HD)
                    ins = pool.tensor_copy(dst[s].rearrange("p (t h) -> p h t", h=H)[:, g * HG:(g + 1) * HG, :],
                                           src[s, :, SEQ:NTOK])
            ins.then_inc(bd_ready, 1)

            def rope_mla(q, r, t, uses, done):
                for u in uses:
                    pool.wait_ge(s_free[u % S.n], u // S.n + 1)
                x = q[0:r].rearrange("p (n w) -> p n w", n=H)[:, :, NOPE:QH].rearrange("p n (z h) -> p n z h", z=2)
                rope(x, x, r, H, ROPE, t, "m", done)

            rope_mla(qm_s, NS_TOK, ST, [S.at("qup_s", half) for half in range(2)], q_roped_s)
            u = S.at("kup")
            pool.wait_ge(s_full[u % S.n], u // S.n + 1)
            for h in range(H):
                ins = pool.tensor_copy(KT[NOPE:QH, h, :], krT[NOPE:QH, 0:SEQ])
            ins.then_inc(key_rows, 1)
            pool.wait_ge(key_rows, 1)
            for i in range(PT):
                rope_mla(qm_p, P, i, [S.at(f"qup{i}", half) for half in range(2)], q_roped_p)

    return nc


_INS = ["x_prompt", "x_sample", "cache_mla", "cache_cmp_kv", "cache_sel_kv", "state_win_kv", "page_table", "w_in",
        "q_norm_g", "w_uq", "kv_norm_g", "w_uk", "w_uv", "cmp_pos_emb", "cmp_w1", "cmp_b1", "cmp_w2", "w_o",
        "ln_g", "ln_b"]
_OUTS = [("y_prompt", (1, SEQ, D_MODEL)), ("y_sample", (DEC_B, DEC_T, D_MODEL)), ("p_mla", (1, 1, SEQ, ROW)),
         ("p_cmp", (1, 1, SEQ, 2, G, HD)), ("p_sel", (1, 1, SEQ, 2, G, HD)), ("p_win", (1, 1, SEQ, 2, G, HD)),
         ("s_mla", (1, DEC_B, DEC_T, ROW)), ("s_cmp", (1, DEC_B, DEC_T, 2, G, HD)),
         ("s_sel", (1, DEC_B, DEC_T, 2, G, HD)), ("s_win", (1, DEC_B, WIN, 2, G, HD))]
OUT_NAMES = [f"out_{name}" for name, _ in _OUTS]


def kernel(**inputs):
    import concourse.bacc as bacc
    from concourse.bass_utils import run_bass_kernel_spmd

    nc = bacc.Bacc("TRN2", target_bir_lowering=False, num_devices=1, dynamic_dma_scratch_size=1024)
    arrays, io = {}, {}
    for name in _INS:
        a = np.ascontiguousarray(inputs[name])
        arrays[f"in_{name}"] = a
        io[name] = nc.dram_tensor(f"in_{name}", a.shape, mybir.dt.from_np(a.dtype), kind="ExternalInput").ap()
    arrays["in_const"] = constants()
    io["const"] = nc.dram_tensor("in_const", (P, C_W), F32, kind="ExternalInput").ap()
    for name, shape in _OUTS:
        io[name] = nc.dram_tensor(f"out_{name}", shape, F32, kind="ExternalOutput").ap()
    build(nc, io)
    r = run_bass_kernel_spmd(nc, [arrays], core_ids=[0])
    return tuple(r.results[0][n] for n in OUT_NAMES)
```

```python
import math
from contextlib import ExitStack

import numpy as np

import concourse.bass as bass
from concourse import mybir
from concourse.alu_op_type import AluOpType as ALU

F32 = mybir.dt.float32
I32 = mybir.dt.int32
ACT = mybir.ActivationFunctionType
AX_X = mybir.AxisListType.X

P = 128
D_MODEL = 1024
SEQ = 512
DEC_B, DEC_T = 8, 4
PAST = 1024
PAGE = 128
PAGES = PAST // PAGE
NS_TOK = DEC_B * DEC_T
NTOK = SEQ + NS_TOK
PT = SEQ // P
NT = PT + 1
ST = PT
KC = D_MODEL // P
H = 8
G, HG = 2, 4
HD = 64
NOPE, ROPE, KVL, QL = 64, 32, 128, 256
QH = NOPE + ROPE
ROW = KVL + ROPE
MW = H * HD
KVW = 2 * G * HD
CMP_B, CMP_S, SELB = 32, 16, 64
WIN = 512
CH = PAST // CMP_S
CHP = SEQ // CMP_S
NBLK = PAST // SELB
SEL_TILES = NBLK + 1
GB = 4
NG = DEC_B // GB
RB = DEC_T * H
MLA_SCALE = (NOPE + ROPE) ** -0.5
NSA_SCALE = HD ** -0.5
ALPHA = 2 ** 0.25
RMS_EPS, LN_EPS = 1e-6, 1e-5
NEG = -1e30
CLAMP = 1e28

CUTS = np.cumsum([0, QL, KVL, ROPE, MW, MW, KVW, KVW, KVW, 3 * H, MW]).tolist()
BLK = [(CUTS[0], CUTS[3] - CUTS[0]), (CUTS[4], MW), (CUTS[5], 2 * KVW), (CUTS[3], MW),
       (CUTS[7], KVW + 3 * H), (CUTS[9], MW)]
B_MLA, B_Q, B_CMPSEL, B_ZMLA, B_WINGATE, B_ZNSA = range(6)
IN_W = CUTS[-1]

C_PARTS = [("ident", P), ("cosn", NT * 32), ("sinn", NT * 64), ("cosm", NT * 16), ("sinm", NT * 32),
           ("winzero", 4), ("zero", 512), ("tri", P), ("cmpmask", PT * CHP), ("newmask", NG * NS_TOK),
           ("imap", SEL_TILES), ("headsum", P), ("jidx", SEL_TILES), ("cmplast", PAST // CMP_S), ("eps", 2)]
C_AT = {}
C_W = 0
for _n, _w in C_PARTS:
    C_AT[_n] = (C_W, _w)
    C_W += _w


def rows(t):
    return P if t < PT else NS_TOK


def constants():
    c = np.zeros((P, C_W), np.float32)

    def put(name):
        a, w = C_AT[name]
        return c[:, a:a + w]

    put("ident")[:] = np.eye(P, dtype=np.float32)
    for t in range(NT):
        r = rows(t)
        pos = np.arange(r) + P * t if t < PT else PAST + np.arange(r) % DEC_T
        for d, cn, sn in ((HD, "cosn", "sinn"), (ROPE, "cosm", "sinm")):
            inv = (np.float32(1.0) / (np.float32(10000.0) ** (np.arange(0, d, 2, dtype=np.float32) / np.float32(d)))).astype(np.float32)
            ang = pos.astype(np.float32)[:, None] * inv[None, :]
            h = d // 2
            put(cn)[:r, t * h:(t + 1) * h] = np.cos(ang)
            put(sn)[:r, t * d:t * d + h] = -np.sin(ang)
            put(sn)[:r, t * d + h:(t + 1) * d] = np.sin(ang)
    p = np.arange(P)
    tok = (p // H) % DEC_T
    put("winzero")[:] = np.where(np.arange(4)[None, :] <= tok[:, None], NEG, 0.0)
    put("tri")[:] = np.where(p[None, :] > p[:, None], NEG, 0.0)
    for t in range(PT):
        n = np.arange(CHP)
        bad = (n[None, :] * CMP_S + CMP_B - 1 > (p + P * t)[:, None]) | (n[None, :] >= CHP - 1)
        put("cmpmask")[:, t * CHP:(t + 1) * CHP] = np.where(bad, NEG, 0.0)
    for g in range(NG):
        s = np.arange(NS_TOK)
        b = GB * g + p // RB
        ok = (s[None, :] // DEC_T == b[:, None]) & (s[None, :] % DEC_T <= tok[:, None])
        put("newmask")[:, g * NS_TOK:(g + 1) * NS_TOK] = np.where(ok, 0.0, NEG)
    i, j = np.arange(CH)[:, None], np.arange(SEL_TILES)[None, :]
    lo, hi = np.maximum(i * CMP_S, j * SELB), np.minimum(i * CMP_S + CMP_B, (j + 1) * SELB)
    put("imap")[:CH] = np.maximum(hi - lo, 0) / CMP_B
    put("headsum")[:] = (p[:, None] // HG == p[None, :] // HG)
    put("jidx")[:] = np.arange(SEL_TILES)[None, :]
    put("cmplast")[:, CH - 1] = NEG
    put("eps")[:] = (RMS_EPS, LN_EPS)
    return c


class Uses:

    def __init__(self, n, bank0, steps, count):
        self.n, self.bank0, self.base, at = n, bank0, {}, 0
        for step in steps:
            if count(*step):
                self.base[step] = at
                at += count(*step)

    def at(self, *step, j=0):
        return self.base[step] + j


def weave(a, b):
    out, done, total = [], [0.0, 0.0], [sum(w for _, w in x) for x in (a, b)]
    at = [0, 0]
    while at[0] < len(a) or at[1] < len(b):
        k = int(at[0] == len(a) or (at[1] < len(b) and done[1] / total[1] < done[0] / total[0]))
        steps, w = (a, b)[k][at[k]]
        out += steps
        done[k] += w
        at[k] += 1
    return out


KINDS = ("pcmp", "psel", "pwin", "pmla")
UNITS = ([(i, kind, h) for i in range(PT) for kind in KINDS[:3] for h in range(G if kind == "pcmp" else H)]
         + [(i, "pmla", h) for i in range(PT) for h in range(H)])
NU, N_NSA = len(UNITS), len(UNITS) - PT * H
BRANCHES = []
for _u in UNITS:
    if _u[:2] not in BRANCHES:
        BRANCHES.append(_u[:2])
T_LAG, V_LAG = 3, 5
ORDER = [ST] + list(range(PT))

ITEMS = [("mla", 0), ("mla", 1), ("sel", 0), ("win", 0), ("sel", 1), ("win", 1)]
PAGES_OF = {"mla": PAGES, "sel": PAGES, "win": WIN // PAGE}
BANKS_OF = {k: n // 4 for k, n in PAGES_OF.items()}
KEYS_T = {"mla": 4, "sel": 2, "win": 1}


def plan():
    posts = (B_MLA, B_Q, B_WINGATE)
    steps = [("x", 0), ("x", 1)]
    seq = [(b, t) for b in range(len(BLK)) for t in range(NT)]
    products = []
    for n, (b, t) in enumerate(seq):
        now = [("proj", b, t)]
        if b == 0 and t + 2 < NT:
            now.append(("x", t + 2))
        for lag in (2, 1):
            if n >= lag and seq[n - lag][0] in posts and lag == 1 + (seq[n - lag][0] == B_MLA):
                now.append(("post", *seq[n - lag]))
        products.append((now, BLK[b][1] / 512 * 3.4))
    first = 2 * NT + 1
    for now, _ in products[:first]:
        steps += now
    cmp = [([("pos",)], 1), ([("bias",)], 1)] + [([("chunks", 0, k, half)], 1) for k in range(2) for half in range(2)]
    for t in range(NT):
        def chunks(k, half):
            return ([("chunks", t + 1, k, half)], 1) if t + 1 < NT else ([], 1)

        cmp += [([("hid", t, 0)], 2), chunks(0, 0), ([("hid", t, 1)], 2), chunks(0, 1), ([("hexp", t)], .5),
                chunks(1, 0), ([("hsilu", t)], .5), chunks(1, 1), ([], 1), ([("cmpout", t)], 1)]
    steps += weave(products[first:], cmp + [([], 6)])

    s = [([("wuk", 0)], 1), ([("wuk", 1)], 1), ([("qup_s",)], 1.5), ([("keys", *ITEMS[0], 0)], 2),
         ([("qhead",)], 1), ([("keys", *ITEMS[0], 1)], 2), ([("qlat",)], 1.5)]

    def compressed(g):
        return [([(f"{k}", g)], 1) for k in ("cscore", "cexp", "cnorm", "cturn", "imp0", "imp1", "drop")]

    for n, x in enumerate(ITEMS):
        last = ITEMS[n - 1] if n else None
        nxt = ITEMS[n + 1] if n + 1 < len(ITEMS) else None
        body = [([("score", *x, 0)], 1)]
        if last:
            body.append(([("probs", *last)], 1))
        body.append(([("score", *x, 1)], 1))
        if last:
            body.append(([("pv", *last)], 2))
        body += [([("keys", *x, 2)], 1.5), ([("keys", *x, 3)], 1.5), ([("score", *x, 2)], 1), ([("new", *x)], .5),
                 ([("score", *x, 3)], 1), ([("min", *x)], 1.5)]
        body += [([("keys", *nxt, 0)] if nxt else [], 1.5), ([("exp", *x)], 1.5),
                 ([("keys", *nxt, 1)] if nxt else [], 1.5), ([("norm", *x)], 1.5)]
        if last and last[0] != "sel":
            body.insert(6, ([("oturn", "sel" if last[0] == "win" else "mla", last[1])], 1))
        c = {("mla", 1): (0, 0), ("win", 0): (4, 1)}.get(x)
        if c:
            a, g = c
            mixed = body[:a]
            for j, step in enumerate(body[a:]):
                mixed.append(step)
                if j < 7:
                    mixed.append(compressed(g)[j])
            body = mixed
        if x == ("sel", 0):
            body.insert(9, ([("omla",)], 1))
        s += body
    s += [([("probs", *ITEMS[-1])], 1.5), ([("pv", *ITEMS[-1])], 2.5), ([("oturn", "sel", NG - 1)], 1), ([("onsa",)], 1)]

    def slot(m):
        now = []
        if m < NU:
            now.append(("pscore", m))
        if T_LAG <= m < NU + T_LAG:
            now.append(("pturn", m - T_LAG))
        if V_LAG <= m < NU + V_LAG:
            now.append(("pvalue", m - V_LAG))
        n = m - V_LAG
        if 0 <= n < NU and (n + 1 == NU or UNITS[n + 1][:2] != UNITS[n][:2]):
            now.append(("branch", *UNITS[n][:2]))
        return now

    def cost(m):
        i, kind, _ = UNITS[min(m, NU - 1)]
        return 0.5 if kind == "pcmp" else 0.4 * (i + 1) + 0.2

    p = [(slot(m), cost(m)) for m in range(N_NSA)]
    for j in range(HG):
        p.insert(N_NSA // 2 + 4 * j, ([("kup", j)], .6))
    for t in range(PT):
        p.insert(N_NSA // 2 + 18 + 4 * t, ([("vup", t)], .6))
    p.insert(N_NSA, ([("qup", 0)], 1))
    p.append(([("qh", 0)], 1))
    steps += weave(s, p)

    for m in range(N_NSA, NU + V_LAG):
        steps += slot(m)
        k, h = divmod(m - N_NSA, H)
        if h == 1 and k + 1 < PT:
            steps.append(("qup", k + 1))
        if h == 4 and k + 1 < PT:
            steps.append(("qh", k + 1))
        for n, m0 in OUT_AT.items():
            for d, kind in ((0, "mix"), (1, "out"), (2, "root"), (3, "norm_y")):
                if m - N_NSA == m0 + d:
                    steps.append((kind, n))
    steps += [(kind, NT - 1) for kind in ("mix", "out", "root", "norm_y")]
    return steps


OUT_AT = {0: 12, 1: 18, 2: 24, 3: 30}


def s_uses(kind, *_):
    return {"bias": 1, "qup_s": 2, "qlat": 1, "omla": 1, "new": 1, "cscore": 1, "imp0": 1, "imp1": 1, "kup": 1,
            "vup": 1, "qup": 2, "pscore": 1, "out": 2}.get(kind, int(kind == "hid" and _[1] == 0))


def a_uses(kind, *a):
    return 1 if kind == "proj" else BANKS_OF[a[0]] if kind == "score" and a[2] == 0 else 0


def t_uses(kind, *a):
    if kind == "post":
        return 2 if a[0] == B_Q else 1
    if kind == "keys":
        return KEYS_T[a[0]]
    if kind == "probs":
        return PAGES_OF[a[0]] // 4 + 1
    return {"x": 2, "pos": 1, "wuk": 1, "chunks": 2, "qhead": 1, "cturn": 1, "oturn": 1, "onsa": 1, "qh": 2, "pturn": 1,
            "mix": 2}.get(kind, 0)


def o_uses(kind, *a):
    return int(kind == "cmpout" or (kind == "pv" and a[0] != "win"))


def v_uses(kind, *a):
    return int(kind == "pvalue" and UNITS[a[0]][2] == 0)


def build(nc, io):
    STEPS = plan()
    A = Uses(2, 0, STEPS, a_uses)
    S = Uses(2, 2, STEPS, s_uses)
    T = Uses(2, 4, STEPS, t_uses)
    O = Uses(1, 6, STEPS, o_uses)
    V = Uses(1, 7, STEPS, v_uses)
    SLOT = 2048
    SLOTS = 5
    R_AT, r_dmas = {}, []
    for kind, g in ITEMS[2:]:
        for b in range(GB if kind == "sel" else GB // 2):
            R_AT[(kind, g, b)] = len(r_dmas)
            r_dmas.append(PAGES if kind == "sel" else 2)

    def ring_landed(u):
        return 16 * sum(r_dmas[v] for v in range(u % SLOTS, u + 1, SLOTS))

    with ExitStack() as ctx:
        def sb(name, parts, cols, dt=F32):
            return ctx.enter_context(nc.sbuf_tensor(name, [parts, cols], dt))

        def sem(name):
            return ctx.enter_context(nc.semaphore(name))

        psum = ctx.enter_context(nc.psum_tensor("psum", [P, 8, 512], F32))

        def bank_of(pool, u):
            return psum[:, pool.bank0 + u % pool.n, :]

        const = sb("const", P, C_W)
        gains = sb("gains", P, QL + KVL)
        wuq = sb("wuq", P, 2 * H * QH)
        wuk = sb("wuk", P, H * NOPE)
        wuv = sb("wuv", P, H * HD)
        w2 = sb("w2", HD, 2 * HD)
        b1 = sb("b1", HD, 2)
        wring = sb("wring", P, 2 * 4096)
        row = sb("row", P, NT * ROW)
        zsil = sb("zsil", P, NT * 2 * MW)
        kv = sb("kv", P, NT * 3 * KVW)
        gate = sb("gate", P, NT * 3 * H)
        cqT = sb("cqT", P, 2 * NTOK)
        ckvT = sb("ckvT", P, NTOK)
        krT = sb("krT", QH, NTOK)
        selKT = sb("selKT", P, NTOK)
        winKT = sb("winKT", P, NTOK)
        qnT = sb("qnT", P, HG * NTOK)
        qrT = sb("qrT", P, HG * NTOK)
        small = sb("small", P, 256)
        rtmp = sb("rtmp", P, 2 * 512)
        ring = sb("ring", P, SLOTS * SLOT)
        mid = sb("mid", P, 4096)
        w1h = sb("w1h", P, 2048 + 1536)
        bufA = sb("bufA", P, 4896)
        comp = sb("comp", P, 2080)
        ptab = sb("ptab", 1, DEC_B * PAGES, I32)
        gdram = nc.dram_tensor("gate_rows", [3, DEC_B * RB], F32).ap()

        def C(name):
            a, w = C_AT[name]
            return const[:, a:a + w]

        ident = C("ident")
        wr = wring[:, :].rearrange("p (s c n) -> p s c n", s=2, c=KC)
        wo = ring[:, 0:4 * SLOT].rearrange("p (c n) -> p c n", c=KC)
        row3 = row[:, :].rearrange("p (t n) -> p t n", t=NT)
        zs = zsil[:, :].rearrange("p (t n) -> p t n", t=NT)
        kv3 = kv[:, :].rearrange("p (t n) -> p t n", t=NT)
        gate3 = gate[:, :].rearrange("p (t n) -> p t n", t=NT)
        cqT3 = cqT[:, :].rearrange("p (c t) -> p c t", c=2)
        qnT3 = qnT[:, :].rearrange("p (h t) -> p h t", h=HG)
        qrT3 = qrT[:, :].rearrange("p (h t) -> p h t", h=HG)
        wuq3 = wuq[:, :].rearrange("p (c n) -> p c n", c=2)

        class Carve:

            def __init__(self, buf):
                self.buf, self.at = buf, 0

            def __call__(self, n, parts=P):
                self.at += n
                assert self.at <= self.buf.shape[1]
                return self.buf[0:parts, self.at - n:self.at]

        take = Carve(bufA)
        xT = take(KC * NTOK).rearrange("p (c t) -> p c t", c=KC)
        take = Carve(mid)
        xin = take(2048).rearrange("p (s n) -> p s n", s=2)
        araw = take(3 * 416).rearrange("p (s n) -> p s n", s=3)
        peN = take(256, 16)
        peT = take(32).rearrange("p (k n) -> p k n", k=2)
        chT = mid[:, :].rearrange("p (k g c n) -> p k g c n", k=2, g=G, c=8)
        take = Carve(comp)
        qraw = take(1024).rearrange("p (s n) -> p s n", s=2)
        qrot = take(1024).rearrange("p (s n) -> p s n", s=2)
        take = Carve(comp)
        kcT = take(NTOK)
        vc = take(DEC_B * P, CH).rearrange("p (b n) -> p b n", b=DEC_B)
        vcbd = take(G * HG * HD).rearrange("p (g n) -> p g n", g=G)
        take = Carve(w1h)
        w1 = take(2048).rearrange("p (k c r e) -> p k c r e", k=2, c=8, r=2)
        hsh = take(512, HD).rearrange("p (k g n) -> p k g n", k=2, g=G)
        hid = take(512, HD).rearrange("p (k g n) -> p k g n", k=2, g=G)
        hez = take(512, HD).rearrange("p (k g n) -> p k g n", k=2, g=G)
        SR = DEC_B * RB
        take = Carve(bufA)
        qnbd, qrbd = take(SR), take(SR)
        qlatT = take(SR)
        qrope = take(SR)
        krp = mid[0:ROPE, 2048:4096].rearrange("p (s n) -> p s n", s=2)
        Ps = take(PAST + NS_TOK)
        olatT = take(SR)
        qm = take(H * QH)
        qhPc = take(H * NS_TOK)
        qhT, Pc = qhPc[0:NOPE, :], qhPc[:, 0:2 * CH]
        wukTo = take(H * P)
        wukT, orow = wukTo[0:NOPE, :], wukTo[:, 0:P]
        take = Carve(w1h)
        kt = take(2048).rearrange("p (s n) -> p s n", s=2)
        PTs = take(9 * P).rearrange("p (k n) -> p k n", k=9)
        oTs = take(HG * NS_TOK).rearrange("p (h t) -> p h t", h=HG)
        PcT = take(256, CH).rearrange("p (v n) -> p v n", v=2)
        take = Carve(wring)
        Pp = take(2048).rearrange("p (s n) -> p s n", s=4)
        PTp = take(2048).rearrange("p (s n) -> p s n", s=4)
        KT = take(4096, QH).rearrange("p (h n) -> p h n", h=H)
        QT = ring[0:QH, 4 * SLOT:].rearrange("p (s h n) -> p s h n", s=2, h=H)
        take = Carve(mid)
        padK = take(2 * G * SEQ).rearrange("p (b g n) -> p b g n", b=2, g=G)
        Vm = take(2048).rearrange("p (t n) -> p t n", t=PT)
        acc = bufA[:, 4896 - MW:4896]
        otmp = rtmp[:, 512:1024]
        take = Carve(bufA)
        yb = take(2 * D_MODEL).rearrange("p (s n) -> p s n", s=2)
        take = Carve(comp)
        mixT = take(2 * KC * P).rearrange("p (s c n) -> p s c n", s=2, c=KC)
        take = Carve(w1h)
        lng, lnb = take(D_MODEL), take(D_MODEL)
        take = Carve(small)
        ssq = take(2 * NT).rearrange("p (t n) -> p t n", t=NT)
        rstd = take(2 * NT).rearrange("p (t n) -> p t n", t=NT)
        nmin = take(4)
        lsum, rl = take(1), take(1)
        cmin, csum, crl = take(1), take(1), take(1)
        grow = take(6).rearrange("p (b g) -> p b g", b=3)
        impr, impm, dropb = take(SEL_TILES), take(SEL_TILES), take(SEL_TILES)
        selc = take(2)
        biasv = take(2, HD)
        nmp = take(4 * H).rearrange("p (s h) -> p s h", s=4)
        lp = take(4 * H).rearrange("p (s h) -> p s h", s=4)
        coef = take(H)
        bnst = take(12).rearrange("p (s n) -> p s n", s=2)
        bnag = take(4).rearrange("p (s n) -> p s n", s=2)
        lnr = take(2)

        for pool, name in ((A, "a"), (S, "s"), (T, "t"), (O, "o"), (V, "v")):
            pool.full = [sem(f"{name}_full{i}") for i in range(pool.n)]
            pool.free = [sem(f"{name}_free{i}") for i in range(pool.n)]

        def wait_full(eng, pool, u):
            eng.wait_ge(pool.full[u % pool.n], u // pool.n + 1)

        def wait_copied(eng, pool, u):
            eng.wait_ge(pool.free[u % pool.n], u // pool.n + 1)

        c_land = [sem(f"c_land{i}") for i in range(2)]
        m_land = [sem(f"m_land{i}") for i in range(DEC_B)]
        r_land = [sem(f"r_land{i}") for i in range(SLOTS)]
        sel_read = sem("sel_read")
        const_in, page_in, wsmall_in, pos_in, wo_in, ln_in = (
            sem(n) for n in ("const_in", "page_in", "wsmall_in", "pos_in", "wo_in", "ln_in"))
        x_in = [sem(f"x_in{i}") for i in range(2)]
        w_in = [sem(f"w_in{i}") for i in range(2)]
        y_in = [sem(f"y_in{i}") for i in range(2)]
        y_out = [sem(f"y_out{i}") for i in range(2)]
        cmp_out, rows_out, win_copy, grow_out, grow_in = (
            sem(n) for n in ("cmp_out", "rows_out", "win_copy", "grow_out", "grow_in"))
        roped = sem("roped")
        sqrt_done = sem("sqrt_done")
        normed = sem("normed")
        z_exp = sem("z_exp")
        gate_done = sem("gate_done")
        h_shift, h_exp, h_done = sem("h_shift"), sem("h_exp"), sem("h_done")
        q_roped = sem("q_roped")
        bd_ready = sem("bd_ready")
        pad_ready = sem("pad_ready")
        sp_min, sp_exp, sp_norm = sem("sp_min"), sem("sp_exp"), sem("sp_norm")
        cp_min, cp_exp, cp_norm = sem("cp_min"), sem("cp_exp"), sem("cp_norm")
        mixed = sem("mixed")
        key_rows = sem("key_rows")
        p_exp = sem("p_exp")
        y_var, y_sqrt, y_norm, y_done = sem("y_var"), sem("y_sqrt"), sem("y_norm"), sem("y_done")
        act_own, dve_own, pool_own = sem("act_own"), sem("dve_own"), sem("pool_own")

        def own(eng, s):
            count = [0]

            def f(ins):
                count[0] += 1
                ins.then_inc(s, 1)
                eng.wait_ge(s, count[0])
            return f

        def nchunks(t):
            return P if t < PT else CHP

        def chunks_out(copy, eng, t, k, j):
            n = nchunks(t)
            u = T.at("chunks", t, k, j // 2, j=j % 2)
            wait_full(eng, T, u)
            bank = bank_of(T, u)[:, 0:4 * n].rearrange("p (c z n) -> p c z n", c=2, z=2)
            for g in range(G):
                for z in range(2):
                    ins = copy(chT[z * HD:(z + 1) * HD, k, g, 2 * j:2 * j + 2, 0:n],
                               bank[g * HD:(g + 1) * HD, :, z, :])
            ins.then_inc(T.free[u % T.n], 1)

        def slot(u):
            k = SLOTS - 1 - u % SLOTS
            return ring[:, k * SLOT:(k + 1) * SLOT]

        def mla_pages(bb):
            w = PAGES * ROW
            at = SLOTS * SLOT - (bb + 1) * w
            return ring[:, at:at + w].rearrange("p (k n) -> p k n", k=PAGES)

        def x_of(t):
            return io["x_prompt"][0, t * P:(t + 1) * P] if t < PT else io["x_sample"].rearrange("b t d -> (b t) d")

        def y_of(t):
            return io["y_prompt"][0, t * P:(t + 1) * P] if t < PT else io["y_sample"].rearrange("b t d -> (b t) d")

        block = ctx.enter_context(nc.Block())

        @block.sync
        def _(sp):
            def load_x(t):
                if t >= 2:
                    wait_full(sp, T, T.at("x", t - 2, j=1))
                sp.dma_start(xin[0:rows(t), t % 2, :], x_of(t)).then_inc(x_in[t % 2], 16)

            def load_w(b):
                if b >= 2:
                    wait_full(sp, A, A.at("proj", b - 2, NT - 1))
                a, w = BLK[b]
                src = io["w_in"][0].rearrange("(c p) n -> p c n", p=P)[:, :, a:a + w]
                sp.dma_start(wr[:, b % 2, :, 0:w], src).then_inc(w_in[b % 2], 16)

            def page(b, k):
                return sp.value_load(ptab[0:1, b * PAGES + k:b * PAGES + k + 1], min_val=0,
                                     max_val=io["cache_mla"].shape[1] - 1)

            def load_chunks(t):
                dst = ring[:, t % 2 * 2 * SLOT:(t % 2 + 1) * 2 * SLOT]
                if t >= 2:
                    wait_full(sp, T, T.at("chunks", t - 2, 1, 1, j=1))
                if t == PT:
                    sp.wait_ge(cmp_out, 16 * NT)
                    sp.dma_start(dst[0:CHP, :], io["p_cmp"].rearrange(
                        "a b (c s) k g d -> (a b c) (s k g d)", s=CMP_S)).then_inc(c_land[t % 2], 16)
                    return
                cache = io["cache_cmp_kv"][0].rearrange("n (c s) k g d -> n c (s k g d)", s=CMP_S)
                for s in range(2):
                    for k in range(PAGES):
                        n = page(2 * t + s, k)
                        o = s * CH + k * (PAGE // CMP_S)
                        sp.dma_start(dst[o:o + PAGE // CMP_S, :],
                                     cache[bass.ds(n, 1)].rearrange("a c f -> (a c) f")).then_inc(c_land[t % 2], 16)

            def load_pages(dst, landed, b, cache):
                for k in range(PAGES):
                    n = page(b, k)
                    sp.dma_start(dst[:, k, :], cache[bass.ds(n, 1)].rearrange("a t f -> (a t) f")).then_inc(landed, 16)

            sp.dma_start(const[:, :], io["const"]).then_inc(const_in, 16)
            load_x(0)
            load_x(1)
            load_w(0)
            sp.dma_start(gains[:, 0:QL], io["q_norm_g"][0].partition_broadcast(P)).then_inc(wsmall_in, 16)
            sp.dma_start(gains[:, QL:], io["kv_norm_g"][0].partition_broadcast(P)).then_inc(wsmall_in, 16)
            load_x(2)
            sp.dma_start(wuk[:, :], io["w_uk"][0]).then_inc(wsmall_in, 16)
            sp.dma_start(wuv[:, :], io["w_uv"][0]).then_inc(wsmall_in, 16)
            sp.dma_start(wuq3, io["w_uq"][0].rearrange("(c p) n -> p c n", p=P)).then_inc(wsmall_in, 16)
            load_w(1)
            load_x(3)
            for k in range(2):
                for r in range(2):
                    sp.dma_start(w1[:, k, :, r, :],
                                 io["cmp_w1"][0, k, r * CMP_S:(r + 1) * CMP_S].rearrange(
                                     "(c q) d e -> (q d) c e", q=2)).then_inc(wsmall_in, 16)
            sp.dma_start(w2[:, :].rearrange("p (k n) -> p k n", k=2),
                         io["cmp_w2"][0].rearrange("k e d -> e k d")).then_inc(wsmall_in, 16)
            with nc.allow_non_contiguous_dma(reason="128 values"):
                sp.dma_start(b1[:, :], io["cmp_b1"][0].rearrange("k e -> e k")).then_inc(wsmall_in, 16)
            for k in range(2):
                sp.dma_start(peN[:, k * P:(k + 1) * P].rearrange("p (q d) -> p q d", q=2),
                             io["cmp_pos_emb"][0, :, k].rearrange("(n q) d -> n q d", q=2)).then_inc(pos_in, 16)
            sp.dma_start(ptab[:, :], io["page_table"].rearrange("b k -> (b k)").unsqueeze(0)).then_inc(page_in, 16)
            load_x(4)
            load_w(2)
            sp.wait_ge(page_in, 16)
            load_chunks(0)
            load_w(3)
            load_chunks(1)
            load_chunks(2)
            for t in range(NT):
                wait_copied(sp, A, A.at("proj", B_CMPSEL, t))
                dst = (io["p_cmp"][0, 0, t * P:(t + 1) * P] if t < PT
                       else io["s_cmp"][0].rearrange("b t k g d -> (b t) k g d"))
                sp.dma_start(dst.rearrange("t k g d -> t (k g d)"), kv3[0:rows(t), t, 0:KVW]).then_inc(cmp_out, 16)
            load_w(4)
            load_chunks(3)
            load_w(5)
            load_pages(mla_pages(0), m_land[0], 0, io["cache_mla"][0])
            load_chunks(4)
            sp.dma_start(io["s_win"][0, :, 0:WIN - DEC_T].rearrange("b t k g d -> b (t k g d)"),
                         io["state_win_kv"][0, :, DEC_T:].rearrange("b t k g d -> b (t k g d)")).then_inc(win_copy, 16)
            for t in range(NT):
                sp.wait_ge(normed, t + 1)
                sp.wait_ge(roped, t + 1)
                dst = io["p_mla"][0, 0, t * P:(t + 1) * P] if t < PT else io["s_mla"][0].rearrange("b t f -> (b t) f")
                sp.dma_start(dst, row3[0:rows(t), t, :]).then_inc(rows_out, 16)
            sp.wait_ge(gate_done, NT)
            with nc.allow_non_contiguous_dma(reason="768 values"):
                sp.dma_start(gdram.rearrange("b (t h) -> t b h", h=H),
                             gate3[0:NS_TOK, ST, :].rearrange("p (b h) -> p b h", b=3)).then_inc(grow_out, 16)
                sp.wait_ge(grow_out, 16)
                sp.dma_start(grow, gdram.rearrange("b (g p) -> p b g", p=P)).then_inc(grow_in, 16)
            wait_full(sp, T, T.at("chunks", PT - 1, 1, 1, j=1))
            for b in range(1, DEC_B):
                if b == GB:
                    wait_full(sp, T, T.at("chunks", PT, 1, 1, j=1))
                load_pages(mla_pages(b), m_land[b], b, io["cache_mla"][0])
            for t in range(NT):
                sp.wait_ge(roped, 3 * NT + t + 1)
                r = rows(t)
                dst = (io["p_sel"][0, 0, t * P:(t + 1) * P] if t < PT
                       else io["s_sel"][0].rearrange("b t k g d -> (b t) k g d"))
                sp.dma_start(dst.rearrange("t k g d -> t (k g d)"), kv3[0:r, t, KVW:2 * KVW]).then_inc(rows_out, 16)
                if t < PT:
                    sp.dma_start(io["p_win"][0, 0, t * P:(t + 1) * P].rearrange("t k g d -> t (k g d)"),
                                 kv3[0:r, t, 2 * KVW:]).then_inc(rows_out, 16)
                else:
                    for b in range(DEC_B):
                        sp.dma_start(io["s_win"][0, b, WIN - DEC_T:].rearrange("t k g d -> t (k g d)"),
                                     kv3[b * DEC_T:(b + 1) * DEC_T, t, 2 * KVW:]).then_inc(rows_out, 16)
            for (kind, g, b), u in R_AT.items():
                if u < 2:
                    wait_full(sp, O, O.at("pv", "mla", 0))
                elif u < SLOTS:
                    wait_full(sp, O, O.at("pv", "mla", 1))
                else:
                    last = list(R_AT)[u - SLOTS]
                    if last[0] == "sel":
                        sp.wait_ge(sel_read, last[1] * GB + last[2] + 1)
                    else:
                        wait_full(sp, O, O.at("pv", "sel", last[1]))
                if kind == "sel":
                    load_pages(slot(u).rearrange("p (k n) -> p k n", k=PAGES), r_land[u % SLOTS], g * GB + b,
                               io["cache_sel_kv"][0].rearrange("n t k g d -> n t (k g d)"))
                else:
                    dst = slot(u).rearrange("p (b k n) -> p b k n", b=2, n=KVW)
                    for c in range(2):
                        src = io["state_win_kv"][0, g * GB + 2 * b + c].rearrange("(k p) z g d -> p k (z g d)", p=P)
                        sp.dma_start(dst[:, c], src).then_inc(r_land[u % SLOTS], 16)
            wait_full(sp, A, A.at("score", *ITEMS[-1], 0))
            sp.dma_start(lng, io["ln_g"][0].partition_broadcast(P)).then_inc(ln_in, 16)
            sp.dma_start(lnb, io["ln_b"][0].partition_broadcast(P)).then_inc(ln_in, 16)
            wait_full(sp, O, O.at("pv", "sel", NG - 1))
            sp.dma_start(wo, io["w_o"][0].rearrange("(c p) n -> p c n", p=P)).then_inc(wo_in, 16)
            wait_full(sp, T, T.at("onsa"))

            def store_y(n):
                sp.wait_ge(y_done, n + 1)
                sp.dma_start(y_of(ORDER[n]), yb[0:rows(ORDER[n]), n % 2, :]).then_inc(y_out[n % 2], 16)

            for n, t in enumerate(ORDER):
                if n >= 2:
                    sp.wait_ge(y_out[n % 2], 16 * (n // 2))
                sp.dma_start(yb[0:rows(t), n % 2, :], x_of(t)).then_inc(y_in[n % 2], 16)
                if n >= 1:
                    store_y(n - 1)
            store_y(NT - 1)
            sp.wait_ge(y_out[0], 16 * ((NT + 1) // 2))
            sp.wait_ge(y_out[1], 16 * (NT // 2))
            sp.wait_ge(win_copy, 16)
            sp.wait_ge(rows_out, 16 * (NT + 2 * PT + 1 + DEC_B))

        @block.tensor
        def _(pe):
            def claim(pool, u):
                if u >= pool.n:
                    pe.wait_ge(pool.free[u % pool.n], u // pool.n)
                return bank_of(pool, u)

            def turn(out, in_):
                return pe.transpose(out, in_, ident[0:in_.shape[0], 0:in_.shape[0]])

            def turn_x(t):
                pe.wait_ge(x_in[t % 2], 16 * (t // 2 + 1))
                r = rows(t)
                for j in range(2):
                    u = T.at("x", t, j=j)
                    bank = claim(T, u)
                    for c in range(4):
                        k = 4 * j + c
                        ins = turn(bank[:, c * r:(c + 1) * r], xin[0:r, t % 2, k * P:(k + 1) * P])
                    ins.then_inc(T.full[u % T.n], 1)

            def project(b, t):
                if t == 0:
                    pe.wait_ge(w_in[b % 2], 16 * (b // 2 + 1))
                if b == 0:
                    for j in range(2):
                        wait_copied(pe, T, T.at("x", t, j=j))
                w = BLK[b][1]
                u = A.at("proj", b, t)
                bank = claim(A, u)
                for c in range(KC):
                    ins = pe.matmul(bank[0:rows(t), 0:w], xT[:, c, t * P:t * P + rows(t)], wr[:, b % 2, c, 0:w],
                                    start=(c == 0), stop=(c == KC - 1))
                ins.then_inc(A.full[u % A.n], 1)

            def post(b, t):
                r = rows(t)
                if b == B_MLA:
                    pe.wait_ge(normed, t + 1)
                    pe.wait_ge(roped, t + 1)
                    u = T.at("post", b, t)
                    bank = claim(T, u)
                    for c in range(2):
                        turn(bank[:, c * r:(c + 1) * r], araw[0:r, t % 3, c * P:(c + 1) * P])
                    turn(bank[:, 2 * r:3 * r], row3[0:r, t, 0:KVL])
                    turn(bank[0:QH, 3 * r:4 * r], row3[0:r, t, ROW - QH:ROW]).then_inc(T.full[u % T.n], 1)
                elif b == B_Q:
                    for v, src in enumerate((qraw, qrot)):
                        if v == 0:
                            wait_copied(pe, A, A.at("proj", b, t))
                        else:
                            pe.wait_ge(roped, NT + t + 1)
                        u = T.at("post", b, t, j=v)
                        bank = claim(T, u)
                        for hh in range(HG):
                            ins = turn(bank[:, hh * r:(hh + 1) * r], src[0:r, t % 2, hh * P:(hh + 1) * P])
                        ins.then_inc(T.full[u % T.n], 1)
                else:
                    pe.wait_ge(roped, 3 * NT + t + 1)
                    u = T.at("post", b, t)
                    bank = claim(T, u)
                    turn(bank[:, 0:r], kv3[0:r, t, KVW:KVW + G * HD])
                    turn(bank[:, r:2 * r], kv3[0:r, t, 2 * KVW:2 * KVW + G * HD]).then_inc(T.full[u % T.n], 1)

            def turn_chunks(t, k, half):
                n = nchunks(t)
                if k == 0 and half == 0:
                    pe.wait_ge(c_land[t % 2], 16 * (2 * PAGES * (t // 2) + (2 * PAGES if t < PT else 1)))
                src = ring[0:n, t % 2 * 2 * SLOT:(t % 2 + 1) * 2 * SLOT].rearrange("p (s k f) -> p s k f", k=2, f=G * HD)
                for j in (2 * half, 2 * half + 1):
                    u = T.at("chunks", t, k, half, j=j % 2)
                    bank = claim(T, u)
                    for c in range(4):
                        ins = turn(bank[:, c * n:(c + 1) * n], src[:, 4 * j + c, k, :])
                    ins.then_inc(T.full[u % T.n], 1)

            def hidden(t, k):
                n = nchunks(t)
                u = S.at("hid", t, 0)
                bank = claim(S, u) if k == 0 else bank_of(S, u)
                for j in range(4):
                    wait_copied(pe, T, T.at("chunks", t, k, j // 2, j=j % 2))
                for g in range(G):
                    q = (k * G + g) * P
                    for c in range(8):
                        ins = pe.matmul(bank[:, q:q + n], w1[:, k, c, :, :].rearrange("p r e -> p (r e)"),
                                        chT[:, k, g, c, 0:n], start=(c == 0), stop=(c == 7))
                if k == 1:
                    ins.then_inc(S.full[u % S.n], 1)

            def compress_out(t):
                pe.wait_ge(h_done, t + 1)
                n, u = nchunks(t), O.at("cmpout", t)
                bank = claim(O, u)
                wk, wv = w2[:, 0:HD], w2[:, HD:2 * HD]
                for g in range(G):
                    pe.matmul(bank[g * HD:(g + 1) * HD, 0:n], wk, hid[:, 0, g, 0:n], start=True, stop=True)
                for g in range(G):
                    if t < PT:
                        for s in range(2):
                            o = P + (s * G + g) * HD
                            ins = pe.matmul(bank[0:CH, o:o + HD], hid[:, 1, g, s * CH:(s + 1) * CH], wv,
                                            start=True, stop=True)
                    else:
                        for hh in range(HG):
                            ins = pe.matmul(bank[hh * CHP:(hh + 1) * CHP, P + g * HD:P + (g + 1) * HD],
                                            hid[:, 1, g, 0:CHP], wv, start=True, stop=True)
                ins.then_inc(O.full[u % O.n], 1)

            def query_up(first, q, r, half):
                u = first + half
                bank = claim(S, u)
                for c in range(2):
                    ins = pe.matmul(bank[0:r, 0:4 * QH], cqT3[:, c, q:q + r],
                                    wuq3[:, c, half * 4 * QH:(half + 1) * 4 * QH], start=(c == 0), stop=(c == 1))
                ins.then_inc(S.full[u % S.n], 1)

            def source(kind, g, b):
                if kind == "mla":
                    return mla_pages(g * GB + b)
                if kind == "sel":
                    return slot(R_AT[(kind, g, b)]).rearrange("p (k n) -> p k n", k=PAGES)
                return slot(R_AT[(kind, g, b // 2)]).rearrange("p (b k n) -> p b k n", b=2, k=4)[:, b % 2]

            def turn_keys(kind, g, b):
                if kind == "mla":
                    pe.wait_ge(m_land[g * GB + b], 16 * PAGES)
                else:
                    u = R_AT[(kind, g, b if kind == "sel" else b // 2)]
                    pe.wait_ge(r_land[u % SLOTS], ring_landed(u))
                src = source(kind, g, b)
                for j in range(KEYS_T[kind]):
                    u = T.at("keys", kind, g, b, j=j)
                    bank = claim(T, u)
                    for k in range(4):
                        page = src[:, 4 * (j % 2) + k, :]
                        out = bank[:, k * P:(k + 1) * P]
                        if kind != "mla":
                            ins = turn(out, page[:, 0:G * HD])
                        elif j < 2:
                            ins = turn(out, page[:, 0:KVL])
                        else:
                            ins = turn(out[0:ROPE], page[:, KVL:ROW])
                    ins.then_inc(T.full[u % T.n], 1)

            def score(kind, g, b):
                rc = slice(g * P + b * RB, g * P + (b + 1) * RB)
                u0 = A.at("score", kind, g, 0)
                for j in range(KEYS_T[kind]):
                    wait_copied(pe, T, T.at("keys", kind, g, b, j=j))
                for j in range(BANKS_OF[kind]):
                    u = u0 + j
                    out = (claim(A, u) if b == 0 else bank_of(A, u))[b * RB:(b + 1) * RB, :]
                    keys = slice(j * 512, (j + 1) * 512)
                    if kind == "mla":
                        pe.matmul(out, qlatT[:, rc], kt[:, b % 2, keys], start=True, stop=False)
                        ins = pe.matmul(out, qrope[0:ROPE, rc], krp[:, b % 2, keys], start=False, stop=True)
                    else:
                        ins = pe.matmul(out, qrbd[:, rc], kt[:, b % 2, keys], start=True, stop=True)
                    if b == GB - 1:
                        ins.then_inc(A.full[u % A.n], 1)

            def score_new(kind, g):
                u = S.at("new", kind, g)
                cols, new = slice(g * P, (g + 1) * P), slice(SEQ, NTOK)
                out = claim(S, u)[:, 0:NS_TOK]
                if kind == "mla":
                    pe.matmul(out, qlatT[:, cols], ckvT[:, new], start=True, stop=False)
                    ins = pe.matmul(out, qrope[NOPE:QH, cols], krT[NOPE:QH, new], start=False, stop=True)
                else:
                    kT = selKT if kind == "sel" else winKT
                    ins = pe.matmul(out, qrbd[:, cols], kT[:, new], start=True, stop=True)
                ins.then_inc(S.full[u % S.n], 1)

            def turn_probs(kind, g):
                tiles = PAGES_OF[kind] + 1
                pe.wait_ge(sp_norm, ITEMS.index((kind, g)) + 1)
                for j in range(0, tiles, 4):
                    u = T.at("probs", kind, g, j=j // 4)
                    bank = claim(T, u)
                    for k in range(j, min(j + 4, tiles)):
                        w = P if k < tiles - 1 else NS_TOK
                        ins = turn(bank[0:w, (k - j) * P:(k - j + 1) * P], Ps[:, k * P:k * P + w])
                    ins.then_inc(T.full[u % T.n], 1)

            def weigh(kind, g):
                pages = PAGES_OF[kind]
                for j in range(pages // 4 + 1):
                    wait_copied(pe, T, T.at("probs", kind, g, j=j))
                u = O.at("pv", "sel" if kind == "win" else kind, g)
                out = bank_of(O, u) if kind == "win" else claim(O, u)
                if kind == "mla":
                    new, v = row3[0:NS_TOK, ST, 0:KVL], slice(0, KVL)
                else:
                    col = KVW if kind == "sel" else 2 * KVW
                    new, v = kv3[0:NS_TOK, ST, col + G * HD:col + KVW], slice(G * HD, KVW)
                pe.matmul(out[:, 0:P], PTs[0:NS_TOK, pages, :], new, start=(kind != "win"), stop=False)
                if kind == "sel":
                    for b in range(GB):
                        pe.matmul(out[b * RB:(b + 1) * RB, 0:P], PcT[:, 1, b * RB:(b + 1) * RB],
                                  vc[:, g * GB + b, :], start=False, stop=False)
                for k in range(pages):
                    for b in range(GB):
                        last = k == pages - 1
                        ins = pe.matmul(out[b * RB:(b + 1) * RB, 0:P], PTs[:, k, b * RB:(b + 1) * RB],
                                        source(kind, g, b)[:, k, v], start=False, stop=last and kind != "sel")
                        if last and kind == "sel":
                            ins.then_inc(sel_read, 1)
                if kind != "sel":
                    ins.then_inc(O.full[u % O.n], 1)

            def scores(n):
                i, kind, h = UNITS[n]
                u = S.at("pscore", n)
                bank = claim(S, u)
                q, keys = slice(i * P, (i + 1) * P), (i + 1) * P
                if kind == "pcmp":
                    if h == 0 and i == 0:
                        wait_copied(pe, O, O.at("cmpout", NT - 1))
                    for hh in range(HG):
                        ins = pe.matmul(bank[:, hh * CHP:(hh + 1) * CHP], qnT3[h * HD:(h + 1) * HD, hh, q],
                                        kcT[h * HD:(h + 1) * HD, SEQ:NTOK], start=True, stop=True)
                elif kind == "pmla":
                    if h == 0:
                        for j in range(2):
                            wait_copied(pe, T, T.at("qh", i, j=j))
                    if h == 0 and i == 0:
                        for j in range(HG):
                            wait_copied(pe, S, S.at("kup", j))
                        pe.wait_ge(key_rows, 1)
                    ins = pe.matmul(bank[:, 0:keys], QT[:, i % 2, h, :], KT[:, h, 0:keys], start=True, stop=True)
                else:
                    if h == 0 and i == 0:
                        pe.wait_ge(pad_ready, 1)
                    g, hh = h // HG, h % HG
                    ins = pe.matmul(bank[:, 0:keys], qrT3[:, hh, q], padK[:, int(kind == "pwin"), g, 0:keys],
                                    start=True, stop=True)
                ins.then_inc(S.full[u % S.n], 1)

            def turn_p(n):
                i, kind, h = UNITS[n]
                u = T.at("pturn", n)
                pe.wait_ge(p_exp, n + 1)
                bank = claim(T, u)
                for j in range(1 if kind == "pcmp" else i + 1):
                    ins = turn(bank[:, j * P:(j + 1) * P], Pp[:, n % 4, j * P:(j + 1) * P])
                ins.then_inc(T.full[u % T.n], 1)

            def values(n):
                i, kind, h = UNITS[n]
                first = n - h
                u = V.at("pvalue", first)
                bank = claim(V, u) if h == 0 else bank_of(V, u)
                wait_copied(pe, T, T.at("pturn", n))
                if kind == "pcmp":
                    ins = pe.matmul(bank[:, h * 256:(h + 1) * 256], PTp[:, n % 4, 0:P], vcbd[:, h, :],
                                    start=True, stop=True)
                else:
                    if kind == "pmla" and h == 0 and i == 0:
                        for t in range(PT):
                            wait_copied(pe, S, S.at("vup", t))
                    for j in range(i + 1):
                        if kind == "pmla":
                            v = Vm[:, j, h * HD:(h + 1) * HD]
                        else:
                            o = (KVW if kind == "psel" else 2 * KVW) + G * HD + (h // HG) * HD
                            v = kv3[:, j, o:o + HD]
                        ins = pe.matmul(bank[:, h * HD:(h + 1) * HD], PTp[:, n % 4, j * P:(j + 1) * P], v,
                                        start=(j == 0), stop=(j == i))
                if n + 1 == NU or UNITS[n + 1][:2] != (i, kind):
                    ins.then_inc(V.full[u % V.n], 1)

            pe.wait_ge(const_in, 16)
            for step in STEPS:
                kind, a = step[0], step[1:]
                if kind == "x":
                    turn_x(*a)
                elif kind == "proj":
                    project(*a)
                elif kind == "post":
                    post(*a)
                elif kind == "pos":
                    pe.wait_ge(pos_in, 32)
                    u = T.at("pos")
                    bank = claim(T, u)
                    for k in range(2):
                        ins = turn(bank[:, 16 * k:16 * k + 16], peN[:, k * P:(k + 1) * P])
                    ins.then_inc(T.full[u % T.n], 1)
                elif kind == "bias":
                    pe.wait_ge(wsmall_in, 16 * 11)
                    wait_copied(pe, T, T.at("pos"))
                    u = S.at("bias")
                    bank = claim(S, u)
                    for k in range(2):
                        for r in range(2):
                            for c in range(8):
                                ins = pe.matmul(bank[0:HD, k:k + 1], w1[:, k, c, r, :],
                                                peT[:, k, 8 * r + c:8 * r + c + 1],
                                                start=(r == 0 and c == 0), stop=(r == 1 and c == 7))
                    ins.then_inc(S.full[u % S.n], 1)
                elif kind == "chunks":
                    turn_chunks(*a)
                elif kind == "hid":
                    hidden(*a)
                elif kind == "cmpout":
                    compress_out(*a)
                elif kind == "wuk":
                    u = T.at(*step)
                    bank = claim(T, u)
                    for c in range(4):
                        h = 4 * a[0] + c
                        ins = turn(bank[0:NOPE, c * P:(c + 1) * P], wuk[:, h * NOPE:(h + 1) * NOPE])
                    ins.then_inc(T.full[u % T.n], 1)
                elif kind == "qup_s":
                    for half in range(2):
                        query_up(S.at("qup_s"), SEQ, NS_TOK, half)
                elif kind == "qhead":
                    pe.wait_ge(q_roped, 1)
                    u = T.at("qhead")
                    bank = claim(T, u)
                    for h in range(H):
                        ins = turn(bank[0:QH, h * NS_TOK:(h + 1) * NS_TOK], qm[0:NS_TOK, h * QH:(h + 1) * QH])
                    ins.then_inc(T.full[u % T.n], 1)
                elif kind == "qlat":
                    for j in range(2):
                        wait_copied(pe, T, T.at("wuk", j))
                    wait_copied(pe, T, T.at("qhead"))
                    u = S.at("qlat")
                    bank = claim(S, u)
                    for h in range(H):
                        ins = pe.matmul(bank[:, h * NS_TOK:(h + 1) * NS_TOK], wukT[:, h * P:(h + 1) * P],
                                        qhT[:, h * NS_TOK:(h + 1) * NS_TOK], start=True, stop=True)
                    ins.then_inc(S.full[u % S.n], 1)
                elif kind == "keys":
                    turn_keys(*a)
                elif kind == "score":
                    if step == ("score", "mla", 0, 0):
                        wait_copied(pe, S, S.at("qlat"))
                    if step == ("score", "sel", 0, 0):
                        pe.wait_ge(bd_ready, 1)
                    score(*a)
                elif kind == "new":
                    score_new(*a)
                elif kind == "probs":
                    turn_probs(*a)
                elif kind == "pv":
                    weigh(*a)
                elif kind == "oturn":
                    wait_copied(pe, O, O.at("pv", *a))
                    u = T.at(*step)
                    turn(claim(T, u)[:, 0:P], orow).then_inc(T.full[u % T.n], 1)
                elif kind == "omla":
                    wait_copied(pe, T, T.at("oturn", "mla", NG - 1))
                    u = S.at("omla")
                    bank = claim(S, u)
                    oh = olatT.rearrange("p (t h) -> p t h", h=H)
                    for h in range(H):
                        ins = pe.matmul(bank[0:NS_TOK, h * HD:(h + 1) * HD], oh[:, :, h], wuv[:, h * HD:(h + 1) * HD],
                                        start=True, stop=True)
                    ins.then_inc(S.full[u % S.n], 1)
                elif kind == "cscore":
                    if a[0] == 0:
                        pe.wait_ge(bd_ready, 1)
                    u = S.at(*step)
                    bank = claim(S, u)
                    for b in range(GB):
                        bb = a[0] * GB + b
                        ins = pe.matmul(bank[b * RB:(b + 1) * RB, 0:CH], qnbd[:, bb * RB:(bb + 1) * RB],
                                        kcT[:, bb * CH:(bb + 1) * CH], start=True, stop=True)
                    ins.then_inc(S.full[u % S.n], 1)
                elif kind == "cturn":
                    pe.wait_ge(cp_norm, a[0] + 1)
                    u = T.at(*step)
                    bank = claim(T, u)
                    turn(bank[0:CH, 0:P], Pc[:, 0:CH])
                    turn(bank[0:CH, P:2 * P], Pc[:, CH:2 * CH]).then_inc(T.full[u % T.n], 1)
                elif kind == "imp0":
                    wait_copied(pe, T, T.at("cturn", a[0]))
                    u = S.at(*step)
                    pe.matmul(claim(S, u)[:, 0:SEL_TILES], PcT[:, 0, :], C("imap")[0:CH, :], start=True,
                              stop=True).then_inc(S.full[u % S.n], 1)
                elif kind == "imp1":
                    wait_copied(pe, S, S.at("imp0", a[0]))
                    u = S.at(*step)
                    pe.matmul(claim(S, u)[:, 0:SEL_TILES], C("headsum"), impr, start=True,
                              stop=True).then_inc(S.full[u % S.n], 1)
                elif kind == "onsa":
                    wait_copied(pe, T, T.at("oturn", "sel", NG - 1))
                    u = T.at("onsa")
                    bank = claim(T, u)
                    for hh in range(HG):
                        ins = turn(bank[0:NS_TOK, hh * P:(hh + 1) * P], oTs[:, hh, :])
                    ins.then_inc(T.full[u % T.n], 1)
                elif kind == "kup":
                    j = a[0]
                    u = S.at(*step)
                    pe.matmul(claim(S, u), wuk[:, j * P:(j + 1) * P], ckvT[:, 0:SEQ], start=True,
                              stop=True).then_inc(S.full[u % S.n], 1)
                elif kind == "vup":
                    t = a[0]
                    u = S.at(*step)
                    pe.matmul(claim(S, u), ckvT[:, t * P:(t + 1) * P], wuv[:, :], start=True,
                              stop=True).then_inc(S.full[u % S.n], 1)
                elif kind == "qup":
                    for half in range(2):
                        query_up(S.at(*step), a[0] * P, P, half)
                elif kind == "qh":
                    pe.wait_ge(q_roped, a[0] + 2)
                    for half in range(2):
                        u = T.at(*step, j=half)
                        bank = claim(T, u)
                        for c in range(4):
                            h = 4 * half + c
                            ins = turn(bank[0:QH, c * P:(c + 1) * P], qm[:, h * QH:(h + 1) * QH])
                        ins.then_inc(T.full[u % T.n], 1)
                elif kind == "pscore":
                    scores(*a)
                elif kind == "pturn":
                    turn_p(*a)
                elif kind == "pvalue":
                    values(*a)
                elif kind == "mix":
                    n, t = a[0], ORDER[a[0]]
                    r = rows(t)
                    if n == 0:
                        wait_copied(pe, S, S.at("omla"))
                        wait_copied(pe, T, T.at("onsa"))
                    else:
                        pe.wait_ge(mixed, PT + n)
                    for j in range(2):
                        u = T.at(*step, j=j)
                        bank = claim(T, u)
                        for c in range(4):
                            ins = turn(bank[:, c * r:(c + 1) * r], zs[0:r, t, (4 * j + c) * P:(4 * j + c + 1) * P])
                        ins.then_inc(T.full[u % T.n], 1)
                elif kind == "out":
                    n, r = a[0], rows(ORDER[a[0]])
                    if n == 0:
                        pe.wait_ge(wo_in, 16)
                    for j in range(2):
                        wait_copied(pe, T, T.at("mix", n, j=j))
                    for half in range(2):
                        u = S.at(*step, j=half)
                        bank = claim(S, u)
                        for c in range(KC):
                            ins = pe.matmul(bank[0:r, :], mixT[:, n % 2, c, 0:r], wo[:, c, half * 512:(half + 1) * 512],
                                            start=(c == 0), stop=(c == KC - 1))
                        ins.then_inc(S.full[u % S.n], 1)

        @block.scalar
        def _(act):
            ok = own(act, act_own)

            def arrive(pool, u):
                wait_full(act, pool, u)
                return bank_of(pool, u)

            def block_out(b, t):
                r, w = rows(t), BLK[b][1]
                u = A.at("proj", b, t)
                bank = arrive(A, u)
                free = A.free[u % A.n]
                if b == B_MLA:
                    if t >= 3:
                        wait_full(act, T, T.at("post", b, t - 3))
                    act.copy(araw[0:r, t % 3, :], bank[0:r, 0:w]).then_inc(free, 1)
                    wait_copied(act, A, u)
                    junk = zs[0:r, t, 0:QL]
                    ok(act.activation(junk, araw[0:r, t % 3, 0:QL], ACT.Square, accum_out=ssq[0:r, t, 0:1]))
                    ok(act.activation(junk[:, 0:KVL], araw[0:r, t % 3, QL:QL + KVL], ACT.Square,
                                      accum_out=ssq[0:r, t, 1:2]))
                    eps = C("eps")[0:r, 0:1]
                    act.activation(rstd[0:r, t, 0:1], ssq[0:r, t, 0:1], ACT.Sqrt, bias=eps, scale=1.0 / QL)
                    act.activation(rstd[0:r, t, 1:2], ssq[0:r, t, 1:2], ACT.Sqrt, bias=eps,
                                   scale=1.0 / KVL).then_inc(sqrt_done, 1)
                elif b in (B_ZMLA, B_ZNSA):
                    o = 0 if b == B_ZMLA else MW
                    act.activation(zs[0:r, t, o:o + MW], bank[0:r, :], ACT.Exp, scale=-1.0).then_inc(z_exp, 1)
                elif b == B_Q:
                    if t >= 2:
                        wait_full(act, T, T.at("post", b, t - 2, j=1))
                    act.copy(qraw[0:r, t % 2, :].rearrange("p (h g d) -> p h g d", h=HG, g=G),
                             bank[0:r, :].rearrange("p (g h d) -> p h g d", h=HG, g=G)).then_inc(free, 1)
                elif b == B_CMPSEL:
                    act.copy(kv3[0:r, t, 0:2 * KVW], bank[0:r, :]).then_inc(free, 1)
                else:
                    act.copy(kv3[0:r, t, 2 * KVW:3 * KVW], bank[0:r, 0:KVW])
                    act.activation(gate3[0:r, t, :], bank[0:r, KVW:w], ACT.Exp, scale=-1.0).then_inc(free, 1)

            def query_out(u, r, half):
                act.copy(qm[0:r, half * 4 * QH:(half + 1) * 4 * QH],
                         arrive(S, u)[0:r, 0:4 * QH]).then_inc(S.free[u % S.n], 1)

            def keys_out(kind, g, b):
                for j in (0, 2) if kind == "mla" else (0,):
                    u = T.at("keys", kind, g, b, j=j)
                    bank = arrive(T, u)
                    if j < 2:
                        ins = act.copy(kt[:, b % 2, 0:512], bank)
                    else:
                        ins = act.copy(krp[:, b % 2, 0:512], bank[0:ROPE, :])
                    ins.then_inc(T.free[u % T.n], 1)

            def probs_out(kind, g):
                tiles = PAGES_OF[kind] + 1
                for j in range(0, tiles, 8):
                    u = T.at("probs", kind, g, j=j // 4)
                    m = min(4, tiles - j)
                    bank = arrive(T, u)
                    r = NS_TOK if m == 1 else P
                    act.copy(PTs[0:r, j:j + m, :],
                             bank[0:r, 0:m * P].rearrange("p (k n) -> p k n", k=m)).then_inc(T.free[u % T.n], 1)

            def exp_unit(n):
                i, kind, h = UNITS[n]
                u, k = S.at("pscore", n), BRANCHES.index((i, kind)) % 4
                wait_copied(act, S, u)
                if kind == "pcmp":
                    for hh in range(HG):
                        c, s = h * HG + hh, slice(hh * CHP, (hh + 1) * CHP)
                        ins = act.activation(Pp[:, n % 4, s], Pp[:, n % 4, s], ACT.Exp, bias=nmp[:, k, c:c + 1],
                                             scale=-1.0, accum_out=lp[:, k, c:c + 1])
                else:
                    w = (i + 1) * P
                    ins = act.activation(Pp[:, n % 4, 0:w], Pp[:, n % 4, 0:w], ACT.Exp, bias=nmp[:, k, h:h + 1],
                                         scale=-1.0, accum_out=lp[:, k, h:h + 1])
                ins.then_inc(p_exp, 1)

            act.wait_ge(const_in, 16)
            for step in STEPS:
                kind, a = step[0], step[1:]
                if kind == "x":
                    u, r = T.at(*step, j=0), rows(a[0])
                    act.copy(xT[:, 0:4, a[0] * P:a[0] * P + r],
                             arrive(T, u)[:, 0:4 * r].rearrange("p (c n) -> p c n", c=4)).then_inc(T.free[u % T.n], 1)
                elif kind == "proj":
                    block_out(*a)
                elif kind == "chunks":
                    t, k, half = a
                    chunks_out(act.copy, act, t, k, 2 * half)
                elif kind == "hid" and a[1] == 1:
                    t, n = a[0], nchunks(a[0])
                    bh = arrive(S, S.at("hid", t, 0))[HD:P, :].rearrange("p (k g n) -> p k g n", k=2, g=G)
                    if t >= 1:
                        wait_copied(act, S, S.at("hid", t - 1, 0))
                    act.copy(hsh[:, :, :, 0:n - 1], bh[:, :, :, 1:n]).then_inc(h_shift, 1)
                elif kind == "hexp":
                    t, n = a[0], nchunks(a[0])
                    wait_copied(act, S, S.at("hid", t, 0))
                    act.activation(hez[:, :, :, 0:n], hid[:, :, :, 0:n], ACT.Exp, scale=-1.0).then_inc(h_exp, 1)
                elif kind == "qup_s":
                    for half in range(2):
                        query_out(S.at(*step) + half, NS_TOK, half)
                elif kind == "qlat":
                    u = S.at("qlat")
                    act.copy(qlatT.rearrange("p (t h) -> p h t", h=H),
                             arrive(S, u)[:, 0:SR].rearrange("p (h t) -> p h t", h=H)).then_inc(S.free[u % S.n], 1)
                elif kind == "keys":
                    keys_out(*a)
                elif kind == "exp":
                    w = PAGES_OF[a[0]] * P + NS_TOK
                    act.wait_ge(sp_min, ITEMS.index(a) + 1)
                    act.activation(Ps[:, 0:w], Ps[:, 0:w], ACT.Exp, bias=nmin[:, 3:4], scale=-1.0,
                                   accum_out=lsum).then_inc(sp_exp, 1)
                elif kind == "cexp":
                    act.wait_ge(cp_min, a[0] + 1)
                    act.activation(Pc[:, 0:CH], Pc[:, 0:CH], ACT.Exp, bias=cmin, scale=-1.0,
                                   accum_out=csum).then_inc(cp_exp, 1)
                elif kind == "probs":
                    probs_out(*a)
                elif kind == "pv" and a[0] == "mla":
                    u = O.at(*step)
                    act.copy(orow, arrive(O, u)[:, 0:P]).then_inc(O.free[u % O.n], 1)
                elif kind == "oturn" and a[0] == "mla":
                    u = T.at(*step)
                    act.copy(olatT[:, a[1] * P:(a[1] + 1) * P], arrive(T, u)[:, 0:P]).then_inc(T.free[u % T.n], 1)
                elif kind == "kup":
                    u, j = S.at(*step), a[0]
                    bank = arrive(S, u)
                    act.copy(KT[0:NOPE, 2 * j, :], bank[0:NOPE, :])
                    act.copy(KT[0:NOPE, 2 * j + 1, :], bank[NOPE:P, :]).then_inc(S.free[u % S.n], 1)
                elif kind == "qup":
                    for half in range(2):
                        query_out(S.at(*step) + half, P, half)
                elif kind == "qh":
                    u = T.at(*step, j=0)
                    act.copy(QT[:, a[0] % 2, 0:4, :],
                             arrive(T, u)[0:QH, :].rearrange("p (h n) -> p h n", h=4)).then_inc(T.free[u % T.n], 1)
                elif kind == "pscore":
                    exp_unit(*a)
                elif kind == "pturn" and a[0] % 2 == 0:
                    n = a[0]
                    u, w = T.at(*step), P if UNITS[n][1] == "pcmp" else (UNITS[n][0] + 1) * P
                    act.copy(PTp[:, n % 4, 0:w], arrive(T, u)[:, 0:w]).then_inc(T.free[u % T.n], 1)
                elif kind == "mix":
                    u, r = T.at(*step, j=0), rows(ORDER[a[0]])
                    act.copy(mixT[:, a[0] % 2, 0:4, 0:r],
                             arrive(T, u)[:, 0:4 * r].rearrange("p (c n) -> p c n", c=4)).then_inc(T.free[u % T.n], 1)
                elif kind == "root":
                    n, r = a[0], rows(ORDER[a[0]])
                    act.wait_ge(y_var, n + 1)
                    act.activation(lnr[0:r, n % 2:n % 2 + 1], bnag[0:r, n % 2, 1:2], ACT.Sqrt,
                                   bias=C("eps")[0:r, 1:2]).then_inc(y_sqrt, 1)

        @block.vector
        def _(dve):
            ok = own(dve, dve_own)

            def arrive(pool, u):
                wait_full(dve, pool, u)
                return bank_of(pool, u)

            def four(bank, n):
                return bank[:, 0:4 * n].rearrange("p (c n) -> p c n", c=4)

            def work_on(b, t):
                r = rows(t)
                u = A.at("proj", b, t)
                if b == B_MLA:
                    if t == 0:
                        dve.wait_ge(wsmall_in, 16 * 11)
                    dve.wait_ge(sqrt_done, t + 1)
                    ok(dve.reciprocal(rstd[0:r, t, :], rstd[0:r, t, :]))
                    a = araw[0:r, t % 3, :]
                    dve.scalar_tensor_tensor(out=row3[0:r, t, 0:KVL], in0=a[:, QL:QL + KVL], scalar=rstd[0:r, t, 1:2],
                                             in1=gains[0:r, QL:], op0=ALU.mult, op1=ALU.mult)
                    dve.scalar_tensor_tensor(out=a[:, 0:QL], in0=a[:, 0:QL], scalar=rstd[0:r, t, 0:1],
                                             in1=gains[0:r, 0:QL], op0=ALU.mult, op1=ALU.mult).then_inc(normed, 1)
                elif b in (B_ZMLA, B_ZNSA):
                    m, o = (t, 0) if b == B_ZMLA else (NT + t, MW)
                    dve.wait_ge(z_exp, m + 1)
                    z = zs[0:r, t, o:o + MW]
                    ok(dve.tensor_scalar(z, z, 1.0, None, ALU.add))
                    ok(dve.reciprocal(z, z))
                    dve.tensor_tensor(z, bank_of(A, u)[0:r, :], z, ALU.mult).then_inc(A.free[u % A.n], 1)
                elif b == B_WINGATE:
                    wait_copied(dve, A, u)
                    e = gate3[0:r, t, :]
                    ok(dve.tensor_scalar(e, e, 1.0, None, ALU.add))
                    dve.reciprocal(e, e).then_inc(gate_done, 1)

            def post_out(b, t):
                r, c0 = rows(t), t * P
                u = T.at("post", b, t)
                if b == B_MLA:
                    bank = arrive(T, u)
                    dve.tensor_copy(cqT3[:, :, c0:c0 + r], bank[:, 0:2 * r].rearrange("p (c n) -> p c n", c=2))
                    dve.tensor_copy(ckvT[:, c0:c0 + r], bank[:, 2 * r:3 * r])
                    dve.tensor_copy(krT[NOPE:QH, c0:c0 + r], bank[NOPE:QH, 3 * r:4 * r]).then_inc(T.free[u % T.n], 1)
                elif b == B_Q:
                    for v, dst in enumerate((qnT3, qrT3)):
                        dve.tensor_copy(dst[:, :, c0:c0 + r], four(arrive(T, u + v), r)).then_inc(
                            T.free[(u + v) % T.n], 1)
                else:
                    bank = arrive(T, u)
                    dve.tensor_copy(selKT[:, c0:c0 + r], bank[:, 0:r])
                    dve.tensor_copy(winKT[:, c0:c0 + r], bank[:, r:2 * r]).then_inc(T.free[u % T.n], 1)

            def compressed(t):
                u = O.at("cmpout", t)
                bank = arrive(O, u)
                if t < PT:
                    dve.tensor_copy(kcT[:, t * P:(t + 1) * P], bank[:, 0:P])
                    ins = dve.tensor_copy(vc[:, 2 * t:2 * t + 2, :],
                                          bank[0:CH, P:3 * P].rearrange("p (b n) -> p b n", b=2))
                else:
                    ok(dve.memset(vcbd, 0.0))
                    dve.tensor_copy(kcT[:, SEQ:NTOK], bank[:, 0:CHP])
                    for hh in range(HG):
                        s = slice(hh * CHP, (hh + 1) * CHP)
                        ins = dve.tensor_copy(vcbd[s, :, hh * HD:(hh + 1) * HD],
                                              bank[s, P:2 * P].rearrange("p (g d) -> p g d", g=G))
                ins.then_inc(O.free[u % O.n], 1)

            def hidden_sum(t):
                n, u = nchunks(t), S.at("hid", t, 0)
                bank = arrive(S, u)[0:HD, :].rearrange("p (k g n) -> p k g n", k=2, g=G)
                dve.wait_ge(h_shift, t + 1)
                if t >= 1:
                    wait_full(dve, O, O.at("cmpout", t - 1))
                dve.memset(hid[:, :, :, n - 1:n], 0.0)
                for k in range(2):
                    ins = dve.scalar_tensor_tensor(out=hid[:, k, :, 0:n - 1], in0=bank[:, k, :, 0:n - 1],
                                                   scalar=biasv[:, k:k + 1], in1=hsh[:, k, :, 0:n - 1],
                                                   op0=ALU.add, op1=ALU.add)
                ins.then_inc(S.free[u % S.n], 1)

            def hidden_silu(t):
                n = nchunks(t)
                dve.wait_ge(h_exp, t + 1)
                e, h = hez[:, :, :, 0:n], hid[:, :, :, 0:n]
                ok(dve.tensor_scalar(e, e, 1.0, None, ALU.add))
                ok(dve.reciprocal(e, e))
                dve.tensor_tensor(h, h, e, ALU.mult).then_inc(h_done, 1)

            def minimum(pool, u, out, src, mask, scale, least):
                dve.tensor_tensor_reduce(out, src, mask, -scale, CLAMP, ALU.add, ALU.min, least).then_inc(
                    pool.free[u % pool.n], 1)

            def newest(kind, g):
                u, at = S.at("new", kind, g), PAGES_OF[kind] * P
                minimum(S, u, Ps[:, at:at + NS_TOK], arrive(S, u)[:, 0:NS_TOK],
                        C("newmask")[:, g * NS_TOK:(g + 1) * NS_TOK], MLA_SCALE if kind == "mla" else NSA_SCALE,
                        nmin[:, 2:3])

            def minima(kind, g):
                n = BANKS_OF[kind]
                for j in range(n):
                    u = A.at("score", kind, g, 0) + j
                    out, src = Ps[:, j * 512:(j + 1) * 512], arrive(A, u)
                    scale = MLA_SCALE if kind == "mla" else NSA_SCALE
                    if kind == "mla":
                        mask = C("zero")
                    elif kind == "win":
                        a = C_AT["winzero"][0]
                        mask = const[:, a:a + WIN]
                    else:
                        out, src = (x.rearrange("p (a b) -> p a b", b=SELB) for x in (out, src))
                        mask = dropb[:, 8 * j:8 * j + 8].unsqueeze(2).broadcast_to([P, 8, SELB])
                    minimum(A, u, out, src, mask, scale, nmin[:, j:j + 1])
                for j in range(n):
                    wait_copied(dve, A, A.at("score", kind, g, 0) + j)
                wait_copied(dve, S, S.at("new", kind, g))
                first = 0 if n == 2 else 1
                if n == 1:
                    ok(dve.tensor_copy(nmin[:, 1:2], nmin[:, 0:1]))
                dve.tensor_reduce(nmin[:, 3:4], nmin[:, first:3], AX_X, ALU.min).then_inc(sp_min, 1)

            def normalise(kind, g):
                w = PAGES_OF[kind] * P + NS_TOK
                dve.wait_ge(sp_exp, ITEMS.index((kind, g)) + 1)
                ok(dve.reciprocal(rl, lsum))
                if kind == "mla":
                    ins = dve.tensor_scalar(Ps[:, 0:w], Ps[:, 0:w], rl, None, ALU.mult)
                else:
                    gates = grow[:, 1 if kind == "sel" else 2, g:g + 1]
                    ins = dve.tensor_scalar(Ps[:, 0:w], Ps[:, 0:w], rl, gates, ALU.mult, ALU.mult)
                ins.then_inc(sp_norm, 1)

            def keys_out(kind, g, b):
                for j in {"mla": (1, 3), "sel": (1,), "win": ()}[kind]:
                    u = T.at("keys", kind, g, b, j=j)
                    bank = arrive(T, u)
                    if j < 2:
                        ins = dve.tensor_copy(kt[:, b % 2, 512:], bank)
                    else:
                        ins = dve.tensor_copy(krp[:, b % 2, 512:], bank[0:ROPE, :])
                    ins.then_inc(T.free[u % T.n], 1)

            def probs_out(kind, g):
                tiles = PAGES_OF[kind] + 1
                for j in range(4, tiles, 8):
                    u = T.at("probs", kind, g, j=j // 4)
                    m = min(4, tiles - j)
                    bank = arrive(T, u)
                    r = NS_TOK if m == 1 else P
                    dve.tensor_copy(PTs[0:r, j:j + m, :],
                                    bank[0:r, 0:m * P].rearrange("p (k n) -> p k n", k=m)).then_inc(T.free[u % T.n], 1)

            def nsa_out(g):
                u = T.at("oturn", "sel", g)
                bank = arrive(T, u)
                for k in range(G):
                    s = slice(k * HD, (k + 1) * HD)
                    ins = dve.tensor_copy(
                        oTs[s, :, g * GB * DEC_T:(g + 1) * GB * DEC_T],
                        bank[s, 0:P].rearrange("p (t h) -> p h t", h=H)[:, k * HG:(k + 1) * HG, :])
                ins.then_inc(T.free[u % T.n], 1)

            def drop_block():
                mids = slice(1, SEL_TILES - 2)
                ok(dve.tensor_reduce(selc[:, 0:1], impm[:, mids], AX_X, ALU.min))
                ok(dve.scalar_tensor_tensor(out=impm[:, mids], in0=impm[:, mids], scalar=selc[:, 0:1],
                                            in1=C("jidx")[:, mids], op0=ALU.is_le, op1=ALU.mult))
                ok(dve.tensor_reduce(selc[:, 1:2], impm[:, mids], AX_X, ALU.max))
                ok(dve.tensor_scalar(dropb, C("jidx"), selc[:, 1:2], NEG, ALU.is_equal, ALU.mult))

            a_tri = C_AT["tri"][0]

            def min_unit(n):
                i, kind, h = UNITS[n]
                u, k = S.at("pscore", n), BRANCHES.index((i, kind)) % 4
                bank = arrive(S, u)
                if kind == "pcmp":
                    for hh in range(HG):
                        s = slice(hh * CHP, (hh + 1) * CHP)
                        c = h * HG + hh
                        ins = dve.tensor_tensor_reduce(Pp[:, n % 4, s], bank[:, s],
                                                       C("cmpmask")[:, i * CHP:(i + 1) * CHP], -NSA_SCALE, CLAMP,
                                                       ALU.add, ALU.min, nmp[:, k, c:c + 1])
                else:
                    w = (i + 1) * P
                    mask = const[:, a_tri - i * P:a_tri + P]
                    ins = dve.tensor_tensor_reduce(Pp[:, n % 4, 0:w], bank[:, 0:w], mask,
                                                   -(MLA_SCALE if kind == "pmla" else NSA_SCALE), CLAMP,
                                                   ALU.add, ALU.min, nmp[:, k, h:h + 1])
                ins.then_inc(S.free[u % S.n], 1)

            def heads(x):
                return x.rearrange("p (h d) -> p h d", h=H)

            def branch_out(i, kind):
                m = BRANCHES.index((i, kind))
                b, k = KINDS.index(kind), m % 4
                if m == 0:
                    dve.wait_ge(roped, 4 * NT)
                u = V.at("pvalue", UNITS.index((i, kind, 0)))
                bank = heads(arrive(V, u))
                ok(dve.tensor_scalar(coef, lp[:, k, :], 1e-30, None, ALU.max))
                ok(dve.reciprocal(coef, coef))
                if kind != "pmla":
                    ok(dve.tensor_tensor(coef, coef, gate3[:, i, b * H:(b + 1) * H], ALU.mult))
                dst = acc if kind == "pcmp" else otmp
                dve.tensor_tensor(heads(dst), bank, coef.unsqueeze(2).broadcast_to([P, H, HD]), ALU.mult).then_inc(
                    V.free[u % V.n], 1)
                wait_copied(dve, V, u)
                if kind in ("psel", "pwin"):
                    ok(dve.tensor_tensor(acc, acc, otmp, ALU.add))
                if kind == "pwin":
                    z = zs[:, i, MW:]
                    dve.tensor_tensor(z, z, acc, ALU.mult).then_inc(mixed, 1)
                if kind == "pmla":
                    z = zs[:, i, 0:MW]
                    dve.tensor_tensor(z, z, otmp, ALU.mult).then_inc(mixed, 1)

            for step in STEPS:
                kind, a = step[0], step[1:]
                if kind == "x":
                    u, r = T.at(*step, j=1), rows(a[0])
                    dve.tensor_copy(xT[:, 4:8, a[0] * P:a[0] * P + r], four(arrive(T, u), r)).then_inc(T.free[u % T.n], 1)
                elif kind == "proj":
                    work_on(*a)
                elif kind == "post":
                    post_out(*a)
                elif kind == "pos":
                    u = T.at("pos")
                    dve.tensor_copy(peT, arrive(T, u)[:, 0:32].rearrange("p (k n) -> p k n", k=2)).then_inc(
                        T.free[u % T.n], 1)
                elif kind == "bias":
                    u = S.at("bias")
                    dve.tensor_tensor(biasv, arrive(S, u)[0:HD, 0:2], b1[:, :], ALU.add).then_inc(S.free[u % S.n], 1)
                    wait_copied(dve, S, u)
                elif kind == "chunks":
                    t, k, half = a
                    chunks_out(dve.tensor_copy, dve, t, k, 2 * half + 1)
                elif kind == "hid" and a[1] == 1:
                    hidden_sum(a[0])
                elif kind == "hsilu":
                    hidden_silu(a[0])
                elif kind == "cmpout":
                    compressed(a[0])
                elif kind == "wuk":
                    u = T.at(*step)
                    dve.tensor_copy(wukT[:, a[0] * 512:(a[0] + 1) * 512], arrive(T, u)[0:NOPE, :]).then_inc(
                        T.free[u % T.n], 1)
                elif kind == "qhead":
                    u = T.at("qhead")
                    bank = arrive(T, u)[:, 0:H * NS_TOK]
                    dve.tensor_copy(qhT, bank[0:NOPE, :])
                    for p0 in (0, NOPE):
                        ins = dve.tensor_copy(qrope[p0:p0 + ROPE, :].rearrange("p (t h) -> p h t", h=H),
                                              bank[NOPE:QH, :].rearrange("p (h t) -> p h t", h=H))
                    ins.then_inc(T.free[u % T.n], 1)
                elif kind == "keys":
                    keys_out(*a)
                elif kind == "new":
                    newest(*a)
                elif kind == "min":
                    minima(*a)
                elif kind == "norm":
                    if step == ("norm", "sel", 0):
                        dve.wait_ge(grow_in, 16)
                    normalise(*a)
                elif kind == "probs":
                    probs_out(*a)
                elif kind == "pv" and a[0] == "win":
                    u = O.at("pv", "sel", a[1])
                    dve.tensor_copy(orow, arrive(O, u)[:, 0:P]).then_inc(O.free[u % O.n], 1)
                elif kind == "oturn" and a[0] == "sel":
                    nsa_out(a[1])
                elif kind == "omla":
                    u = S.at("omla")
                    zm = zs[0:NS_TOK, ST, 0:MW]
                    dve.tensor_tensor(zm, arrive(S, u)[0:NS_TOK, :], zm, ALU.mult).then_inc(S.free[u % S.n], 1)
                elif kind == "cscore":
                    u = S.at(*step)
                    minimum(S, u, Pc[:, 0:CH], arrive(S, u)[:, 0:CH], C("cmplast"), NSA_SCALE, cmin)
                    wait_copied(dve, S, u)
                    dve.tensor_scalar(cmin, cmin, 1.0, None, ALU.mult).then_inc(cp_min, 1)
                elif kind == "cnorm":
                    dve.wait_ge(grow_in, 16)
                    dve.wait_ge(cp_exp, a[0] + 1)
                    ok(dve.reciprocal(crl, csum))
                    ok(dve.tensor_scalar(Pc[:, 0:CH], Pc[:, 0:CH], crl, None, ALU.mult))
                    dve.tensor_scalar(Pc[:, CH:], Pc[:, 0:CH], grow[:, 0, a[0]:a[0] + 1], None, ALU.mult).then_inc(cp_norm, 1)
                elif kind == "cturn":
                    u = T.at(*step)
                    dve.tensor_copy(PcT, arrive(T, u)[0:CH, 0:2 * P].rearrange("p (v n) -> p v n", v=2)).then_inc(
                        T.free[u % T.n], 1)
                elif kind in ("imp0", "imp1"):
                    u = S.at(*step)
                    dve.tensor_copy(impr if kind == "imp0" else impm, arrive(S, u)[:, 0:SEL_TILES]).then_inc(
                        S.free[u % S.n], 1)
                elif kind == "drop":
                    wait_copied(dve, S, S.at("imp1", a[0]))
                    drop_block()
                elif kind == "onsa":
                    u = T.at("onsa")
                    zn = zs[0:NS_TOK, ST, MW:].rearrange("p (g h d) -> p g h d", g=G, h=HG)
                    on = arrive(T, u)[0:NS_TOK, :].rearrange("p (h g d) -> p h g d", g=G, h=HG)
                    for k in range(G):
                        ins = dve.tensor_tensor(zn[:, k], on[:, :, k, :], zn[:, k], ALU.mult)
                    ins.then_inc(T.free[u % T.n], 1)
                elif kind == "vup":
                    u = S.at(*step)
                    dve.tensor_copy(Vm[:, a[0], :], arrive(S, u)).then_inc(S.free[u % S.n], 1)
                elif kind == "qh":
                    u = T.at(*step, j=1)
                    dve.tensor_copy(QT[:, a[0] % 2, 4:8, :],
                                    arrive(T, u)[0:QH, :].rearrange("p (h n) -> p h n", h=4)).then_inc(T.free[u % T.n], 1)
                elif kind == "pscore":
                    min_unit(*a)
                elif kind == "pturn" and a[0] % 2 == 1:
                    n = a[0]
                    u, w = T.at(*step), P if UNITS[n][1] == "pcmp" else (UNITS[n][0] + 1) * P
                    dve.tensor_copy(PTp[:, n % 4, 0:w], arrive(T, u)[:, 0:w]).then_inc(T.free[u % T.n], 1)
                elif kind == "branch":
                    branch_out(*a)
                elif kind == "mix":
                    u, r = T.at(*step, j=1), rows(ORDER[a[0]])
                    dve.tensor_copy(mixT[:, a[0] % 2, 4:8, 0:r], four(arrive(T, u), r)).then_inc(T.free[u % T.n], 1)
                elif kind == "out":
                    n, r = a[0], rows(ORDER[a[0]])
                    dve.wait_ge(y_in[n % 2], 16 * (n // 2 + 1))
                    y = yb[0:r, n % 2, :]
                    for half in range(2):
                        u = S.at(*step, j=half)
                        yh = y[:, half * 512:(half + 1) * 512]
                        dve.scalar_tensor_tensor(out=yh, in0=yh, scalar=ALPHA, in1=arrive(S, u)[0:r, :],
                                                 op0=ALU.mult, op1=ALU.add).then_inc(S.free[u % S.n], 1)
                        wait_copied(dve, S, u)
                        ok(dve.bn_stats(bnst[0:r, half, :], yh))
                    dve.bn_aggr(bnag[0:r, n % 2, :], bnst[0:r]).then_inc(y_var, 1)
                elif kind == "norm_y":
                    n, r = a[0], rows(ORDER[a[0]])
                    y, root = yb[0:r, n % 2, :], lnr[0:r, n % 2:n % 2 + 1]
                    dve.wait_ge(y_sqrt, n + 1)
                    ok(dve.reciprocal(root, root))
                    dve.tensor_scalar(y, y, bnag[0:r, n % 2, 0:1], root, ALU.subtract, ALU.mult).then_inc(y_norm, 1)

        @block.gpsimd
        def _(pool):
            ok = own(pool, pool_own)

            def rope(out, x, r, n, d, t, table, done, value):
                h = d // 2
                half = 512 if n * d > 256 else 256
                ta, tb = (rtmp[0:r, j * half:j * half + n * d].rearrange("p (n z h) -> p n z h", n=n, z=2)
                          for j in range(2))
                cos = C("cos" + table)[0:r, t * h:(t + 1) * h]
                sin = C("sin" + table)[0:r, t * d:(t + 1) * d].rearrange("p (z h) -> p z h", z=2)
                for z in range(2):
                    pool.tensor_tensor(ta[:, :, z, :], x[:, :, z, :], cos.unsqueeze(1).broadcast_to([r, n, h]), ALU.mult)
                    ins = pool.tensor_tensor(tb[:, :, z, :], x[:, :, 1 - z, :],
                                             sin[:, z, :].unsqueeze(1).broadcast_to([r, n, h]), ALU.mult)
                ok(ins)
                pool.tensor_tensor(out, ta, tb, ALU.add).then_inc(done, 1)
                pool.wait_ge(done, value)

            def halves(x, n):
                return x.rearrange("p (n z h) -> p n z h", n=n, z=2)

            pool.wait_ge(const_in, 16)
            turns = 0
            for step in STEPS:
                if step[0] != "proj" or step[1] in (B_ZMLA, B_ZNSA):
                    continue
                b, t = step[1:]
                r = rows(t)
                turns += 1
                wait_copied(pool, A, A.at("proj", b, t))
                if b == B_MLA:
                    rope(halves(row3[0:r, t, KVL:ROW], 1), halves(araw[0:r, t % 3, QL + KVL:], 1), r, 1, ROPE, t, "m",
                         roped, turns)
                elif b == B_Q:
                    if t >= 2:
                        wait_full(pool, T, T.at("post", b, t - 2, j=1))
                    rope(halves(qrot[0:r, t % 2, :], H), halves(qraw[0:r, t % 2, :], H), r, H, HD, t, "n", roped, turns)
                else:
                    o = KVW if b == B_CMPSEL else 2 * KVW
                    k = halves(kv3[0:r, t, o:o + G * HD], G)
                    rope(k, k, r, G, HD, t, "n", roped, turns)

            def rope_queries(r, t, value):
                x = qm[0:r].rearrange("p (n w) -> p n w", n=H)[:, :, NOPE:QH].rearrange("p n (z h) -> p n z h", z=2)
                rope(x, x, r, H, ROPE, t, "m", q_roped, value)

            wait_full(pool, A, A.at("proj", B_ZNSA, NT - 1))
            ok(pool.memset(bufA[:, 0:2 * SR], 0.0))
            wait_copied(pool, T, T.at("post", B_WINGATE, NT - 1))
            for dst, src in ((qnbd, qnT3), (qrbd, qrT3)):
                for g in range(G):
                    s = slice(g * HD, (g + 1) * HD)
                    ins = pool.tensor_copy(dst[s].rearrange("p (t h) -> p h t", h=H)[:, g * HG:(g + 1) * HG, :],
                                           src[s, :, SEQ:NTOK])
            ins.then_inc(bd_ready, 1)
            pool.wait_ge(bd_ready, 1)
            wait_full(pool, S, S.at("hid", NT - 1, 0))
            ok(pool.memset(padK, 0.0))
            for b, src in enumerate((selKT, winKT)):
                for g in range(G):
                    s = slice(g * HD, (g + 1) * HD)
                    ins = pool.tensor_copy(padK[s, b, g, :], src[s, 0:SEQ])
            ins.then_inc(pad_ready, 1)
            pool.wait_ge(pad_ready, 1)
            for half in range(2):
                wait_copied(pool, S, S.at("qup_s") + half)
            rope_queries(NS_TOK, ST, 1)
            wait_full(pool, S, S.at("kup", 0))
            for h in range(H):
                ins = pool.tensor_copy(KT[NOPE:QH, h, :], krT[NOPE:QH, 0:SEQ])
            ins.then_inc(key_rows, 1)
            pool.wait_ge(key_rows, 1)

            def output(n):
                y = yb[0:rows(ORDER[n]), n % 2, :]
                r = rows(ORDER[n])
                if n == 0:
                    pool.wait_ge(ln_in, 32)
                pool.wait_ge(y_norm, n + 1)
                ok(pool.tensor_tensor(y, y, lng[0:r], ALU.mult))
                pool.tensor_tensor(y, y, lnb[0:r], ALU.add).then_inc(y_done, 1)

            for step in STEPS:
                if step[0] == "qup":
                    for half in range(2):
                        wait_copied(pool, S, S.at(*step) + half)
                    rope_queries(P, step[1], step[1] + 2)
                elif step[0] == "norm_y":
                    output(step[1])

    return nc



    return nc


_INS = ["x_prompt", "x_sample", "cache_mla", "cache_cmp_kv", "cache_sel_kv", "state_win_kv", "page_table", "w_in",
        "q_norm_g", "w_uq", "kv_norm_g", "w_uk", "w_uv", "cmp_pos_emb", "cmp_w1", "cmp_b1", "cmp_w2", "w_o",
        "ln_g", "ln_b"]
_OUTS = [("y_prompt", (1, SEQ, D_MODEL)), ("y_sample", (DEC_B, DEC_T, D_MODEL)), ("p_mla", (1, 1, SEQ, ROW)),
         ("p_cmp", (1, 1, SEQ, 2, G, HD)), ("p_sel", (1, 1, SEQ, 2, G, HD)), ("p_win", (1, 1, SEQ, 2, G, HD)),
         ("s_mla", (1, DEC_B, DEC_T, ROW)), ("s_cmp", (1, DEC_B, DEC_T, 2, G, HD)),
         ("s_sel", (1, DEC_B, DEC_T, 2, G, HD)), ("s_win", (1, DEC_B, WIN, 2, G, HD))]
OUT_NAMES = [f"out_{name}" for name, _ in _OUTS]


def kernel(**inputs):
    import concourse.bacc as bacc
    from concourse.bass_utils import run_bass_kernel_spmd

    nc = bacc.Bacc("TRN2", target_bir_lowering=False, num_devices=1, dynamic_dma_scratch_size=1024)
    arrays, io = {}, {}
    for name in _INS:
        a = np.ascontiguousarray(inputs[name])
        arrays[f"in_{name}"] = a
        io[name] = nc.dram_tensor(f"in_{name}", a.shape, mybir.dt.from_np(a.dtype), kind="ExternalInput").ap()
    arrays["in_const"] = constants()
    io["const"] = nc.dram_tensor("in_const", (P, C_W), F32, kind="ExternalInput").ap()
    for name, shape in _OUTS:
        io[name] = nc.dram_tensor(f"out_{name}", shape, F32, kind="ExternalOutput").ap()
    build(nc, io)
    r = run_bass_kernel_spmd(nc, [arrays], core_ids=[0])
    return tuple(r.results[0][n] for n in OUT_NAMES)
```

```python
import math
from contextlib import ExitStack

import numpy as np

import concourse.bass as bass
from concourse import mybir
from concourse.alu_op_type import AluOpType as ALU

F32 = mybir.dt.float32
I32 = mybir.dt.int32
ACT = mybir.ActivationFunctionType
AX_X = mybir.AxisListType.X

P = 128
D_MODEL = 1024
SEQ = 512
DEC_B, DEC_T = 8, 4
PAST = 1024
PAGE = 128
PAGES = PAST // PAGE
NS_TOK = DEC_B * DEC_T
NTOK = SEQ + NS_TOK
PT = SEQ // P
NT = PT + 1
ST = PT
KC = D_MODEL // P
H = 8
G, HG = 2, 4
HD = 64
NOPE, ROPE, KVL, QL = 64, 32, 128, 256
QH = NOPE + ROPE
ROW = KVL + ROPE
MW = H * HD
KVW = 2 * G * HD
CMP_B, CMP_S, SELB = 32, 16, 64
WIN = 512
CH = PAST // CMP_S
CHP = SEQ // CMP_S
NBLK = PAST // SELB
SEL_TILES = NBLK + 1
GB = 4
NG = DEC_B // GB
RB = DEC_T * H
MLA_SCALE = (NOPE + ROPE) ** -0.5
NSA_SCALE = HD ** -0.5
ALPHA = 2 ** 0.25
RMS_EPS, LN_EPS = 1e-6, 1e-5
NEG = -1e30
CLAMP = 1e28

CUTS = np.cumsum([0, QL, KVL, ROPE, MW, MW, KVW, KVW, KVW, 3 * H, MW]).tolist()
BLK = [(CUTS[0], CUTS[3] - CUTS[0]), (CUTS[4], MW), (CUTS[5], 2 * KVW), (CUTS[3], MW),
       (CUTS[7], KVW + 3 * H), (CUTS[9], MW)]
B_MLA, B_Q, B_CMPSEL, B_ZMLA, B_WINGATE, B_ZNSA = range(6)
IN_W = CUTS[-1]

C_PARTS = [("ident", P), ("cosn", NT * 32), ("sinn", NT * 64), ("cosm", NT * 16), ("sinm", NT * 32),
           ("winzero", 4), ("zero", 512), ("tri", P), ("cmpmask", PT * CHP), ("newmask", NG * NS_TOK),
           ("imap", SEL_TILES), ("headsum", P), ("jidx", SEL_TILES), ("cmplast", PAST // CMP_S), ("eps", 2)]
C_AT = {}
C_W = 0
for _n, _w in C_PARTS:
    C_AT[_n] = (C_W, _w)
    C_W += _w


def rows(t):
    return P if t < PT else NS_TOK


def constants():
    c = np.zeros((P, C_W), np.float32)

    def put(name):
        a, w = C_AT[name]
        return c[:, a:a + w]

    put("ident")[:] = np.eye(P, dtype=np.float32)
    for t in range(NT):
        r = rows(t)
        pos = np.arange(r) + P * t if t < PT else PAST + np.arange(r) % DEC_T
        for d, cn, sn in ((HD, "cosn", "sinn"), (ROPE, "cosm", "sinm")):
            inv = (np.float32(1.0) / (np.float32(10000.0) ** (np.arange(0, d, 2, dtype=np.float32) / np.float32(d)))).astype(np.float32)
            ang = pos.astype(np.float32)[:, None] * inv[None, :]
            h = d // 2
            put(cn)[:r, t * h:(t + 1) * h] = np.cos(ang)
            put(sn)[:r, t * d:t * d + h] = -np.sin(ang)
            put(sn)[:r, t * d + h:(t + 1) * d] = np.sin(ang)
    p = np.arange(P)
    tok = (p // H) % DEC_T
    put("winzero")[:] = np.where(np.arange(4)[None, :] <= tok[:, None], NEG, 0.0)
    put("tri")[:] = np.where(p[None, :] > p[:, None], NEG, 0.0)
    for t in range(PT):
        n = np.arange(CHP)
        bad = (n[None, :] * CMP_S + CMP_B - 1 > (p + P * t)[:, None]) | (n[None, :] >= CHP - 1)
        put("cmpmask")[:, t * CHP:(t + 1) * CHP] = np.where(bad, NEG, 0.0)
    for g in range(NG):
        s = np.arange(NS_TOK)
        b = GB * g + p // RB
        ok = (s[None, :] // DEC_T == b[:, None]) & (s[None, :] % DEC_T <= tok[:, None])
        put("newmask")[:, g * NS_TOK:(g + 1) * NS_TOK] = np.where(ok, 0.0, NEG)
    i, j = np.arange(CH)[:, None], np.arange(SEL_TILES)[None, :]
    lo, hi = np.maximum(i * CMP_S, j * SELB), np.minimum(i * CMP_S + CMP_B, (j + 1) * SELB)
    put("imap")[:CH] = np.maximum(hi - lo, 0) / CMP_B
    put("headsum")[:] = (p[:, None] // HG == p[None, :] // HG)
    put("jidx")[:] = np.arange(SEL_TILES)[None, :]
    put("cmplast")[:, CH - 1] = NEG
    put("eps")[:] = (RMS_EPS, LN_EPS)
    return c


class Uses:

    def __init__(self, n, bank0, steps, count):
        self.n, self.bank0, self.base, at = n, bank0, {}, 0
        for step in steps:
            if count(*step):
                self.base[step] = at
                at += count(*step)

    def at(self, *step, j=0):
        return self.base[step] + j


def weave(a, b):
    out, done, total = [], [0.0, 0.0], [sum(w for _, w in x) for x in (a, b)]
    at = [0, 0]
    while at[0] < len(a) or at[1] < len(b):
        k = int(at[0] == len(a) or (at[1] < len(b) and done[1] / total[1] < done[0] / total[0]))
        steps, w = (a, b)[k][at[k]]
        out += steps
        done[k] += w
        at[k] += 1
    return out


KINDS = ("pcmp", "psel", "pwin", "pmla")
UNITS = ([(i, kind, h) for i in range(PT) for kind in KINDS[:3] for h in range(G if kind == "pcmp" else H)]
         + [(i, "pmla", h) for i in range(PT) for h in range(H)])
NU, N_NSA = len(UNITS), len(UNITS) - PT * H
BRANCHES = []
for _u in UNITS:
    if _u[:2] not in BRANCHES:
        BRANCHES.append(_u[:2])
T_LAG, V_LAG = 3, 5
ORDER = [ST] + list(range(PT))

ITEMS = [("mla", 0), ("mla", 1), ("sel", 0), ("win", 0), ("sel", 1), ("win", 1)]
PAGES_OF = {"mla": PAGES, "sel": PAGES, "win": WIN // PAGE}
BANKS_OF = {k: n // 4 for k, n in PAGES_OF.items()}
KEYS_T = {"mla": 4, "sel": 2, "win": 1}


OUT_AT = {0: 11, 1: 17, 2: 24, 3: 33}


def output_steps(n):
    return [("mix", n), ("out", n, 0), ("out", n, 1), ("root", n), ("norm_y", n)]


def turn_parts(kind, *a):
    if kind == "keys":
        return (KEYS_T[a[0]] + 1) // 2
    return (PAGES_OF[a[0]] // 4 + 2) // 2 if kind == "probs" else 0


def plan():
    posts = (B_MLA, B_Q, B_WINGATE)
    steps = [("x", 0), ("x", 1)]
    seq = [(b, t) for b in range(len(BLK)) for t in range(NT)]
    products = []
    for n, (b, t) in enumerate(seq):
        now = [("zrecip", *seq[n - 1])] if n and seq[n - 1][0] in (B_ZMLA, B_ZNSA) else []
        now.append(("proj", b, t))
        if b == 0 and t + 2 < NT:
            now.append(("x", t + 2))
        if b == 0:
            now.append(("rms", t))
        for lag in (2, 1):
            if n >= lag and seq[n - lag][0] in posts and lag == 1 + (seq[n - lag][0] == B_MLA):
                now.append(("post", *seq[n - lag]))
        products.append((now, BLK[b][1] / 512 * 3.4))
    first = 2 * NT + 1
    for now, _ in products[:first]:
        steps += now
    cmp = [([("pos",)], 1), ([("bias",)], 1), ([("qup_s",)], 1)]
    cmp += [([("chunks", 0, k, half)], 1) for k in range(2) for half in range(2)]
    for t in range(NT):
        def chunks(k, half):
            return ([("chunks", t + 1, k, half)], 1) if t + 1 < NT else ([], 1)

        cmp += [([("hid", t, 0)], 2), ([("cmpout", t - 1)] if t else [], 1), chunks(0, 0), ([("hid", t, 1)], 2),
                chunks(0, 1), ([("hexp", t)], .5), chunks(1, 0), ([("hsilu", t)], .5), chunks(1, 1)]
    cmp.append(([("cmpout", NT - 1)], 1))
    cmp += [([("pad", 0)], .5), ([("pad", 1)], .5)]
    cmp += [([("keys", *ITEMS[0], b, part)], 1) for b in range(2) for part in range(2)]
    steps += weave(products[first:], cmp + [([], 6)])

    s = [([("qhead",)], 1), ([("wuk", 0)], 1), ([("wuk", 1)], 1), ([("qlat",)], 1.5), ([("zrecip", *seq[-1])], .5)]

    def compressed(g):
        return [([(k, g)], 1) for k in ("cscore", "cexp", "cnorm", "cturn", "imp0", "imp1", "drop")]

    for n, x in enumerate(ITEMS):
        last = ITEMS[n - 1] if n else None
        nxt = ITEMS[n + 1] if n + 1 < len(ITEMS) else None
        body = [([("score", *x, 0)], 1)]
        if last:
            body.append(([("probs", *last)], 1))
        body.append(([("score", *x, 1)], 1))
        if last:
            body.append(([("pv", *last)], 2))
        body += [([("keys", *x, 2)], 1.5), ([("keys", *x, 3)], 1.5), ([("score", *x, 2)], 1), ([("new", *x)], .5),
                 ([("score", *x, 3)], 1), ([("min", *x)], 1.5)]
        body += [([("keys", *nxt, 0)] if nxt else [], 1.5), ([("exp", *x)], 1.5),
                 ([("keys", *nxt, 1)] if nxt else [], 1.5), ([("norm", *x)], 1.5)]
        if last and last[0] == "sel":
            g = last[1]
            body.insert(8, ([("kup", 2 * g)], .6))
            body.insert(10, ([("kup", 2 * g + 1)], .6))
        if last and last[0] != "sel":
            body.insert(6, ([("oturn", "sel" if last[0] == "win" else "mla", last[1])], 1))
        c = {("mla", 1): (0, 0), ("win", 0): (4, 1)}.get(x)
        if c:
            a, g = c
            mixed = body[:a]
            for j, step in enumerate(body[a:]):
                mixed.append(step)
                if j < 7:
                    mixed.append(compressed(g)[j])
            body = mixed
        if x == ("sel", 0):
            body.insert(9, ([("omla",)], 1))
        s += body
    s += [([("probs", *ITEMS[-1])], 1.5), ([("pv", *ITEMS[-1])], 2.5), ([("oturn", "sel", NG - 1)], 1), ([("onsa",)], 1)]
    s = [([(*step, part) for step in now] if n else now, w / max(n, 1))
         for now, w in s for n in [turn_parts(*now[0]) if now else 0] for part in range(max(n, 1))]

    def slot(m):
        now = []
        if m < NU:
            now.append(("pscore", m))
        if T_LAG <= m < NU + T_LAG:
            now.append(("pturn", m - T_LAG))
        if V_LAG <= m < NU + V_LAG:
            now.append(("pvalue", m - V_LAG))
        n = m - V_LAG
        if 0 <= n < NU and (n + 1 == NU or UNITS[n + 1][:2] != UNITS[n][:2]):
            now.append(("branch", *UNITS[n][:2]))
        return now

    def cost(m):
        i, kind, _ = UNITS[min(m, NU - 1)]
        return 0.5 if kind == "pcmp" else 0.4 * (i + 1) + 0.2

    p = [(slot(m), cost(m)) for m in range(N_NSA)]
    for t in range(PT):
        p.insert(N_NSA // 2 + 18 + 4 * t, ([("vup", t)], .6))
    p.insert(N_NSA, ([("qup", 0)], 1))
    p.append(([("qh", 0)], 1))
    steps += weave(s, p)

    for m in range(N_NSA, NU + V_LAG):
        steps += slot(m)
        k, h = divmod(m - N_NSA, H)
        if h == 1 and k + 1 < PT:
            steps.append(("qup", k + 1))
        if h == 4 and k + 1 < PT:
            steps.append(("qh", k + 1))
        for n, m0 in OUT_AT.items():
            if 0 <= m - N_NSA - m0 < (5 if n < PT - 1 else 2):
                steps.append(output_steps(n)[m - N_NSA - m0])
    (_, _, out1, root, norm), (mix_, out0_, out1_, root_, norm_) = output_steps(PT - 1), output_steps(PT)
    steps += [out1, mix_, root, out0_, norm, out1_, root_, norm_]
    return steps


def s_uses(kind, *a):
    return {"qlat": 1, "omla": 1, "new": 1, "cscore": 1, "imp0": 1, "imp1": 1, "kup": 1,
            "vup": 1, "pscore": 1}.get(kind, 0)


def a_uses(kind, *a):
    if kind == "score":
        return BANKS_OF[a[0]] if a[2] == 0 else 0
    if kind == "out":
        return int(a != (0, 1))
    return {"proj": 1, "qup": 2}.get(kind, 0)


def t_uses(kind, *a):
    if kind == "post":
        return 2 if a[0] == B_Q else 1
    if kind == "keys":
        return min(2, KEYS_T[a[0]] - 2 * a[3])
    if kind == "probs":
        return min(2, PAGES_OF[a[0]] // 4 + 1 - 2 * a[2])
    return {"x": 2, "pos": 1, "wuk": 1, "qhead": 1, "cturn": 1, "oturn": 1, "onsa": 1, "qh": 2, "pturn": 1,
            "mix": 2}.get(kind, 0)


def spare_bank(i, kind, h=0):
    return kind == "pmla" and i % 2 == 1 and h == 0


def o_uses(kind, *a):
    return int(kind == "cmpout" or (kind == "pv" and a[0] != "win") or (kind == "pvalue" and spare_bank(*UNITS[a[0]])))


def v_uses(kind, *a):
    return int(kind == "pvalue" and UNITS[a[0]][2] == 0 and not spare_bank(*UNITS[a[0]]))


def build(nc, io):
    STEPS = plan()
    A = Uses(2, 0, STEPS, a_uses)
    S = Uses(2, 2, STEPS, s_uses)
    T = Uses(2, 4, STEPS, t_uses)
    K = Uses(2, 2, STEPS, lambda kind, *a: 2 if kind == "chunks" else 0)
    B = Uses(1, 7, STEPS, lambda kind, *a: 2 if kind == "qup_s" else int(kind == "bias" or (kind == "hid" and a[1] == 0)))
    O = Uses(1, 6, STEPS, o_uses)
    V = Uses(1, 7, STEPS, v_uses)
    SLOT, SLOTS = 2048, 5
    LOADS = [(("sel", 0, 2), 5, None), (("sel", 0, 3), 6, None), (("sel", 0, 0), 4, ("mla", 0)),
             (("sel", 0, 1), 3, ("mla", 0)), (("win", 0, 0), 2, ("mla", 1)), (("win", 0, 1), 1, ("mla", 1)),
             (("sel", 1, 0), 0, ("mla", 1)), (("sel", 1, 1), 4, ("sel", 0)), (("sel", 1, 2), 3, ("sel", 0)),
             (("sel", 1, 3), 6, ("sel", 0)), (("win", 1, 0), 2, ("win", 0)), (("win", 1, 1), 1, ("win", 0))]
    SLOT_OF = {what: k for what, k, _ in LOADS}

    def ring_landed(what):
        n = 0
        for w, k, _ in LOADS:
            if k == SLOT_OF[what]:
                n += 16 * (PAGES if w[0] == "sel" else 2)
                if w == what:
                    return n

    with ExitStack() as ctx:
        def sb(name, parts, cols, dt=F32):
            return ctx.enter_context(nc.sbuf_tensor(name, [parts, cols], dt))

        def sem(name):
            return ctx.enter_context(nc.semaphore(name))

        psum = ctx.enter_context(nc.psum_tensor("psum", [P, 8, 512], F32))

        def bank_of(pool, u):
            return psum[:, pool.bank0 + u % pool.n, :]

        const = sb("const", P, C_W)
        gains = sb("gains", P, QL + KVL)
        wuq = sb("wuq", P, 2 * H * QH)
        wuk = sb("wuk", P, H * NOPE)
        wuv = sb("wuv", P, H * HD)
        w2 = sb("w2", HD, 2 * HD)
        b1 = sb("b1", HD, 2)
        wring = sb("wring", P, 2 * 4096)
        row = sb("row", P, NT * ROW)
        zsil = sb("zsil", P, NT * 2 * MW)
        kv = sb("kv", P, NT * 3 * KVW)
        gate = sb("gate", P, NT * 3 * H)
        cqT = sb("cqT", P, 2 * NTOK)
        ckvT = sb("ckvT", P, NTOK)
        krT = sb("krT", QH, NTOK)
        selKT = sb("selKT", P, NTOK)
        winKT = sb("winKT", P, NTOK)
        qnT = sb("qnT", P, HG * NTOK)
        qrT = sb("qrT", P, HG * NTOK)
        small = sb("small", P, 256)
        rtmp = sb("rtmp", P, 2 * 512)
        ring = sb("ring", P, SLOTS * SLOT)
        mid = sb("mid", P, 4096)
        w1h = sb("w1h", P, 2048 + 1536)
        bufA = sb("bufA", P, 4896)
        comp = sb("comp", P, 2080)
        ptab = sb("ptab", 1, DEC_B * PAGES, I32)
        gdram = nc.dram_tensor("gate_rows", [3, DEC_B * RB], F32).ap()

        def C(name):
            a, w = C_AT[name]
            return const[:, a:a + w]

        ident = C("ident")
        wr = wring[:, :].rearrange("p (s c n) -> p s c n", s=2, c=KC)
        wo = ring[:, 0:4 * SLOT].rearrange("p (c n) -> p c n", c=KC)
        row3 = row[:, :].rearrange("p (t n) -> p t n", t=NT)
        zs = zsil[:, :].rearrange("p (t n) -> p t n", t=NT)
        kv3 = kv[:, :].rearrange("p (t n) -> p t n", t=NT)
        gate3 = gate[:, :].rearrange("p (t n) -> p t n", t=NT)
        cqT3 = cqT[:, :].rearrange("p (c t) -> p c t", c=2)
        qnT3 = qnT[:, :].rearrange("p (h t) -> p h t", h=HG)
        qrT3 = qrT[:, :].rearrange("p (h t) -> p h t", h=HG)
        wuq3 = wuq[:, :].rearrange("p (c n) -> p c n", c=2)

        class Carve:

            def __init__(self, buf):
                self.buf, self.at = buf, 0

            def __call__(self, n, parts=P):
                self.at += n
                assert self.at <= self.buf.shape[1]
                return self.buf[0:parts, self.at - n:self.at]

        take = Carve(bufA)
        xT = take(KC * NTOK).rearrange("p (c t) -> p c t", c=KC)
        take = Carve(mid)
        xin = take(2048).rearrange("p (s n) -> p s n", s=2)
        araw = take(3 * 416).rearrange("p (s n) -> p s n", s=3)
        peN = take(256, 16)
        peT = take(32).rearrange("p (k n) -> p k n", k=2)
        chT = mid[:, :].rearrange("p (k g c n) -> p k g c n", k=2, g=G, c=8)
        take = Carve(comp)
        qraw = take(1024).rearrange("p (s n) -> p s n", s=2)
        qrot = take(1024).rearrange("p (s n) -> p s n", s=2)
        take = Carve(comp)
        kcT = take(NTOK)
        vc = take(DEC_B * P, CH).rearrange("p (b n) -> p b n", b=DEC_B)
        vcbd = take(G * HG * HD).rearrange("p (g n) -> p g n", g=G)
        take = Carve(w1h)
        w1 = take(2048).rearrange("p (k c r e) -> p k c r e", k=2, c=8, r=2)
        hsh = take(512, HD).rearrange("p (k g n) -> p k g n", k=2, g=G)
        hid = take(512, HD).rearrange("p (k g n) -> p k g n", k=2, g=G)
        hez = take(512, HD).rearrange("p (k g n) -> p k g n", k=2, g=G)
        SR = DEC_B * RB
        take = Carve(bufA)
        qnbd, qrbd = take(SR), take(SR)
        qlatT = take(SR)
        qrope = take(SR)
        krp = mid[0:ROPE, 2048:4096].rearrange("p (s n) -> p s n", s=2)
        Ps = take(PAST + NS_TOK)
        olatT = take(SR)
        qm = take(H * QH)
        qhPc = take(H * NS_TOK)
        qhT, Pc = qhPc[0:NOPE, :], qhPc[:, 0:2 * CH]
        wukTo = take(H * P)
        wukT, orow = wukTo[0:NOPE, :], wukTo[:, 0:P]
        take = Carve(w1h)
        kt = take(2048).rearrange("p (s n) -> p s n", s=2)
        PTs = take(9 * P).rearrange("p (k n) -> p k n", k=9)
        oTs = take(HG * NS_TOK).rearrange("p (h t) -> p h t", h=HG)
        PcT = take(256, CH).rearrange("p (v n) -> p v n", v=2)
        take = Carve(wring)
        Pp = take(2048).rearrange("p (s n) -> p s n", s=4)
        PTp = take(2048).rearrange("p (s n) -> p s n", s=4)
        KT = take(4096, QH).rearrange("p (h n) -> p h n", h=H)
        QT = ring[0:QH, 4 * SLOT:].rearrange("p (s h n) -> p s h n", s=2, h=H)
        take = Carve(mid)
        padK = take(2 * G * SEQ).rearrange("p (b g n) -> p b g n", b=2, g=G)
        Vm = take(2048).rearrange("p (t n) -> p t n", t=PT)
        acc = bufA[:, 4896 - MW:4896]
        ezr = rtmp[:, :].rearrange("p (s n) -> p s n", s=2)
        otmp = rtmp[:, 512:1024]
        qs = [gains[0:NS_TOK, :], acc[0:NS_TOK, 0:4 * QH]]
        take = Carve(bufA)
        yb = take(2 * D_MODEL).rearrange("p (s n) -> p s n", s=2)
        take = Carve(comp)
        mixT = take(2 * KC * P).rearrange("p (s c n) -> p s c n", s=2, c=KC)
        take = Carve(w1h)
        lng, lnb = take(D_MODEL), take(D_MODEL)
        take = Carve(small)
        ssq = take(2 * NT).rearrange("p (t n) -> p t n", t=NT)
        rstd = take(2 * NT).rearrange("p (t n) -> p t n", t=NT)
        nmin = take(4)
        lsum, rl = take(1), take(1)
        cmin, csum, crl = take(1), take(1), take(1)
        grow = take(6).rearrange("p (b g) -> p b g", b=3)
        impr, impm, dropb = take(SEL_TILES), take(SEL_TILES), take(SEL_TILES)
        selc = take(2)
        biasv = take(2, HD)
        nmp = take(4 * H).rearrange("p (s h) -> p s h", s=4)
        lp = take(4 * H).rearrange("p (s h) -> p s h", s=4)
        coef = take(H)
        bnst = take(12).rearrange("p (s n) -> p s n", s=2)
        bnag = take(4).rearrange("p (s n) -> p s n", s=2)
        lnr, warm = take(2), take(1)

        for pool, name in ((A, "a"), (S, "s"), (T, "t"), (O, "o"), (V, "v"), (K, "c"), (B, "b")):
            pool.full = [sem(f"{name}_full{i}") for i in range(pool.n)]
            pool.free = [sem(f"{name}_free{i}") for i in range(pool.n)]

        def wait_full(eng, pool, u):
            eng.wait_ge(pool.full[u % pool.n], u // pool.n + 1)

        def wait_copied(eng, pool, u):
            eng.wait_ge(pool.free[u % pool.n], u // pool.n + 1)

        c_land = [sem(f"c_land{i}") for i in range(2)]
        m_land = [sem(f"m_land{i}") for i in range(DEC_B)]
        r_land = [sem(f"r_land{i}") for i in range(7)]
        sel_read = sem("sel_read")
        ident_in, const_in, page_in, wsmall_in, pos_in, wo_in, ln_in = (
            sem(n) for n in ("ident_in", "const_in", "page_in", "wsmall_in", "pos_in", "wo_in", "ln_in"))
        x_in = [sem(f"x_in{i}") for i in range(2)]
        w_in = [sem(f"w_in{i}") for i in range(2)]
        y_in = [sem(f"y_in{i}") for i in range(2)]
        y_out = [sem(f"y_out{i}") for i in range(2)]
        cmp_out, rows_out, win_copy, grow_out, grow_in = (
            sem(n) for n in ("cmp_out", "rows_out", "win_copy", "grow_out", "grow_in"))
        roped = sem("roped")
        sqrt_done = sem("sqrt_done")
        normed = sem("normed")
        z_recip = sem("z_recip")
        z_done = sem("z_done")
        gate_done = sem("gate_done")
        h_shift, h_exp, h_done = sem("h_shift"), sem("h_exp"), sem("h_done")
        q_roped = sem("q_roped")
        bd_ready = sem("bd_ready")
        pad_ready = sem("pad_ready")
        sp_min, sp_exp, sp_norm = sem("sp_min"), sem("sp_exp"), sem("sp_norm")
        cp_min, cp_exp, cp_norm = sem("cp_min"), sem("cp_exp"), sem("cp_norm")
        summed = sem("summed")
        mixed_n = sem("mixed_n")
        mixed_m = sem("mixed_m")
        key_rows = sem("key_rows")
        p_exp = sem("p_exp")
        y_var, y_sqrt, y_done = sem("y_var"), sem("y_sqrt"), sem("y_done")
        act_own, dve_own, pool_own = sem("act_own"), sem("dve_own"), sem("pool_own")

        def own(eng, s):
            count = [0]

            def f(ins):
                count[0] += 1
                ins.then_inc(s, 1)
                eng.wait_ge(s, count[0])
            return f

        def nchunks(t):
            return P if t < PT else CHP

        def chunks_out(copy, eng, t, k, j):
            n = nchunks(t)
            u = K.at("chunks", t, k, j // 2, j=j % 2)
            wait_full(eng, K, u)
            bank = bank_of(K, u)[:, 0:4 * n].rearrange("p (c z n) -> p c z n", c=2, z=2)
            for g in range(G):
                for z in range(2):
                    ins = copy(chT[z * HD:(z + 1) * HD, k, g, 2 * j:2 * j + 2, 0:n],
                               bank[g * HD:(g + 1) * HD, :, z, :])
            ins.then_inc(K.free[u % K.n], 1)

        def parts(b):
            w = BLK[b][1]
            cuts = [0, HD, 2 * HD, 3 * HD, w] if b == B_WINGATE else [j * w // 4 for j in range(5)]
            return [(j, cuts[j], cuts[j + 1]) for j in range(4)]

        def value_bank(i, kind):
            pool = O if spare_bank(i, kind) else V
            return pool, pool.at("pvalue", UNITS.index((i, kind, 0)))

        def z_of(b, t):
            r = rows(t)
            return (zs[0:r, t, 0:MW], zs[0:r, t, MW:]) if b == B_ZMLA else (zs[0:r, t, MW:], ezr[0:r, (t + 1) % 2])

        def slot(what):
            k = SLOT_OF[what]
            return ring[:, k * SLOT:(k + 1) * SLOT] if k < SLOTS else wring[:, (k - 3) * SLOT:(k - 2) * SLOT]

        def mla_pages(bb):
            w = PAGES * ROW
            at = SLOTS * SLOT - (bb + 1) * w
            return ring[:, at:at + w].rearrange("p (k n) -> p k n", k=PAGES)

        def x_of(t):
            return io["x_prompt"][0, t * P:(t + 1) * P] if t < PT else io["x_sample"].rearrange("b t d -> (b t) d")

        def y_of(t):
            return io["y_prompt"][0, t * P:(t + 1) * P] if t < PT else io["y_sample"].rearrange("b t d -> (b t) d")

        block = ctx.enter_context(nc.Block())

        @block.sync
        def _(sp):
            def load_x(t):
                if t >= 2:
                    wait_full(sp, T, T.at("x", t - 2, j=1))
                sp.dma_start(xin[0:rows(t), t % 2, :], x_of(t)).then_inc(x_in[t % 2], 16)

            def load_w(b):
                if b >= 2:
                    wait_full(sp, A, A.at("proj", b - 2, NT - 1))
                a, w = BLK[b]
                src = io["w_in"][0].rearrange("(c p) n -> p c n", p=P)[:, :, a:a + w]
                sp.dma_start(wr[:, b % 2, :, 0:w], src).then_inc(w_in[b % 2], 16)

            def page(b, k):
                return sp.value_load(ptab[0:1, b * PAGES + k:b * PAGES + k + 1], min_val=0,
                                     max_val=io["cache_mla"].shape[1] - 1)

            def load_chunks(t):
                dst = ring[:, t % 2 * 2 * SLOT:(t % 2 + 1) * 2 * SLOT]
                if t >= 2:
                    wait_full(sp, K, K.at("chunks", t - 2, 1, 1, j=1))
                if t == PT:
                    sp.wait_ge(cmp_out, 16 * NT)
                    sp.dma_start(dst[0:CHP, :], io["p_cmp"].rearrange(
                        "a b (c s) k g d -> (a b c) (s k g d)", s=CMP_S)).then_inc(c_land[t % 2], 16)
                    return
                cache = io["cache_cmp_kv"][0].rearrange("n (c s) k g d -> n c (s k g d)", s=CMP_S)
                for s in range(2):
                    for k in range(PAGES):
                        n = page(2 * t + s, k)
                        o = s * CH + k * (PAGE // CMP_S)
                        sp.dma_start(dst[o:o + PAGE // CMP_S, :],
                                     cache[bass.ds(n, 1)].rearrange("a c f -> (a c) f")).then_inc(c_land[t % 2], 16)

            def load_pages(dst, landed, b, cache):
                for k in range(PAGES):
                    n = page(b, k)
                    sp.dma_start(dst[:, k, :], cache[bass.ds(n, 1)].rearrange("a t f -> (a t) f")).then_inc(landed, 16)

            sp.dma_start(const[:, 0:P], io["const"][:, 0:P]).then_inc(ident_in, 16)
            load_x(0)
            load_x(1)
            load_w(0)
            sp.dma_start(const[:, P:], io["const"][:, P:]).then_inc(const_in, 16)
            sp.dma_start(gains[:, 0:QL], io["q_norm_g"][0].partition_broadcast(P)).then_inc(wsmall_in, 16)
            sp.dma_start(gains[:, QL:], io["kv_norm_g"][0].partition_broadcast(P)).then_inc(wsmall_in, 16)
            load_x(2)
            sp.dma_start(wuk[:, :], io["w_uk"][0]).then_inc(wsmall_in, 16)
            sp.dma_start(wuv[:, :], io["w_uv"][0]).then_inc(wsmall_in, 16)
            sp.dma_start(wuq3, io["w_uq"][0].rearrange("(c p) n -> p c n", p=P)).then_inc(wsmall_in, 16)
            load_w(1)
            load_x(3)
            for k in range(2):
                for r in range(2):
                    sp.dma_start(w1[:, k, :, r, :],
                                 io["cmp_w1"][0, k, r * CMP_S:(r + 1) * CMP_S].rearrange(
                                     "(c q) d e -> (q d) c e", q=2)).then_inc(wsmall_in, 16)
            sp.dma_start(w2[:, :].rearrange("p (k n) -> p k n", k=2),
                         io["cmp_w2"][0].rearrange("k e d -> e k d")).then_inc(wsmall_in, 16)
            with nc.allow_non_contiguous_dma(reason="128 values"):
                sp.dma_start(b1[:, :], io["cmp_b1"][0].rearrange("k e -> e k")).then_inc(wsmall_in, 16)
            for k in range(2):
                sp.dma_start(peN[:, k * P:(k + 1) * P].rearrange("p (q d) -> p q d", q=2),
                             io["cmp_pos_emb"][0, :, k].rearrange("(n q) d -> n q d", q=2)).then_inc(pos_in, 16)
            sp.dma_start(ptab[:, :], io["page_table"].rearrange("b k -> (b k)").unsqueeze(0)).then_inc(page_in, 16)
            load_x(4)
            load_w(2)
            sp.wait_ge(page_in, 16)
            load_chunks(0)
            load_w(3)
            load_chunks(1)
            load_chunks(2)
            for t in range(NT):
                wait_copied(sp, A, A.at("proj", B_CMPSEL, t))
                dst = (io["p_cmp"][0, 0, t * P:(t + 1) * P] if t < PT
                       else io["s_cmp"][0].rearrange("b t k g d -> (b t) k g d"))
                sp.dma_start(dst.rearrange("t k g d -> t (k g d)"), kv3[0:rows(t), t, 0:KVW]).then_inc(cmp_out, 16)
            load_w(4)
            load_chunks(3)
            load_w(5)
            load_pages(mla_pages(0), m_land[0], 0, io["cache_mla"][0])
            load_chunks(4)
            sp.dma_start(io["s_win"][0, :, 0:WIN - DEC_T].rearrange("b t k g d -> b (t k g d)"),
                         io["state_win_kv"][0, :, DEC_T:].rearrange("b t k g d -> b (t k g d)")).then_inc(win_copy, 16)
            for t in range(NT):
                sp.wait_ge(normed, t + 1)
                sp.wait_ge(roped, t + 1)
                dst = io["p_mla"][0, 0, t * P:(t + 1) * P] if t < PT else io["s_mla"][0].rearrange("b t f -> (b t) f")
                sp.dma_start(dst, row3[0:rows(t), t, :]).then_inc(rows_out, 16)
            sp.wait_ge(gate_done, NT)
            with nc.allow_non_contiguous_dma(reason="768 values"):
                sp.dma_start(gdram.rearrange("b (t h) -> t b h", h=H),
                             gate3[0:NS_TOK, ST, :].rearrange("p (b h) -> p b h", b=3)).then_inc(grow_out, 16)
                sp.wait_ge(grow_out, 16)
                sp.dma_start(grow, gdram.rearrange("b (g p) -> p b g", p=P)).then_inc(grow_in, 16)
            wait_full(sp, K, K.at("chunks", PT - 1, 1, 1, j=1))
            for b in range(1, DEC_B):
                if b == GB:
                    wait_full(sp, K, K.at("chunks", PT, 1, 1, j=1))
                load_pages(mla_pages(b), m_land[b], b, io["cache_mla"][0])
            for t in range(NT):
                sp.wait_ge(roped, 3 * NT + t + 1)
                r = rows(t)
                dst = (io["p_sel"][0, 0, t * P:(t + 1) * P] if t < PT
                       else io["s_sel"][0].rearrange("b t k g d -> (b t) k g d"))
                sp.dma_start(dst.rearrange("t k g d -> t (k g d)"), kv3[0:r, t, KVW:2 * KVW]).then_inc(rows_out, 16)
                if t < PT:
                    sp.dma_start(io["p_win"][0, 0, t * P:(t + 1) * P].rearrange("t k g d -> t (k g d)"),
                                 kv3[0:r, t, 2 * KVW:]).then_inc(rows_out, 16)
                else:
                    for b in range(DEC_B):
                        sp.dma_start(io["s_win"][0, b, WIN - DEC_T:].rearrange("t k g d -> t (k g d)"),
                                     kv3[b * DEC_T:(b + 1) * DEC_T, t, 2 * KVW:]).then_inc(rows_out, 16)
            for what, k, last in LOADS:
                if last is None:
                    wait_full(sp, A, A.at("proj", B_ZNSA, NT - 1))
                elif last[0] == "sel":
                    sp.wait_ge(sel_read, last[1] + 1)
                else:
                    wait_full(sp, O, O.at("pv", *(("sel", last[1]) if last[0] == "win" else last)))
                kind, g, b = what
                if kind == "sel":
                    load_pages(slot(what).rearrange("p (k n) -> p k n", k=PAGES), r_land[k], g * GB + b,
                               io["cache_sel_kv"][0].rearrange("n t k g d -> n t (k g d)"))
                else:
                    dst = slot(what).rearrange("p (b k n) -> p b k n", b=2, n=KVW)
                    for c in range(2):
                        src = io["state_win_kv"][0, g * GB + 2 * b + c].rearrange("(k p) z g d -> p k (z g d)", p=P)
                        sp.dma_start(dst[:, c], src).then_inc(r_land[k], 16)
            wait_full(sp, A, A.at("score", *ITEMS[-1], 0))
            sp.dma_start(lng, io["ln_g"][0].partition_broadcast(P)).then_inc(ln_in, 16)
            sp.dma_start(lnb, io["ln_b"][0].partition_broadcast(P)).then_inc(ln_in, 16)
            wait_full(sp, O, O.at("pv", "sel", NG - 1))
            sp.dma_start(wo, io["w_o"][0].rearrange("(c p) n -> p c n", p=P)).then_inc(wo_in, 16)
            wait_full(sp, T, T.at("onsa"))

            def store_y(n):
                sp.wait_ge(y_done, n + 1)
                sp.dma_start(y_of(ORDER[n]), yb[0:rows(ORDER[n]), n % 2, :]).then_inc(y_out[n % 2], 16)

            for n, t in enumerate(ORDER):
                if n >= 2:
                    sp.wait_ge(y_out[n % 2], 16 * (n // 2))
                sp.dma_start(yb[0:rows(t), n % 2, :], x_of(t)).then_inc(y_in[n % 2], 16)
                if n >= 1:
                    store_y(n - 1)
            store_y(NT - 1)
            sp.wait_ge(y_out[0], 16 * ((NT + 1) // 2))
            sp.wait_ge(y_out[1], 16 * (NT // 2))
            sp.wait_ge(win_copy, 16)
            sp.wait_ge(rows_out, 16 * (NT + 2 * PT + 1 + DEC_B))

        @block.tensor
        def _(pe):
            def claim(pool, u):
                if u >= pool.n:
                    pe.wait_ge(pool.free[u % pool.n], u // pool.n)
                return bank_of(pool, u)

            def turn(out, in_):
                return pe.transpose(out, in_, ident[0:in_.shape[0], 0:in_.shape[0]])

            def turn_x(t):
                pe.wait_ge(x_in[t % 2], 16 * (t // 2 + 1))
                r = rows(t)
                for j in range(2):
                    u = T.at("x", t, j=j)
                    bank = claim(T, u)
                    for c in range(4):
                        k = 4 * j + c
                        ins = turn(bank[:, c * r:(c + 1) * r], xin[0:r, t % 2, k * P:(k + 1) * P])
                    ins.then_inc(T.full[u % T.n], 1)

            def project(b, t):
                if t == 0:
                    pe.wait_ge(w_in[b % 2], 16 * (b // 2 + 1))
                if b == 0:
                    for j in range(2):
                        wait_copied(pe, T, T.at("x", t, j=j))
                w = BLK[b][1]
                u = A.at("proj", b, t)
                bank = claim(A, u)
                for c in range(KC):
                    if t < PT:
                        ins = pe.matmul(bank[:, 0:w], xT[:, c, t * P:(t + 1) * P], wr[:, b % 2, c, 0:w],
                                        start=(c == 0), stop=(c == KC - 1))
                        continue
                    for j, c0, c1 in parts(b):
                        ins = pe.matmul(bank[j * NS_TOK:(j + 1) * NS_TOK, 0:c1 - c0], xT[:, c, SEQ:NTOK],
                                        wr[:, b % 2, c, c0:c1], start=(c == 0), stop=(c == KC - 1))
                ins.then_inc(A.full[u % A.n], 1)

            def post(b, t):
                r = rows(t)
                if b == B_MLA:
                    pe.wait_ge(normed, t + 1)
                    pe.wait_ge(roped, t + 1)
                    u = T.at("post", b, t)
                    bank = claim(T, u)
                    for c in range(2):
                        turn(bank[:, c * r:(c + 1) * r], araw[0:r, t % 3, c * P:(c + 1) * P])
                    turn(bank[:, 2 * r:3 * r], row3[0:r, t, 0:KVL])
                    turn(bank[0:QH, 3 * r:4 * r], row3[0:r, t, ROW - QH:ROW]).then_inc(T.full[u % T.n], 1)
                elif b == B_Q:
                    for v, src in enumerate((qraw, qrot)):
                        if v == 0:
                            wait_copied(pe, A, A.at("proj", b, t))
                        else:
                            pe.wait_ge(roped, NT + t + 1)
                        u = T.at("post", b, t, j=v)
                        bank = claim(T, u)
                        for hh in range(HG):
                            ins = turn(bank[:, hh * r:(hh + 1) * r], src[0:r, t % 2, hh * P:(hh + 1) * P])
                        ins.then_inc(T.full[u % T.n], 1)
                else:
                    pe.wait_ge(roped, 3 * NT + t + 1)
                    u = T.at("post", b, t)
                    bank = claim(T, u)
                    turn(bank[:, 0:r], kv3[0:r, t, KVW:KVW + G * HD])
                    turn(bank[:, r:2 * r], kv3[0:r, t, 2 * KVW:2 * KVW + G * HD]).then_inc(T.full[u % T.n], 1)

            def turn_chunks(t, k, half):
                n = nchunks(t)
                if k == 0 and half == 0:
                    pe.wait_ge(c_land[t % 2], 16 * (2 * PAGES * (t // 2) + (2 * PAGES if t < PT else 1)))
                src = ring[0:n, t % 2 * 2 * SLOT:(t % 2 + 1) * 2 * SLOT].rearrange("p (s k f) -> p s k f", k=2, f=G * HD)
                for j in (2 * half, 2 * half + 1):
                    u = K.at("chunks", t, k, half, j=j % 2)
                    bank = claim(K, u)
                    for c in range(4):
                        ins = turn(bank[:, c * n:(c + 1) * n], src[:, 4 * j + c, k, :])
                    ins.then_inc(K.full[u % K.n], 1)

            def hidden(t, k):
                n = nchunks(t)
                u = B.at("hid", t, 0)
                bank = claim(B, u) if k == 0 else bank_of(B, u)
                for j in range(4):
                    wait_copied(pe, K, K.at("chunks", t, k, j // 2, j=j % 2))
                out = bank.rearrange("p (k g n) -> p k g n", k=2, g=G)[:, k, :, 0:n]
                for c in range(8):
                    ins = pe.matmul(out, w1[:, k, c, :, :].rearrange("p r e -> p (r e)"), chT[:, k, :, c, 0:n],
                                    start=(c == 0), stop=(c == 7))
                if k == 1:
                    ins.then_inc(B.full[u % B.n], 1)

            def compress_out(t):
                pe.wait_ge(h_done, t + 1)
                n, u = nchunks(t), O.at("cmpout", t)
                bank = claim(O, u)
                wk, wv = w2[:, 0:HD], w2[:, HD:2 * HD]
                for g in range(G):
                    pe.matmul(bank[g * HD:(g + 1) * HD, 0:n], wk, hid[:, 0, g, 0:n], start=True, stop=True)
                for g in range(G):
                    if t < PT:
                        for s in range(2):
                            o = P + (s * G + g) * HD
                            ins = pe.matmul(bank[0:CH, o:o + HD], hid[:, 1, g, s * CH:(s + 1) * CH], wv,
                                            start=True, stop=True)
                    else:
                        for hh in range(HG):
                            ins = pe.matmul(bank[hh * CHP:(hh + 1) * CHP, P + g * HD:P + (g + 1) * HD],
                                            hid[:, 1, g, 0:CHP], wv, start=True, stop=True)
                ins.then_inc(O.full[u % O.n], 1)

            def query_up(pool, first, q, r, half):
                u = first + half
                bank = claim(pool, u)
                for c in range(2):
                    ins = pe.matmul(bank[0:r, 0:4 * QH], cqT3[:, c, q:q + r],
                                    wuq3[:, c, half * 4 * QH:(half + 1) * 4 * QH], start=(c == 0), stop=(c == 1))
                ins.then_inc(pool.full[u % pool.n], 1)

            def source(kind, g, b):
                if kind == "mla":
                    return mla_pages(g * GB + b)
                if kind == "sel":
                    return slot((kind, g, b)).rearrange("p (k n) -> p k n", k=PAGES)
                return slot((kind, g, b // 2)).rearrange("p (b k n) -> p b k n", b=2, k=4)[:, b % 2]

            def turn_keys(kind, g, b, part):
                if part == 0 and kind == "mla":
                    pe.wait_ge(m_land[g * GB + b], 16 * PAGES)
                elif part == 0:
                    what = (kind, g, b if kind == "sel" else b // 2)
                    pe.wait_ge(r_land[SLOT_OF[what]], ring_landed(what))
                src = source(kind, g, b)
                for j in range(2 * part, min(2 * part + 2, KEYS_T[kind])):
                    u = T.at("keys", kind, g, b, part, j=j % 2)
                    bank = claim(T, u)
                    for k in range(4):
                        page = src[:, 4 * (j % 2) + k, :]
                        out = bank[:, k * P:(k + 1) * P]
                        if kind != "mla":
                            ins = turn(out, page[:, 0:G * HD])
                        elif j < 2:
                            ins = turn(out, page[:, 0:KVL])
                        else:
                            ins = turn(out[0:ROPE], page[:, KVL:ROW])
                    ins.then_inc(T.full[u % T.n], 1)

            def score(kind, g, b):
                rc = slice(g * P + b * RB, g * P + (b + 1) * RB)
                u0 = A.at("score", kind, g, 0)
                for j in range(KEYS_T[kind]):
                    wait_copied(pe, T, T.at("keys", kind, g, b, j // 2, j=j % 2))
                for j in range(BANKS_OF[kind]):
                    u = u0 + j
                    out = (claim(A, u) if b == 0 else bank_of(A, u))[b * RB:(b + 1) * RB, :]
                    keys = slice(j * 512, (j + 1) * 512)
                    if kind == "mla":
                        pe.matmul(out, qlatT[:, rc], kt[:, b % 2, keys], start=True, stop=False)
                        ins = pe.matmul(out, qrope[0:ROPE, rc], krp[:, b % 2, keys], start=False, stop=True)
                    else:
                        ins = pe.matmul(out, qrbd[:, rc], kt[:, b % 2, keys], start=True, stop=True)
                    if b == GB - 1:
                        ins.then_inc(A.full[u % A.n], 1)

            def score_new(kind, g):
                u = S.at("new", kind, g)
                cols, new = slice(g * P, (g + 1) * P), slice(SEQ, NTOK)
                out = claim(S, u)[:, 0:NS_TOK]
                if kind == "mla":
                    pe.matmul(out, qlatT[:, cols], ckvT[:, new], start=True, stop=False)
                    ins = pe.matmul(out, qrope[NOPE:QH, cols], krT[NOPE:QH, new], start=False, stop=True)
                else:
                    kT = selKT if kind == "sel" else winKT
                    ins = pe.matmul(out, qrbd[:, cols], kT[:, new], start=True, stop=True)
                ins.then_inc(S.full[u % S.n], 1)

            def turn_probs(kind, g, part):
                tiles = PAGES_OF[kind] + 1
                pe.wait_ge(sp_norm, ITEMS.index((kind, g)) + 1)
                for j in range(8 * part, min(8 * part + 8, tiles), 4):
                    u = T.at("probs", kind, g, part, j=j // 4 % 2)
                    bank = claim(T, u)
                    for k in range(j, min(j + 4, tiles)):
                        w = P if k < tiles - 1 else NS_TOK
                        ins = turn(bank[0:w, (k - j) * P:(k - j + 1) * P], Ps[:, k * P:k * P + w])
                    ins.then_inc(T.full[u % T.n], 1)

            def weigh(kind, g):
                pages = PAGES_OF[kind]
                for j in range(pages // 4 + 1):
                    wait_copied(pe, T, T.at("probs", kind, g, j // 2, j=j % 2))
                u = O.at("pv", "sel" if kind == "win" else kind, g)
                out = bank_of(O, u) if kind == "win" else claim(O, u)
                if kind == "mla":
                    new, v = row3[0:NS_TOK, ST, 0:KVL], slice(0, KVL)
                else:
                    col = KVW if kind == "sel" else 2 * KVW
                    new, v = kv3[0:NS_TOK, ST, col + G * HD:col + KVW], slice(G * HD, KVW)
                pe.matmul(out[:, 0:P], PTs[0:NS_TOK, pages, :], new, start=(kind != "win"), stop=False)
                if kind == "sel":
                    for b in range(GB):
                        pe.matmul(out[b * RB:(b + 1) * RB, 0:P], PcT[:, 1, b * RB:(b + 1) * RB],
                                  vc[:, g * GB + b, :], start=False, stop=False)
                for k in range(pages):
                    for b in range(GB):
                        last = k == pages - 1
                        ins = pe.matmul(out[b * RB:(b + 1) * RB, 0:P], PTs[:, k, b * RB:(b + 1) * RB],
                                        source(kind, g, b)[:, k, v], start=False, stop=last and kind != "sel")
                ins.then_inc(sel_read if kind == "sel" else O.full[u % O.n], 1)

            def scores(n):
                i, kind, h = UNITS[n]
                u = S.at("pscore", n)
                bank = claim(S, u)
                q, keys = slice(i * P, (i + 1) * P), (i + 1) * P
                if kind == "pcmp":
                    if h == 0 and i == 0:
                        wait_copied(pe, O, O.at("cmpout", NT - 1))
                    for hh in range(HG):
                        ins = pe.matmul(bank[:, hh * CHP:(hh + 1) * CHP], qnT3[h * HD:(h + 1) * HD, hh, q],
                                        kcT[h * HD:(h + 1) * HD, SEQ:NTOK], start=True, stop=True)
                elif kind == "pmla":
                    if h == 0:
                        for j in range(2):
                            wait_copied(pe, T, T.at("qh", i, j=j))
                    if h == 0 and i == 0:
                        for j in range(HG):
                            wait_copied(pe, S, S.at("kup", j))
                        pe.wait_ge(key_rows, 2)
                    ins = pe.matmul(bank[:, 0:keys], QT[:, i % 2, h, :], KT[:, h, 0:keys], start=True, stop=True)
                else:
                    if h == 0 and i == 0:
                        pe.wait_ge(pad_ready, 1 + int(kind == "pwin"))
                    g, hh = h // HG, h % HG
                    ins = pe.matmul(bank[:, 0:keys], qrT3[:, hh, q], padK[:, int(kind == "pwin"), g, 0:keys],
                                    start=True, stop=True)
                ins.then_inc(S.full[u % S.n], 1)

            def turn_p(n):
                i, kind, h = UNITS[n]
                u = T.at("pturn", n)
                pe.wait_ge(p_exp, n + 1)
                bank = claim(T, u)
                for j in range(1 if kind == "pcmp" else i + 1):
                    ins = turn(bank[:, j * P:(j + 1) * P], Pp[:, n % 4, j * P:(j + 1) * P])
                ins.then_inc(T.full[u % T.n], 1)

            def values(n):
                i, kind, h = UNITS[n]
                pool, u = value_bank(i, kind)
                bank = claim(pool, u) if h == 0 else bank_of(pool, u)
                wait_copied(pe, T, T.at("pturn", n))
                if kind == "pcmp":
                    ins = pe.matmul(bank[:, h * 256:(h + 1) * 256], PTp[:, n % 4, 0:P], vcbd[:, h, :],
                                    start=True, stop=True)
                else:
                    if kind == "pmla" and h == 0 and i == 0:
                        for t in range(PT):
                            wait_copied(pe, S, S.at("vup", t))
                    for j in range(i + 1):
                        if kind == "pmla":
                            v = Vm[:, j, h * HD:(h + 1) * HD]
                        else:
                            o = (KVW if kind == "psel" else 2 * KVW) + G * HD + (h // HG) * HD
                            v = kv3[:, j, o:o + HD]
                        ins = pe.matmul(bank[:, h * HD:(h + 1) * HD], PTp[:, n % 4, j * P:(j + 1) * P], v,
                                        start=(j == 0), stop=(j == i))
                if n + 1 == NU or UNITS[n + 1][:2] != (i, kind):
                    ins.then_inc(pool.full[u % pool.n], 1)

            pe.wait_ge(ident_in, 16)
            for step in STEPS:
                kind, a = step[0], step[1:]
                if kind == "x":
                    turn_x(*a)
                elif kind == "proj":
                    project(*a)
                elif kind == "post":
                    post(*a)
                elif kind == "pos":
                    pe.wait_ge(const_in, 16)
                    pe.wait_ge(pos_in, 32)
                    u = T.at("pos")
                    bank = claim(T, u)
                    for k in range(2):
                        ins = turn(bank[:, 16 * k:16 * k + 16], peN[:, k * P:(k + 1) * P])
                    ins.then_inc(T.full[u % T.n], 1)
                elif kind == "bias":
                    pe.wait_ge(wsmall_in, 16 * 11)
                    wait_copied(pe, T, T.at("pos"))
                    u = B.at("bias")
                    bank = claim(B, u)
                    for k in range(2):
                        for r in range(2):
                            for c in range(8):
                                ins = pe.matmul(bank[0:HD, k:k + 1], w1[:, k, c, r, :],
                                                peT[:, k, 8 * r + c:8 * r + c + 1],
                                                start=(r == 0 and c == 0), stop=(r == 1 and c == 7))
                    ins.then_inc(B.full[u % B.n], 1)
                elif kind == "chunks":
                    turn_chunks(*a)
                elif kind == "hid":
                    hidden(*a)
                elif kind == "cmpout":
                    compress_out(*a)
                elif kind == "wuk":
                    u = T.at(*step)
                    bank = claim(T, u)
                    for c in range(4):
                        h = 4 * a[0] + c
                        ins = turn(bank[0:NOPE, c * P:(c + 1) * P], wuk[:, h * NOPE:(h + 1) * NOPE])
                    ins.then_inc(T.full[u % T.n], 1)
                elif kind == "qup_s":
                    for half in range(2):
                        query_up(B, B.at("qup_s"), SEQ, NS_TOK, half)
                elif kind == "qhead":
                    pe.wait_ge(q_roped, 2)
                    u = T.at("qhead")
                    bank = claim(T, u)
                    for h in range(H):
                        ins = turn(bank[0:QH, h * NS_TOK:(h + 1) * NS_TOK], qs[h // 4][:, h % 4 * QH:(h % 4 + 1) * QH])
                    ins.then_inc(T.full[u % T.n], 1)
                elif kind == "qlat":
                    for j in range(2):
                        wait_copied(pe, T, T.at("wuk", j))
                    wait_copied(pe, T, T.at("qhead"))
                    u = S.at("qlat")
                    bank = claim(S, u)
                    for h in range(H):
                        ins = pe.matmul(bank[:, h * NS_TOK:(h + 1) * NS_TOK], wukT[:, h * P:(h + 1) * P],
                                        qhT[:, h * NS_TOK:(h + 1) * NS_TOK], start=True, stop=True)
                    ins.then_inc(S.full[u % S.n], 1)
                elif kind == "keys":
                    turn_keys(*a)
                elif kind == "score":
                    if step == ("score", "mla", 0, 0):
                        wait_copied(pe, S, S.at("qlat"))
                    if step == ("score", "sel", 0, 0):
                        pe.wait_ge(bd_ready, 1)
                    score(*a)
                elif kind == "new":
                    score_new(*a)
                elif kind == "probs":
                    turn_probs(*a)
                elif kind == "pv":
                    weigh(*a)
                elif kind == "oturn":
                    wait_copied(pe, O, O.at("pv", *a))
                    u = T.at(*step)
                    turn(claim(T, u)[:, 0:P], orow).then_inc(T.full[u % T.n], 1)
                elif kind == "omla":
                    wait_copied(pe, T, T.at("oturn", "mla", NG - 1))
                    u = S.at("omla")
                    bank = claim(S, u)
                    oh = olatT.rearrange("p (t h) -> p t h", h=H)
                    for h in range(H):
                        ins = pe.matmul(bank[0:NS_TOK, h * HD:(h + 1) * HD], oh[:, :, h], wuv[:, h * HD:(h + 1) * HD],
                                        start=True, stop=True)
                    ins.then_inc(S.full[u % S.n], 1)
                elif kind == "cscore":
                    if a[0] == 0:
                        pe.wait_ge(bd_ready, 1)
                    u = S.at(*step)
                    bank = claim(S, u)
                    for b in range(GB):
                        bb = a[0] * GB + b
                        ins = pe.matmul(bank[b * RB:(b + 1) * RB, 0:CH], qnbd[:, bb * RB:(bb + 1) * RB],
                                        kcT[:, bb * CH:(bb + 1) * CH], start=True, stop=True)
                    ins.then_inc(S.full[u % S.n], 1)
                elif kind == "cturn":
                    pe.wait_ge(cp_norm, a[0] + 1)
                    u = T.at(*step)
                    bank = claim(T, u)
                    turn(bank[0:CH, 0:P], Pc[:, 0:CH])
                    turn(bank[0:CH, P:2 * P], Pc[:, CH:2 * CH]).then_inc(T.full[u % T.n], 1)
                elif kind == "imp0":
                    wait_copied(pe, T, T.at("cturn", a[0]))
                    u = S.at(*step)
                    pe.matmul(claim(S, u)[:, 0:SEL_TILES], PcT[:, 0, :], C("imap")[0:CH, :], start=True,
                              stop=True).then_inc(S.full[u % S.n], 1)
                elif kind == "imp1":
                    wait_copied(pe, S, S.at("imp0", a[0]))
                    u = S.at(*step)
                    pe.matmul(claim(S, u)[:, 0:SEL_TILES], C("headsum"), impr, start=True,
                              stop=True).then_inc(S.full[u % S.n], 1)
                elif kind == "onsa":
                    wait_copied(pe, T, T.at("oturn", "sel", NG - 1))
                    u = T.at("onsa")
                    bank = claim(T, u)
                    for hh in range(HG):
                        ins = turn(bank[0:NS_TOK, hh * P:(hh + 1) * P], oTs[:, hh, :])
                    ins.then_inc(T.full[u % T.n], 1)
                elif kind == "kup":
                    j = a[0]
                    u = S.at(*step)
                    pe.matmul(claim(S, u), wuk[:, j * P:(j + 1) * P], ckvT[:, 0:SEQ], start=True,
                              stop=True).then_inc(S.full[u % S.n], 1)
                elif kind == "vup":
                    t = a[0]
                    u = S.at(*step)
                    pe.matmul(claim(S, u), ckvT[:, t * P:(t + 1) * P], wuv[:, :], start=True,
                              stop=True).then_inc(S.full[u % S.n], 1)
                elif kind == "qup":
                    for half in range(2):
                        query_up(A, A.at(*step), a[0] * P, P, half)
                elif kind == "qh":
                    pe.wait_ge(q_roped, a[0] + 3)
                    for half in range(2):
                        u = T.at(*step, j=half)
                        bank = claim(T, u)
                        for c in range(4):
                            h = 4 * half + c
                            ins = turn(bank[0:QH, c * P:(c + 1) * P], qm[:, h * QH:(h + 1) * QH])
                        ins.then_inc(T.full[u % T.n], 1)
                elif kind == "pscore":
                    scores(*a)
                elif kind == "pturn":
                    turn_p(*a)
                elif kind == "pvalue":
                    values(*a)
                elif kind == "mix":
                    n, t = a[0], ORDER[a[0]]
                    r = rows(t)
                    if n == 0:
                        wait_copied(pe, S, S.at("omla"))
                        wait_copied(pe, T, T.at("onsa"))
                    else:
                        pe.wait_ge(mixed_n, n)
                        pe.wait_ge(mixed_m, n)
                    for j in range(2):
                        u = T.at(*step, j=j)
                        bank = claim(T, u)
                        for c in range(4):
                            ins = turn(bank[:, c * r:(c + 1) * r], zs[0:r, t, (4 * j + c) * P:(4 * j + c + 1) * P])
                        ins.then_inc(T.full[u % T.n], 1)
                elif kind == "out":
                    n, half = a
                    if step == ("out", 0, 0):
                        pe.wait_ge(wo_in, 16)
                    if half == 0:
                        for j in range(2):
                            wait_copied(pe, T, T.at("mix", n, j=j))
                    elif n == 0:
                        continue
                    u = A.at(*step)
                    bank = claim(A, u)
                    for c in range(KC):
                        if n:
                            ins = pe.matmul(bank, mixT[:, n % 2, c, :], wo[:, c, half * 512:(half + 1) * 512],
                                            start=(c == 0), stop=(c == KC - 1))
                            continue
                        w = D_MODEL // 4
                        for j in range(4):
                            ins = pe.matmul(bank[j * NS_TOK:(j + 1) * NS_TOK, 0:w], mixT[:, 0, c, 0:NS_TOK],
                                            wo[:, c, j * w:(j + 1) * w], start=(c == 0), stop=(c == KC - 1))
                    ins.then_inc(A.full[u % A.n], 1)

        @block.scalar
        def _(act):
            ok = own(act, act_own)

            def arrive(pool, u):
                wait_full(act, pool, u)
                return bank_of(pool, u)

            def block_out(b, t):
                r, w = rows(t), BLK[b][1]
                u = A.at("proj", b, t)
                bank = arrive(A, u)
                free = A.free[u % A.n]

                def pieces():
                    if t < PT:
                        return [(0, w, bank[:, 0:w])]
                    return [(c0, c1, bank[j * NS_TOK:(j + 1) * NS_TOK, 0:c1 - c0]) for j, c0, c1 in parts(b)]

                if b == B_MLA:
                    if t >= 3:
                        wait_full(act, T, T.at("post", b, t - 3))
                    for c0, c1, src in pieces():
                        ins = act.copy(araw[0:r, t % 3, c0:c1], src)
                    ins.then_inc(free, 1)
                    wait_copied(act, A, u)
                    junk = zs[0:r, t, 0:QL]
                    ok(act.activation(junk, araw[0:r, t % 3, 0:QL], ACT.Square, accum_out=ssq[0:r, t, 0:1]))
                    ok(act.activation(junk[:, 0:KVL], araw[0:r, t % 3, QL:QL + KVL], ACT.Square,
                                      accum_out=ssq[0:r, t, 1:2]))
                    if t == 0:
                        act.wait_ge(const_in, 16)
                    eps = C("eps")[0:r, 0:1]
                    act.activation(rstd[0:r, t, 0:1], ssq[0:r, t, 0:1], ACT.Sqrt, bias=eps, scale=1.0 / QL)
                    act.activation(rstd[0:r, t, 1:2], ssq[0:r, t, 1:2], ACT.Sqrt, bias=eps,
                                   scale=1.0 / KVL).then_inc(sqrt_done, 1)
                elif b in (B_ZMLA, B_ZNSA):
                    z, e = z_of(b, t)
                    if b == B_ZNSA and t == 0:
                        act.wait_ge(roped, 4 * NT)
                    if b == B_ZNSA and t >= 2:
                        act.wait_ge(z_done, NT + t - 1)
                    for c0, c1, src in pieces():
                        act.copy(z[:, c0:c1], src)
                    for c0, c1, src in pieces():
                        ins = act.activation(e[:, c0:c1], src, ACT.Exp, scale=-1.0)
                    ins.then_inc(free, 1)
                elif b == B_Q:
                    if t >= 2:
                        wait_full(act, T, T.at("post", b, t - 2, j=1))
                    for c0, c1, src in pieces():
                        h0, n = c0 // HD, (c1 - c0) // HD
                        dst = qraw[0:r, t % 2, :].rearrange("p (h g d) -> p g h d", h=HG, g=G)
                        if n < H:
                            ins = act.copy(dst[:, h0 // HG, h0 % HG:h0 % HG + n, :], src.rearrange("p (h d) -> p h d", d=HD))
                        else:
                            ins = act.copy(dst, src.rearrange("p (g h d) -> p g h d", g=G, d=HD))
                    ins.then_inc(free, 1)
                elif b == B_CMPSEL:
                    for c0, c1, src in pieces():
                        ins = act.copy(kv3[0:r, t, c0:c1], src)
                    ins.then_inc(free, 1)
                else:
                    for c0, c1, src in pieces():
                        end = min(c1, KVW)
                        act.copy(kv3[0:r, t, 2 * KVW + c0:2 * KVW + end], src[:, 0:end - c0])
                    act.activation(gate3[0:r, t, :], src[:, KVW - c0:], ACT.Exp, scale=-1.0).then_inc(free, 1)

            def keys_out(kind, g, b, part):
                for j in range(2 * part + 0, min(2 * part + 2, KEYS_T[kind]), 2):
                    u = T.at("keys", kind, g, b, part, j=0)
                    bank = arrive(T, u)
                    if j < 2:
                        ins = act.copy(kt[:, b % 2, 0:512], bank)
                    else:
                        ins = act.copy(krp[:, b % 2, 0:512], bank[0:ROPE, :])
                    ins.then_inc(T.free[u % T.n], 1)

            def probs_out(kind, g, part):
                tiles = PAGES_OF[kind] + 1
                for j in range(8 * part, min(8 * part + 8, tiles), 8):
                    u = T.at("probs", kind, g, part)
                    m = min(4, tiles - j)
                    bank = arrive(T, u)
                    r = NS_TOK if m == 1 else P
                    act.copy(PTs[0:r, j:j + m, :],
                             bank[0:r, 0:m * P].rearrange("p (k n) -> p k n", k=m)).then_inc(T.free[u % T.n], 1)

            def exp_unit(n):
                i, kind, h = UNITS[n]
                u, k = S.at("pscore", n), BRANCHES.index((i, kind)) % 4
                wait_copied(act, S, u)
                if kind == "pcmp":
                    for hh in range(HG):
                        c, s = h * HG + hh, slice(hh * CHP, (hh + 1) * CHP)
                        ins = act.activation(Pp[:, n % 4, s], Pp[:, n % 4, s], ACT.Exp, bias=nmp[:, k, c:c + 1],
                                             scale=-1.0, accum_out=lp[:, k, c:c + 1])
                else:
                    w = (i + 1) * P
                    ins = act.activation(Pp[:, n % 4, 0:w], Pp[:, n % 4, 0:w], ACT.Exp, bias=nmp[:, k, h:h + 1],
                                         scale=-1.0, accum_out=lp[:, k, h:h + 1])
                ins.then_inc(p_exp, 1)

            for step in STEPS:
                kind, a = step[0], step[1:]
                if kind == "x":
                    u, r = T.at(*step, j=0), rows(a[0])
                    act.copy(xT[:, 0:4, a[0] * P:a[0] * P + r],
                             arrive(T, u)[:, 0:4 * r].rearrange("p (c n) -> p c n", c=4)).then_inc(T.free[u % T.n], 1)
                elif kind == "proj":
                    block_out(*a)
                elif kind == "chunks":
                    t, k, half = a
                    chunks_out(act.copy, act, t, k, 2 * half)
                elif kind == "hid" and a[1] == 1:
                    t, n = a[0], nchunks(a[0])
                    bh = arrive(B, B.at("hid", t, 0))[HD:P, :].rearrange("p (k g n) -> p k g n", k=2, g=G)
                    if t >= 1:
                        wait_copied(act, B, B.at("hid", t - 1, 0))
                    act.copy(hsh[:, :, :, 0:n - 1], bh[:, :, :, 1:n]).then_inc(h_shift, 1)
                elif kind == "hexp":
                    t, n = a[0], nchunks(a[0])
                    wait_copied(act, B, B.at("hid", t, 0))
                    act.activation(hez[:, :, :, 0:n], hid[:, :, :, 0:n], ACT.Exp, scale=-1.0).then_inc(h_exp, 1)
                elif kind == "qup_s":
                    act.wait_ge(normed, NT)
                    for half in range(2):
                        u = B.at(*step) + half
                        act.copy(qs[half], arrive(B, u)[0:NS_TOK, 0:4 * QH]).then_inc(B.free[u % B.n], 1)
                elif kind == "wuk":
                    u = T.at(*step)
                    act.copy(wukT[:, a[0] * 512:(a[0] + 1) * 512], arrive(T, u)[0:NOPE, :]).then_inc(T.free[u % T.n], 1)
                elif kind == "qlat":
                    u = S.at("qlat")
                    act.copy(qlatT.rearrange("p (t h) -> p h t", h=H),
                             arrive(S, u)[:, 0:SR].rearrange("p (h t) -> p h t", h=H)).then_inc(S.free[u % S.n], 1)
                elif kind == "keys":
                    keys_out(*a)
                elif kind == "exp":
                    w = PAGES_OF[a[0]] * P + NS_TOK
                    act.wait_ge(sp_min, ITEMS.index(a) + 1)
                    act.activation(Ps[:, 0:w], Ps[:, 0:w], ACT.Exp, bias=nmin[:, 3:4], scale=-1.0,
                                   accum_out=lsum).then_inc(sp_exp, 1)
                elif kind == "cexp":
                    act.wait_ge(cp_min, a[0] + 1)
                    act.activation(Pc[:, 0:CH], Pc[:, 0:CH], ACT.Exp, bias=cmin, scale=-1.0,
                                   accum_out=csum).then_inc(cp_exp, 1)
                elif kind == "probs":
                    probs_out(*a)
                elif kind == "pv" and a[0] == "mla":
                    u = O.at(*step)
                    act.copy(orow, arrive(O, u)[:, 0:P]).then_inc(O.free[u % O.n], 1)
                elif kind == "oturn" and a[0] == "mla":
                    u = T.at(*step)
                    act.copy(olatT[:, a[1] * P:(a[1] + 1) * P], arrive(T, u)[:, 0:P]).then_inc(T.free[u % T.n], 1)
                elif kind == "kup":
                    u, j = S.at(*step), a[0]
                    bank = arrive(S, u)
                    act.copy(KT[0:NOPE, 2 * j, :], bank[0:NOPE, :])
                    act.copy(KT[0:NOPE, 2 * j + 1, :], bank[NOPE:P, :]).then_inc(S.free[u % S.n], 1)
                elif kind == "qup":
                    for half in range(2):
                        u = A.at(*step) + half
                        act.copy(qm[:, half * 4 * QH:(half + 1) * 4 * QH],
                                 arrive(A, u)[:, 0:4 * QH]).then_inc(A.free[u % A.n], 1)
                elif kind == "qh":
                    u = T.at(*step, j=0)
                    act.copy(QT[:, a[0] % 2, 0:4, :],
                             arrive(T, u)[0:QH, :].rearrange("p (h n) -> p h n", h=4)).then_inc(T.free[u % T.n], 1)
                elif kind == "pscore":
                    exp_unit(*a)
                elif kind == "pturn" and a[0] % 2 == 0:
                    n = a[0]
                    u, w = T.at(*step), P if UNITS[n][1] == "pcmp" else (UNITS[n][0] + 1) * P
                    act.copy(PTp[:, n % 4, 0:w], arrive(T, u)[:, 0:w]).then_inc(T.free[u % T.n], 1)
                elif kind == "mix":
                    u, r = T.at(*step, j=0), rows(ORDER[a[0]])
                    act.copy(mixT[:, a[0] % 2, 0:4, 0:r],
                             arrive(T, u)[:, 0:4 * r].rearrange("p (c n) -> p c n", c=4)).then_inc(T.free[u % T.n], 1)
                elif kind == "root":
                    n, r = a[0], rows(ORDER[a[0]])
                    ok(act.activation(warm[0:r], C("eps")[0:r, 1:2], ACT.Sqrt))
                    act.wait_ge(y_var, n + 1)
                    act.activation(lnr[0:r, n % 2:n % 2 + 1], bnag[0:r, n % 2, 1:2], ACT.Sqrt,
                                   bias=C("eps")[0:r, 1:2]).then_inc(y_sqrt, 1)

        @block.vector
        def _(dve):
            ok = own(dve, dve_own)

            def arrive(pool, u):
                wait_full(dve, pool, u)
                return bank_of(pool, u)

            def four(bank, n):
                return bank[:, 0:4 * n].rearrange("p (c n) -> p c n", c=4)

            def work_on(b, t):
                r = rows(t)
                u = A.at("proj", b, t)
                if b == B_MLA:
                    if t == 0:
                        dve.wait_ge(wsmall_in, 16 * 11)
                    dve.wait_ge(sqrt_done, t + 1)
                    ok(dve.reciprocal(rstd[0:r, t, :], rstd[0:r, t, :]))
                    a = araw[0:r, t % 3, :]
                    dve.scalar_tensor_tensor(out=row3[0:r, t, 0:KVL], in0=a[:, QL:QL + KVL], scalar=rstd[0:r, t, 1:2],
                                             in1=gains[0:r, QL:], op0=ALU.mult, op1=ALU.mult)
                    dve.scalar_tensor_tensor(out=a[:, 0:QL], in0=a[:, 0:QL], scalar=rstd[0:r, t, 0:1],
                                             in1=gains[0:r, 0:QL], op0=ALU.mult, op1=ALU.mult).then_inc(normed, 1)
                elif b == B_WINGATE:
                    wait_copied(dve, A, u)
                    e = gate3[0:r, t, :]
                    ok(dve.tensor_scalar(e, e, 1.0, None, ALU.add))
                    dve.reciprocal(e, e).then_inc(gate_done, 1)

            def post_out(b, t):
                r, c0 = rows(t), t * P
                u = T.at("post", b, t)
                if b == B_MLA:
                    bank = arrive(T, u)
                    dve.tensor_copy(cqT3[:, :, c0:c0 + r], bank[:, 0:2 * r].rearrange("p (c n) -> p c n", c=2))
                    dve.tensor_copy(ckvT[:, c0:c0 + r], bank[:, 2 * r:3 * r])
                    dve.tensor_copy(krT[NOPE:QH, c0:c0 + r], bank[NOPE:QH, 3 * r:4 * r]).then_inc(T.free[u % T.n], 1)
                elif b == B_Q:
                    for v, dst in enumerate((qnT3, qrT3)):
                        dve.tensor_copy(dst[:, :, c0:c0 + r], four(arrive(T, u + v), r)).then_inc(
                            T.free[(u + v) % T.n], 1)
                else:
                    bank = arrive(T, u)
                    dve.tensor_copy(selKT[:, c0:c0 + r], bank[:, 0:r])
                    dve.tensor_copy(winKT[:, c0:c0 + r], bank[:, r:2 * r]).then_inc(T.free[u % T.n], 1)

            def compressed(t):
                u = O.at("cmpout", t)
                bank = arrive(O, u)
                if t < PT:
                    dve.tensor_copy(kcT[:, t * P:(t + 1) * P], bank[:, 0:P])
                    ins = dve.tensor_copy(vc[:, 2 * t:2 * t + 2, :],
                                          bank[0:CH, P:3 * P].rearrange("p (b n) -> p b n", b=2))
                else:
                    ok(dve.memset(vcbd, 0.0))
                    dve.tensor_copy(kcT[:, SEQ:NTOK], bank[:, 0:CHP])
                    for hh in range(HG):
                        s = slice(hh * CHP, (hh + 1) * CHP)
                        ins = dve.tensor_copy(vcbd[s, :, hh * HD:(hh + 1) * HD],
                                              bank[s, P:2 * P].rearrange("p (g d) -> p g d", g=G))
                ins.then_inc(O.free[u % O.n], 1)

            def hidden_sum(t):
                n, u = nchunks(t), B.at("hid", t, 0)
                bank = arrive(B, u)[0:HD, :].rearrange("p (k g n) -> p k g n", k=2, g=G)
                dve.wait_ge(h_shift, t + 1)
                if t >= 1:
                    wait_full(dve, O, O.at("cmpout", t - 1))
                dve.memset(hid[:, :, :, n - 1:n], 0.0)
                for k in range(2):
                    ins = dve.scalar_tensor_tensor(out=hid[:, k, :, 0:n - 1], in0=bank[:, k, :, 0:n - 1],
                                                   scalar=biasv[:, k:k + 1], in1=hsh[:, k, :, 0:n - 1],
                                                   op0=ALU.add, op1=ALU.add)
                ins.then_inc(B.free[u % B.n], 1)

            def hidden_silu(t):
                n = nchunks(t)
                dve.wait_ge(h_exp, t + 1)
                e, h = hez[:, :, :, 0:n], hid[:, :, :, 0:n]
                ok(dve.tensor_scalar(e, e, 1.0, None, ALU.add))
                ok(dve.reciprocal(e, e))
                dve.tensor_tensor(h, h, e, ALU.mult).then_inc(h_done, 1)

            def minimum(pool, u, out, src, mask, scale, least):
                dve.tensor_tensor_reduce(out, src, mask, -scale, CLAMP, ALU.add, ALU.min, least).then_inc(
                    pool.free[u % pool.n], 1)

            def newest(kind, g):
                u, at = S.at("new", kind, g), PAGES_OF[kind] * P
                minimum(S, u, Ps[:, at:at + NS_TOK], arrive(S, u)[:, 0:NS_TOK],
                        C("newmask")[:, g * NS_TOK:(g + 1) * NS_TOK], MLA_SCALE if kind == "mla" else NSA_SCALE,
                        nmin[:, 2:3])

            def minima(kind, g):
                n = BANKS_OF[kind]
                for j in range(n):
                    u = A.at("score", kind, g, 0) + j
                    out, src = Ps[:, j * 512:(j + 1) * 512], arrive(A, u)
                    scale = MLA_SCALE if kind == "mla" else NSA_SCALE
                    if kind == "mla":
                        mask = C("zero")
                    elif kind == "win":
                        a = C_AT["winzero"][0]
                        mask = const[:, a:a + WIN]
                    else:
                        out, src = (x.rearrange("p (a b) -> p a b", b=SELB) for x in (out, src))
                        mask = dropb[:, 8 * j:8 * j + 8].unsqueeze(2).broadcast_to([P, 8, SELB])
                    minimum(A, u, out, src, mask, scale, nmin[:, j:j + 1])
                for j in range(n):
                    wait_copied(dve, A, A.at("score", kind, g, 0) + j)
                wait_copied(dve, S, S.at("new", kind, g))
                first = 0 if n == 2 else 1
                if n == 1:
                    ok(dve.tensor_copy(nmin[:, 1:2], nmin[:, 0:1]))
                dve.tensor_reduce(nmin[:, 3:4], nmin[:, first:3], AX_X, ALU.min).then_inc(sp_min, 1)

            def normalise(kind, g):
                w = PAGES_OF[kind] * P + NS_TOK
                dve.wait_ge(sp_exp, ITEMS.index((kind, g)) + 1)
                ok(dve.reciprocal(rl, lsum))
                if kind == "mla":
                    ins = dve.tensor_scalar(Ps[:, 0:w], Ps[:, 0:w], rl, None, ALU.mult)
                else:
                    gates = grow[:, 1 if kind == "sel" else 2, g:g + 1]
                    ins = dve.tensor_scalar(Ps[:, 0:w], Ps[:, 0:w], rl, gates, ALU.mult, ALU.mult)
                ins.then_inc(sp_norm, 1)

            def keys_out(kind, g, b, part):
                for j in range(2 * part + 1, min(2 * part + 2, KEYS_T[kind]), 2):
                    u = T.at("keys", kind, g, b, part, j=1)
                    bank = arrive(T, u)
                    if j < 2:
                        ins = dve.tensor_copy(kt[:, b % 2, 512:], bank)
                    else:
                        ins = dve.tensor_copy(krp[:, b % 2, 512:], bank[0:ROPE, :])
                    ins.then_inc(T.free[u % T.n], 1)

            def probs_out(kind, g, part):
                tiles = PAGES_OF[kind] + 1
                for j in range(8 * part + 4, min(8 * part + 8, tiles), 8):
                    u = T.at("probs", kind, g, part, j=1)
                    m = min(4, tiles - j)
                    bank = arrive(T, u)
                    r = NS_TOK if m == 1 else P
                    dve.tensor_copy(PTs[0:r, j:j + m, :],
                                    bank[0:r, 0:m * P].rearrange("p (k n) -> p k n", k=m)).then_inc(T.free[u % T.n], 1)

            def nsa_out(g):
                u = T.at("oturn", "sel", g)
                bank = arrive(T, u)
                for k in range(G):
                    s = slice(k * HD, (k + 1) * HD)
                    ins = dve.tensor_copy(
                        oTs[s, :, g * GB * DEC_T:(g + 1) * GB * DEC_T],
                        bank[s, 0:P].rearrange("p (t h) -> p h t", h=H)[:, k * HG:(k + 1) * HG, :])
                ins.then_inc(T.free[u % T.n], 1)

            def drop_block():
                mids = slice(1, SEL_TILES - 2)
                ok(dve.tensor_reduce(selc[:, 0:1], impm[:, mids], AX_X, ALU.min))
                ok(dve.scalar_tensor_tensor(out=impm[:, mids], in0=impm[:, mids], scalar=selc[:, 0:1],
                                            in1=C("jidx")[:, mids], op0=ALU.is_le, op1=ALU.mult))
                ok(dve.tensor_reduce(selc[:, 1:2], impm[:, mids], AX_X, ALU.max))
                ok(dve.tensor_scalar(dropb, C("jidx"), selc[:, 1:2], NEG, ALU.is_equal, ALU.mult))

            a_tri = C_AT["tri"][0]

            def min_unit(n):
                i, kind, h = UNITS[n]
                u, k = S.at("pscore", n), BRANCHES.index((i, kind)) % 4
                bank = arrive(S, u)
                if kind == "pcmp":
                    for hh in range(HG):
                        s = slice(hh * CHP, (hh + 1) * CHP)
                        c = h * HG + hh
                        ins = dve.tensor_tensor_reduce(Pp[:, n % 4, s], bank[:, s],
                                                       C("cmpmask")[:, i * CHP:(i + 1) * CHP], -NSA_SCALE, CLAMP,
                                                       ALU.add, ALU.min, nmp[:, k, c:c + 1])
                else:
                    w = (i + 1) * P
                    mask = const[:, a_tri - i * P:a_tri + P]
                    ins = dve.tensor_tensor_reduce(Pp[:, n % 4, 0:w], bank[:, 0:w], mask,
                                                   -(MLA_SCALE if kind == "pmla" else NSA_SCALE), CLAMP,
                                                   ALU.add, ALU.min, nmp[:, k, h:h + 1])
                ins.then_inc(S.free[u % S.n], 1)

            def heads(x):
                return x.rearrange("p (h d) -> p h d", h=H)

            def branch_out(i, kind):
                m = BRANCHES.index((i, kind))
                b, k = KINDS.index(kind), m % 4
                if m == 0:
                    dve.wait_ge(z_done, 2 * NT)
                pool, u = value_bank(i, kind)
                bank = heads(arrive(pool, u))
                ok(dve.tensor_scalar(coef, lp[:, k, :], 1e-30, None, ALU.max))
                ok(dve.reciprocal(coef, coef))
                if kind != "pmla":
                    ok(dve.tensor_tensor(coef, coef, gate3[:, i, b * H:(b + 1) * H], ALU.mult))
                dst = acc if kind == "pcmp" else otmp
                sums = m - (m + 2) // 3 if kind != "pmla" else 2 * PT
                if kind == "pcmp" and i:
                    dve.wait_ge(mixed_n, i)
                elif sums:
                    dve.wait_ge(summed, sums)
                dve.tensor_tensor(heads(dst), bank, coef.unsqueeze(2).broadcast_to([P, H, HD]), ALU.mult).then_inc(
                    pool.free[u % pool.n], 1)
                if kind == "pmla":
                    wait_copied(dve, pool, u)
                    z = zs[:, i, 0:MW]
                    dve.tensor_tensor(z, z, otmp, ALU.mult).then_inc(mixed_m, 1)

            for step in STEPS:
                kind, a = step[0], step[1:]
                if kind == "x":
                    u, r = T.at(*step, j=1), rows(a[0])
                    dve.tensor_copy(xT[:, 4:8, a[0] * P:a[0] * P + r], four(arrive(T, u), r)).then_inc(T.free[u % T.n], 1)
                elif kind == "rms":
                    work_on(B_MLA, a[0])
                elif kind == "proj" and a[0] != B_MLA:
                    work_on(*a)
                elif kind == "post":
                    post_out(*a)
                elif kind == "pos":
                    u = T.at("pos")
                    dve.tensor_copy(peT, arrive(T, u)[:, 0:32].rearrange("p (k n) -> p k n", k=2)).then_inc(
                        T.free[u % T.n], 1)
                elif kind == "bias":
                    dve.wait_ge(const_in, 16)
                    u = B.at("bias")
                    dve.tensor_tensor(biasv, arrive(B, u)[0:HD, 0:2], b1[:, :], ALU.add).then_inc(B.free[u % B.n], 1)
                    wait_copied(dve, B, u)
                elif kind == "chunks":
                    t, k, half = a
                    chunks_out(dve.tensor_copy, dve, t, k, 2 * half + 1)
                elif kind == "hid" and a[1] == 1:
                    hidden_sum(a[0])
                elif kind == "hsilu":
                    hidden_silu(a[0])
                elif kind == "zrecip":
                    wait_copied(dve, A, A.at("proj", *a))
                    e = z_of(*a)[1]
                    ok(dve.tensor_scalar(e, e, 1.0, None, ALU.add))
                    dve.reciprocal(e, e).then_inc(z_recip, 1)
                elif kind == "cmpout":
                    compressed(a[0])
                elif kind == "qhead":
                    u = T.at("qhead")
                    bank = arrive(T, u)[:, 0:H * NS_TOK]
                    dve.tensor_copy(qhT, bank[0:NOPE, :])
                    for p0 in (0, NOPE):
                        ins = dve.tensor_copy(qrope[p0:p0 + ROPE, :].rearrange("p (t h) -> p h t", h=H),
                                              bank[NOPE:QH, :].rearrange("p (h t) -> p h t", h=H))
                    ins.then_inc(T.free[u % T.n], 1)
                elif kind == "keys":
                    keys_out(*a)
                elif kind == "new":
                    newest(*a)
                elif kind == "min":
                    minima(*a)
                elif kind == "norm":
                    if step == ("norm", "sel", 0):
                        dve.wait_ge(grow_in, 16)
                    normalise(*a)
                elif kind == "probs":
                    probs_out(*a)
                elif kind == "pv" and a[0] == "win":
                    u = O.at("pv", "sel", a[1])
                    dve.tensor_copy(orow, arrive(O, u)[:, 0:P]).then_inc(O.free[u % O.n], 1)
                elif kind == "oturn" and a[0] == "sel":
                    nsa_out(a[1])
                elif kind == "omla":
                    u = S.at("omla")
                    zm = zs[0:NS_TOK, ST, 0:MW]
                    dve.tensor_tensor(zm, arrive(S, u)[0:NS_TOK, :], zm, ALU.mult).then_inc(S.free[u % S.n], 1)
                elif kind == "cscore":
                    u = S.at(*step)
                    minimum(S, u, Pc[:, 0:CH], arrive(S, u)[:, 0:CH], C("cmplast"), NSA_SCALE, cmin)
                    wait_copied(dve, S, u)
                    dve.tensor_scalar(cmin, cmin, 1.0, None, ALU.mult).then_inc(cp_min, 1)
                elif kind == "cnorm":
                    dve.wait_ge(grow_in, 16)
                    dve.wait_ge(cp_exp, a[0] + 1)
                    ok(dve.reciprocal(crl, csum))
                    ok(dve.tensor_scalar(Pc[:, 0:CH], Pc[:, 0:CH], crl, None, ALU.mult))
                    dve.tensor_scalar(Pc[:, CH:], Pc[:, 0:CH], grow[:, 0, a[0]:a[0] + 1], None, ALU.mult).then_inc(cp_norm, 1)
                elif kind == "cturn":
                    u = T.at(*step)
                    dve.tensor_copy(PcT, arrive(T, u)[0:CH, 0:2 * P].rearrange("p (v n) -> p v n", v=2)).then_inc(
                        T.free[u % T.n], 1)
                elif kind in ("imp0", "imp1"):
                    u = S.at(*step)
                    dve.tensor_copy(impr if kind == "imp0" else impm, arrive(S, u)[:, 0:SEL_TILES]).then_inc(
                        S.free[u % S.n], 1)
                elif kind == "drop":
                    wait_copied(dve, S, S.at("imp1", a[0]))
                    drop_block()
                elif kind == "onsa":
                    u = T.at("onsa")
                    zn = zs[0:NS_TOK, ST, MW:].rearrange("p (g h d) -> p g h d", g=G, h=HG)
                    on = arrive(T, u)[0:NS_TOK, :].rearrange("p (h g d) -> p h g d", g=G, h=HG)
                    for k in range(G):
                        ins = dve.tensor_tensor(zn[:, k], on[:, :, k, :], zn[:, k], ALU.mult)
                    ins.then_inc(T.free[u % T.n], 1)
                elif kind == "vup":
                    u = S.at(*step)
                    dve.tensor_copy(Vm[:, a[0], :], arrive(S, u)).then_inc(S.free[u % S.n], 1)
                elif kind == "qh":
                    u = T.at(*step, j=1)
                    dve.tensor_copy(QT[:, a[0] % 2, 4:8, :],
                                    arrive(T, u)[0:QH, :].rearrange("p (h n) -> p h n", h=4)).then_inc(T.free[u % T.n], 1)
                elif kind == "pscore":
                    min_unit(*a)
                elif kind == "pturn" and a[0] % 2 == 1:
                    n = a[0]
                    u, w = T.at(*step), P if UNITS[n][1] == "pcmp" else (UNITS[n][0] + 1) * P
                    dve.tensor_copy(PTp[:, n % 4, 0:w], arrive(T, u)[:, 0:w]).then_inc(T.free[u % T.n], 1)
                elif kind == "branch":
                    branch_out(*a)
                elif kind == "mix":
                    u, r = T.at(*step, j=1), rows(ORDER[a[0]])
                    dve.tensor_copy(mixT[:, a[0] % 2, 4:8, 0:r], four(arrive(T, u), r)).then_inc(T.free[u % T.n], 1)
                elif kind == "out":
                    n, half = a
                    r = rows(ORDER[n])
                    y = yb[0:r, n % 2, :]
                    if half == 0:
                        dve.wait_ge(y_in[n % 2], 16 * (n // 2 + 1))
                    if step == ("out", 0, 0):
                        u, w = A.at(*step), D_MODEL // 4
                        bank = arrive(A, u)
                        for j in range(4):
                            yj = y[:, j * w:(j + 1) * w]
                            ins = dve.scalar_tensor_tensor(out=yj, in0=yj, scalar=ALPHA,
                                                           in1=bank[j * NS_TOK:(j + 1) * NS_TOK, 0:w],
                                                           op0=ALU.mult, op1=ALU.add)
                        ins.then_inc(A.free[u % A.n], 1)
                        wait_copied(dve, A, u)
                    yh = y[:, half * 512:(half + 1) * 512]
                    if n:
                        u = A.at(*step)
                        dve.scalar_tensor_tensor(out=yh, in0=yh, scalar=ALPHA, in1=arrive(A, u),
                                                 op0=ALU.mult, op1=ALU.add).then_inc(A.free[u % A.n], 1)
                        wait_copied(dve, A, u)
                    ok(dve.bn_stats(bnst[0:r, half, :], yh))
                    if half == 1:
                        dve.bn_aggr(bnag[0:r, n % 2, :], bnst[0:r]).then_inc(y_var, 1)
                elif kind == "norm_y":
                    n, r = a[0], rows(ORDER[a[0]])
                    y, root = yb[0:r, n % 2, :], lnr[0:r, n % 2:n % 2 + 1]
                    dve.wait_ge(y_sqrt, n + 1)
                    ok(dve.reciprocal(root, root))
                    if n == 0:
                        dve.wait_ge(ln_in, 32)
                    ok(dve.scalar_tensor_tensor(out=y, in0=y, scalar=bnag[0:r, n % 2, 0:1], in1=lng[0:r],
                                                op0=ALU.subtract, op1=ALU.mult))
                    dve.scalar_tensor_tensor(out=y, in0=y, scalar=root, in1=lnb[0:r], op0=ALU.mult,
                                             op1=ALU.add).then_inc(y_done, 1)

        @block.gpsimd
        def _(pool):
            ok = own(pool, pool_own)

            def rope(out, x, r, n, d, t, table, done, value):
                h = d // 2
                half = 512 if n * d > 256 else 256
                ta, tb = (rtmp[0:r, j * half:j * half + n * d].rearrange("p (n z h) -> p n z h", n=n, z=2)
                          for j in range(2))
                cos = C("cos" + table)[0:r, t * h:(t + 1) * h]
                sin = C("sin" + table)[0:r, t * d:(t + 1) * d].rearrange("p (z h) -> p z h", z=2)
                for z in range(2):
                    pool.tensor_tensor(ta[:, :, z, :], x[:, :, z, :], cos.unsqueeze(1).broadcast_to([r, n, h]), ALU.mult)
                    ins = pool.tensor_tensor(tb[:, :, z, :], x[:, :, 1 - z, :],
                                             sin[:, z, :].unsqueeze(1).broadcast_to([r, n, h]), ALU.mult)
                ok(ins)
                pool.tensor_tensor(out, ta, tb, ALU.add).then_inc(done, 1)
                pool.wait_ge(done, value)

            def halves(x, n):
                return x.rearrange("p (n z h) -> p n z h", n=n, z=2)

            def rope_queries(q, heads, t, value):
                x = q.rearrange("p (n w) -> p n w", n=heads)[:, :, NOPE:QH].rearrange("p n (z h) -> p n z h", z=2)
                rope(x, x, rows(t), heads, ROPE, t, "m", q_roped, value)

            def silu(b, t):
                n = t + 1 if b == B_ZMLA else NT + t + 1
                pool.wait_ge(z_recip, n)
                z, e = z_of(b, t)
                pool.tensor_tensor(z, z, e, ALU.mult).then_inc(z_done, 1)
                pool.wait_ge(z_done, n)

            pool.wait_ge(const_in, 16)
            turns = 0
            for step in STEPS:
                if step[0] == "qup_s":
                    for half in range(2):
                        wait_copied(pool, B, B.at(*step) + half)
                        rope_queries(qs[half], 4, ST, half + 1)
                if step[0] == "zrecip" and step[1:] != (B_ZNSA, NT - 1):
                    silu(*step[1:])
                if step[0] == "pad":
                    j = step[1]
                    wait_full(pool, B, B.at("hid", NT - 1, 0))
                    ok(pool.memset(padK[:, j], 0.0))
                    wait_copied(pool, T, T.at("post", B_WINGATE, NT - 1))
                    for g in range(G):
                        s = slice(g * HD, (g + 1) * HD)
                        ins = pool.tensor_copy(padK[s, j, g, :], (selKT, winKT)[j][s, 0:SEQ])
                    ins.then_inc(pad_ready, 1)
                    pool.wait_ge(pad_ready, j + 1)
                if step[0] != "proj" or step[1] in (B_ZMLA, B_ZNSA):
                    continue
                b, t = step[1:]
                r = rows(t)
                turns += 1
                wait_copied(pool, A, A.at("proj", b, t))
                if b == B_MLA:
                    rope(halves(row3[0:r, t, KVL:ROW], 1), halves(araw[0:r, t % 3, QL + KVL:], 1), r, 1, ROPE, t, "m",
                         roped, turns)
                elif b == B_Q:
                    if t >= 2:
                        wait_full(pool, T, T.at("post", b, t - 2, j=1))
                    rope(halves(qrot[0:r, t % 2, :], H), halves(qraw[0:r, t % 2, :], H), r, H, HD, t, "n", roped, turns)
                else:
                    o = KVW if b == B_CMPSEL else 2 * KVW
                    k = halves(kv3[0:r, t, o:o + G * HD], G)
                    rope(k, k, r, G, HD, t, "n", roped, turns)

            wait_full(pool, A, A.at("proj", B_ZNSA, NT - 1))
            ok(pool.memset(bufA[:, 0:2 * SR], 0.0))
            for dst, src in ((qnbd, qnT3), (qrbd, qrT3)):
                for g in range(G):
                    s = slice(g * HD, (g + 1) * HD)
                    ins = pool.tensor_copy(dst[s].rearrange("p (t h) -> p h t", h=H)[:, g * HG:(g + 1) * HG, :],
                                           src[s, :, SEQ:NTOK])
            ins.then_inc(bd_ready, 1)
            pool.wait_ge(bd_ready, 1)
            silu(B_ZNSA, NT - 1)
            for step in STEPS:
                if step[0] == "branch" and step[2] in ("psel", "pwin"):
                    i, kind = step[1:]
                    bank, u = value_bank(i, kind)
                    wait_copied(pool, bank, u)
                    n = 2 * i + 1 + int(kind == "pwin")
                    pool.tensor_tensor(acc, acc, otmp, ALU.add).then_inc(summed, 1)
                    pool.wait_ge(summed, n)
                    if kind == "pwin":
                        z = zs[:, i, MW:]
                        pool.tensor_tensor(z, z, acc, ALU.mult).then_inc(mixed_n, 1)
                        pool.wait_ge(mixed_n, i + 1)
                if step[0] == "kup" and step[1] % 2 == 0:
                    j = step[1] // 2
                    wait_full(pool, S, S.at(*step))
                    for h in range(4 * j, 4 * j + 4):
                        ins = pool.tensor_copy(KT[NOPE:QH, h, :], krT[NOPE:QH, 0:SEQ])
                    ins.then_inc(key_rows, 1)
                    pool.wait_ge(key_rows, j + 1)
                if step[0] == "qup":
                    for half in range(2):
                        wait_copied(pool, A, A.at(*step) + half)
                    rope_queries(qm, H, step[1], step[1] + 3)

    return nc



    return nc


_INS = ["x_prompt", "x_sample", "cache_mla", "cache_cmp_kv", "cache_sel_kv", "state_win_kv", "page_table", "w_in",
        "q_norm_g", "w_uq", "kv_norm_g", "w_uk", "w_uv", "cmp_pos_emb", "cmp_w1", "cmp_b1", "cmp_w2", "w_o",
        "ln_g", "ln_b"]
_OUTS = [("y_prompt", (1, SEQ, D_MODEL)), ("y_sample", (DEC_B, DEC_T, D_MODEL)), ("p_mla", (1, 1, SEQ, ROW)),
         ("p_cmp", (1, 1, SEQ, 2, G, HD)), ("p_sel", (1, 1, SEQ, 2, G, HD)), ("p_win", (1, 1, SEQ, 2, G, HD)),
         ("s_mla", (1, DEC_B, DEC_T, ROW)), ("s_cmp", (1, DEC_B, DEC_T, 2, G, HD)),
         ("s_sel", (1, DEC_B, DEC_T, 2, G, HD)), ("s_win", (1, DEC_B, WIN, 2, G, HD))]
OUT_NAMES = [f"out_{name}" for name, _ in _OUTS]


def kernel(**inputs):
    import concourse.bacc as bacc
    from concourse.bass_utils import run_bass_kernel_spmd

    nc = bacc.Bacc("TRN2", target_bir_lowering=False, num_devices=1, dynamic_dma_scratch_size=1024)
    arrays, io = {}, {}
    for name in _INS:
        a = np.ascontiguousarray(inputs[name])
        arrays[f"in_{name}"] = a
        io[name] = nc.dram_tensor(f"in_{name}", a.shape, mybir.dt.from_np(a.dtype), kind="ExternalInput").ap()
    arrays["in_const"] = constants()
    io["const"] = nc.dram_tensor("in_const", (P, C_W), F32, kind="ExternalInput").ap()
    for name, shape in _OUTS:
        io[name] = nc.dram_tensor(f"out_{name}", shape, F32, kind="ExternalOutput").ap()
    build(nc, io)
    r = run_bass_kernel_spmd(nc, [arrays], core_ids=[0])
    return tuple(r.results[0][n] for n in OUT_NAMES)
```
